# Optimizing a Trainium2 kernel written in Bass

```python
import jax, jax.numpy as jnp
from jax import lax
import numpy as np

D_MODEL = 1024
BATCH = 1
SEQ = 1024
DEPTH = 2

CHUNK = 64
N_MIXERS = 2
N_GLA_LAYERS = (DEPTH + 1) // 2
N_SGU_LAYERS = DEPTH // 2
EPS = 1e-6

GLA_HEADS = 4
GLA_DK = D_MODEL // 2 // GLA_HEADS
GLA_DV = D_MODEL // GLA_HEADS
GLA_HK = GLA_HEADS * GLA_DK
GLA_HV = GLA_HEADS * GLA_DV
GLA_GATE_RANK = 16
GLA_TAU = 16.0
GLA_IN = 2 * GLA_HK + 2 * GLA_HV + GLA_GATE_RANK

SGU_BLOCK = 128
SGU_GROUPS = 4
SGU_FFN = 4 * D_MODEL
SGU_HALF = SGU_FFN // 2
SGU_GC = SGU_HALF // SGU_GROUPS

N_GROUPS = 4
EXPERTS_PER_GROUP = 8
N_EXPERTS = N_GROUPS * EXPERTS_PER_GROUP
TOP_K = 2
EXPERT_FF = D_MODEL // 2
ROUTE_BLOCK = 128

kernel_name = "hybrid_gla_sgu_hier_moe"

def rmsnorm(x, g):
    xf = x.astype(jnp.float32)
    y = xf * lax.rsqrt(jnp.mean(xf * xf, axis=-1, keepdims=True) + EPS)
    return (y * g.astype(jnp.float32)).astype(x.dtype)

def layernorm(x, g, b):
    xf = x.astype(jnp.float32)
    mu = jnp.mean(xf, axis=-1, keepdims=True)
    xc = xf - mu
    y = xc * lax.rsqrt(jnp.mean(xc * xc, axis=-1, keepdims=True) + EPS)
    return (y * g.astype(jnp.float32) + b.astype(jnp.float32)).astype(x.dtype)

def gla_mixer(h, w_in, w_gate_up, b_gate, head_g, w_out):
    B, S, _ = h.shape
    N = S // CHUNK
    proj = h @ w_in
    q, k, v, r, glr = jnp.split(
        proj, [GLA_HK, 2 * GLA_HK, 2 * GLA_HK + GLA_HV, 2 * GLA_HK + 2 * GLA_HV], axis=-1)
    log_a = jax.nn.log_sigmoid((glr @ w_gate_up + b_gate).astype(jnp.float32)) / GLA_TAU
    scale = GLA_DK ** -0.5

    def to_chunks(t, d):
        return t.astype(jnp.float32).reshape(B, N, CHUNK, GLA_HEADS, d).transpose(1, 0, 3, 2, 4)

    qc = to_chunks(q, GLA_DK) * scale
    kc = to_chunks(k, GLA_DK)
    vc = to_chunks(v, GLA_DV)
    gc = to_chunks(log_a, GLA_DK)

    def step(state, inp):
        q_, k_, v_, g_ = inp
        b = jnp.cumsum(g_, axis=2)
        b_end = b[:, :, -1:, :]
        k_dec = k_ * jnp.exp(b_end - b)
        att = jnp.einsum('bhtk,bhsk->bhts', q_, k_dec)
        o = (jnp.einsum('bhtk,bhkv->bhtv', q_ * jnp.exp(b_end), state)
             + jnp.einsum('bhts,bhsv->bhtv', att, v_))
        new_state = (jnp.exp(b_end)[:, :, 0, :, None] * state
                     + jnp.einsum('bhsk,bhsv->bhkv', k_dec, v_))
        return new_state, o

    s0 = jnp.zeros((B, GLA_HEADS, GLA_DK, GLA_DV), jnp.float32)
    _, o = lax.scan(step, s0, (qc, kc, vc, gc))
    o = o.transpose(1, 0, 3, 2, 4).reshape(B, S, GLA_HEADS, GLA_DV)
    o = rmsnorm(o, head_g).reshape(B, S, GLA_HV)
    o = o * jax.nn.silu(r.astype(jnp.float32))
    return o.astype(h.dtype) @ w_out

def sgu_mixer(h, w_in, ln_g, ln_b, w_s, b_s, w_out):
    B, S, _ = h.shape
    z = jax.nn.gelu(h @ w_in, approximate=False)
    u, v = jnp.split(z, 2, axis=-1)
    v = layernorm(v, ln_g, ln_b)
    pos = jnp.arange(SGU_BLOCK)
    mask = (pos[:, None] // CHUNK) >= (pos[None, :] // CHUNK)
    ws = jnp.where(mask[None], w_s, jnp.zeros_like(w_s))
    vb = v.reshape(B, S // SGU_BLOCK, SGU_BLOCK, SGU_GROUPS, SGU_GC)
    mixed = jnp.einsum('gts,bnsgc->bntgc', ws, vb) + b_s.T[None, None, :, :, None]
    out = u * mixed.reshape(B, S, SGU_HALF)
    return out @ w_out

def routed_experts(xt, expert, gate, w1, w3, w2):
    T, D = xt.shape
    A = T * TOP_K
    NB = -(-A // ROUTE_BLOCK) + N_EXPERTS
    flat_e = expert.reshape(A).astype(jnp.int32)
    flat_tok = jnp.arange(A, dtype=jnp.int32) // TOP_K
    flat_gate = gate.reshape(A)
    order = jnp.argsort(flat_e)
    e_sorted = flat_e[order]
    counts = jnp.bincount(flat_e, length=N_EXPERTS).astype(jnp.int32)
    padded = ((counts + ROUTE_BLOCK - 1) // ROUTE_BLOCK) * ROUTE_BLOCK
    pad_end = jnp.cumsum(padded)
    pad_start = pad_end - padded
    start = jnp.cumsum(counts) - counts
    dest = pad_start[e_sorted] + jnp.arange(A, dtype=jnp.int32) - start[e_sorted]
    buf_tok = jnp.full((NB * ROUTE_BLOCK,), T, jnp.int32).at[dest].set(flat_tok[order])
    buf_gate = jnp.zeros((NB * ROUTE_BLOCK,), flat_gate.dtype).at[dest].set(flat_gate[order])
    blk_e = jnp.minimum(
        jnp.searchsorted(pad_end, jnp.arange(NB, dtype=jnp.int32) * ROUTE_BLOCK, side='right'),
        N_EXPERTS - 1)
    x_pad = jnp.concatenate([xt, jnp.zeros((1, D), xt.dtype)], axis=0)
    xb = x_pad[buf_tok].reshape(NB, ROUTE_BLOCK, D)

    def run(args):
        xblk, e = args
        hid = jax.nn.silu(xblk @ w1[e]) * (xblk @ w3[e])
        return hid @ w2[e]

    yb = lax.map(run, (xb, blk_e)).reshape(NB * ROUTE_BLOCK, D)
    y = jax.ops.segment_sum(yb * buf_gate[:, None].astype(yb.dtype), buf_tok, num_segments=T + 1)
    return y[:T]

def hier_moe(h, w_group, b_group, w_sub, b_sub, w1, w3, w2):
    B, S, D = h.shape
    T = B * S
    xt = h.reshape(T, D)
    xf = xt.astype(jnp.float32)
    p_group = jax.nn.softmax(xf @ w_group.astype(jnp.float32) + b_group.astype(jnp.float32), axis=-1)
    g_w, g_idx = lax.top_k(p_group, 1)
    sub_logits = (jnp.einsum('td,gde->tge', xf, w_sub.astype(jnp.float32))
                  + b_sub.astype(jnp.float32))
    chosen = jnp.take_along_axis(sub_logits, g_idx[:, :, None], axis=1)[:, 0]
    p_sub = jax.nn.softmax(chosen, axis=-1)
    s_w, s_idx = lax.top_k(p_sub, TOP_K)
    s_w = s_w / jnp.sum(s_w, axis=-1, keepdims=True)
    gate = (g_w * s_w).astype(h.dtype)
    expert = g_idx * EXPERTS_PER_GROUP + s_idx
    return routed_experts(xt, expert, gate, w1, w3, w2).reshape(B, S, D)

def setup_inputs(seed: int = 0) -> dict:
    key = jax.random.key(seed)
    ks = jax.random.split(key, 24)
    f32 = jnp.float32
    nrm = lambda k, shape, s: jax.random.normal(k, shape, f32) * s
    NA, NS = N_GLA_LAYERS, N_SGU_LAYERS
    return {
        "x": nrm(ks[0], (BATCH, SEQ, D_MODEL), 1.0),
        "gla_norm": 1.0 + nrm(ks[1], (NA, D_MODEL), 0.02),
        "gla_w_in": nrm(ks[2], (NA, D_MODEL, GLA_IN), D_MODEL ** -0.5),
        "gla_w_gate_up": nrm(ks[3], (NA, GLA_GATE_RANK, GLA_HK), GLA_GATE_RANK ** -0.5),
        "gla_b_gate": nrm(ks[4], (NA, GLA_HK), 0.1),
        "gla_head_g": 1.0 + nrm(ks[5], (NA, GLA_HEADS, GLA_DV), 0.02),
        "gla_w_out": nrm(ks[6], (NA, GLA_HV, D_MODEL), GLA_HV ** -0.5),
        "sgu_norm": 1.0 + nrm(ks[7], (NS, D_MODEL), 0.02),
        "sgu_w_in": nrm(ks[8], (NS, D_MODEL, SGU_FFN), D_MODEL ** -0.5),
        "sgu_ln_g": 1.0 + nrm(ks[9], (NS, SGU_HALF), 0.02),
        "sgu_ln_b": nrm(ks[10], (NS, SGU_HALF), 0.02),
        "sgu_w_s": nrm(ks[11], (NS, SGU_GROUPS, SGU_BLOCK, SGU_BLOCK), SGU_BLOCK ** -0.5),
        "sgu_b_s": 1.0 + nrm(ks[12], (NS, SGU_GROUPS, SGU_BLOCK), 0.1),
        "sgu_w_out": nrm(ks[13], (NS, SGU_HALF, D_MODEL), SGU_HALF ** -0.5),
        "moe_norm": 1.0 + nrm(ks[14], (DEPTH, D_MODEL), 0.02),
        "moe_w_group": nrm(ks[15], (DEPTH, D_MODEL, N_GROUPS), D_MODEL ** -0.5),
        "moe_b_group": nrm(ks[16], (DEPTH, N_GROUPS), 0.01),
        "moe_w_sub": nrm(ks[17], (DEPTH, N_GROUPS, D_MODEL, EXPERTS_PER_GROUP), D_MODEL ** -0.5),
        "moe_b_sub": nrm(ks[18], (DEPTH, N_GROUPS, EXPERTS_PER_GROUP), 0.01),
        "moe_w1": nrm(ks[19], (DEPTH, N_EXPERTS, D_MODEL, EXPERT_FF), D_MODEL ** -0.5),
        "moe_w3": nrm(ks[20], (DEPTH, N_EXPERTS, D_MODEL, EXPERT_FF), D_MODEL ** -0.5),
        "moe_w2": nrm(ks[21], (DEPTH, N_EXPERTS, EXPERT_FF, D_MODEL), EXPERT_FF ** -0.5),
        "final_norm": 1.0 + nrm(ks[22], (D_MODEL,), 0.02),
    }

def reference(x, gla_norm, gla_w_in, gla_w_gate_up, gla_b_gate, gla_head_g, gla_w_out,
              sgu_norm, sgu_w_in, sgu_ln_g, sgu_ln_b, sgu_w_s, sgu_b_s, sgu_w_out,
              moe_norm, moe_w_group, moe_b_group, moe_w_sub, moe_b_sub, moe_w1, moe_w3, moe_w2,
              final_norm):
    for i in range(DEPTH):
        j = i // N_MIXERS
        if i % N_MIXERS == 0:
            x = x + gla_mixer(rmsnorm(x, gla_norm[j]), gla_w_in[j], gla_w_gate_up[j],
                              gla_b_gate[j], gla_head_g[j], gla_w_out[j])
        else:
            x = x + sgu_mixer(rmsnorm(x, sgu_norm[j]), sgu_w_in[j], sgu_ln_g[j], sgu_ln_b[j],
                              sgu_w_s[j], sgu_b_s[j], sgu_w_out[j])
        x = x + hier_moe(rmsnorm(x, moe_norm[i]), moe_w_group[i], moe_b_group[i], moe_w_sub[i],
                         moe_b_sub[i], moe_w1[i], moe_w3[i], moe_w2[i])
    return rmsnorm(x, final_norm)


_drawn_inputs = setup_inputs


def setup_inputs(seed=0):
    import zlib

    import numpy as np

    out = dict(_drawn_inputs(seed))
    spreads = {}
    factors = {'sgu_ln_g': 4.86,
     'sgu_ln_b': 4.296,
     'moe_b_group': 3.299,
     'moe_b_sub': 2.723,
     'final_norm': 2.816}
    for name, (base, spread) in spreads.items():
        noise = np.random.default_rng([zlib.crc32(name.encode()), seed]).standard_normal(out[name].shape)
        drawn = base * np.exp(spread * noise) if base else spread * noise
        out[name] = __import__('jax').numpy.asarray(drawn.astype(out[name].dtype))
    for name, factor in factors.items():
        out[name] = (out[name] * factor).astype(out[name].dtype)
    return out
```

```python
from contextlib import ExitStack

import concourse.bass as bass
from concourse import mybir

F32 = mybir.dt.float32
F32R = mybir.dt.float32r
I32 = mybir.dt.int32
U32 = mybir.dt.uint32
ALU = mybir.AluOpType
ACT = mybir.ActivationFunctionType
AX_X = mybir.AxisListType.X

P = 128
D = 1024
SEQ = 1024
TILES = SEQ // P
DC = D // P
EPS = 1e-6

HEADS = 4
DK = 128
DV = 256
HK = HEADS * DK
HV = HEADS * DV
RANK = 16
TAU = 16.0
CHUNK = 64
CHUNKS = SEQ // CHUNK

HALF = 2048
SG = 4
SLICE = 256
SLICES = HALF // SLICE

NG = 4
NE = 8
EXPERTS = NG * NE
TOP = 2
FF = 512
FC = FF // P
ROUTES = NG + EXPERTS
ASSIGN = SEQ * TOP
OV = ASSIGN // P - 1
COLS = EXPERTS + OV + 1
NOWHERE = 1 << 20

PIECE = 2048
RAW = 4
SPLIT = 2
BLOCK = 6
GLA_AT = 0
MOE_AT = [HEADS * 4, HEADS * 4 + EXPERTS * BLOCK + SLICES * 3]
SGU_V_AT = MOE_AT[0] + EXPERTS * BLOCK
SGU_U_AT = SGU_V_AT + SLICES

HALF_BANK = 256
BANK = 512

G_HEAD = ["A"] * 2 + ["D"] * 8 + ["A"] * 16 + ["D"] * 16
G_V = ["A"] * 8
G_U = ["A"] * 4 + ["D"] * 16
G_CREDIT = 3
LANDED = 32


class Names:
    pass


def build(nc, x, gla_norm, gla_w_in, gla_w_gate_up, gla_b_gate, gla_head_g, gla_w_out,
          sgu_norm, sgu_w_in, sgu_ln_g, sgu_ln_b, sgu_w_s, sgu_b_s, sgu_w_out,
          moe_norm, moe_w_group, moe_b_group, moe_w_sub, moe_b_sub, moe_w1, moe_w3, moe_w2,
          final_norm, out):
    with ExitStack() as ctx:
        m = memory(nc, ctx)
        s = semaphores(nc, ctx)
        d = Names()
        d.h = nc.dram_tensor("h_rows", (SEQ, D), F32, kind="Internal").ap()
        d.y = nc.dram_tensor("y_rows", (ASSIGN, D), F32, kind="Internal").ap()
        d.dec = nc.dram_tensor("decay_rows", (SEQ, HK), F32, kind="Internal").ap()
        d.v = nc.dram_tensor("v_rows", (SEQ, HALF), F32, kind="Internal").ap()
        d.x, d.gla_norm, d.gla_w_in, d.gla_w_gate_up, d.gla_b_gate = x, gla_norm, gla_w_in, gla_w_gate_up, gla_b_gate
        d.gla_head_g, d.gla_w_out, d.sgu_norm, d.sgu_w_in = gla_head_g, gla_w_out, sgu_norm, sgu_w_in
        d.sgu_ln_g, d.sgu_ln_b, d.sgu_w_s, d.sgu_b_s, d.sgu_w_out = sgu_ln_g, sgu_ln_b, sgu_w_s, sgu_b_s, sgu_w_out
        d.moe_norm, d.moe_w_group, d.moe_b_group = moe_norm, moe_w_group, moe_b_group
        d.moe_w_sub, d.moe_b_sub, d.moe_w1, d.moe_w3, d.moe_w2 = moe_w_sub, moe_b_sub, moe_w1, moe_w3, moe_w2
        d.final_norm, d.out = final_norm, out
        block = ctx.enter_context(nc.Block())

        @block.sync
        def _(sp):
            sp_program(sp, m, s, d)

        @block.gpsimd
        def _(pool):
            pool_program(pool, m, s, d)

        @block.scalar
        def _(act):
            act_program(act, m, s, d)

        @block.vector
        def _(dve):
            dve_program(dve, m, s, d)

        @block.tensor
        def _(pe):
            pe_program(pe, m, s, d)



def memory(nc, ctx):
    base = (nc.sbuf_base + 63) // 64 * 64
    top = nc.sbuf_usable_end // 32 * 32
    ctx.enter_context(nc.sbuf_tensor("slab", [P, (top - nc.sbuf_base) // 4 - 8], F32))
    at = [base]

    def put(name, shape, dt=F32):
        size = 4
        for n in shape[1:]:
            size *= n
        t = nc.alloc_sbuf_tensor_at(name, list(shape), dt, offset=at[0])
        at[0] += (size + 31) // 32 * 32
        assert at[0] <= top, (name, at[0] - top)
        return t

    m = Names()
    m.x = put("x_sb", [P, TILES, D])
    m.raw = put("raw", [P, RAW, PIECE])
    m.w_hi = put("w_hi", [P, SPLIT, PIECE], F32R)
    m.w_lo = put("w_lo", [P, SPLIT, PIECE], F32R)
    m.ident = put("ident", [P, P])
    m.ones = put("ones", [P, P])
    m.before = put("before", [P, P])
    m.after = put("after", [P, P])
    m.halves = put("halves", [P, 2])
    m.count_i = put("count_i", [P, P], I32)
    m.count = put("count", [P, P])
    m.label_i = put("label_i", [P, TOP * TILES], I32)
    m.label = put("label", [P, TOP * TILES])
    m.eps = put("eps", [P, 1])
    m.one = put("one", [P, 1])
    m.ss = put("ss", [P, TILES])
    m.std = put("std", [P, TILES])
    m.rstd = put("rstd", [P, TILES])
    region = at[0]

    m.ht_hi = put("ht_hi", [P, DC, SEQ], F32R)
    m.ht_lo = put("ht_lo", [P, DC, SEQ], F32R)
    after_ht = at[0]
    m.h = put("h", [P, 2, D])
    m.gain = put("gain", [P, D])
    after_norm = at[0]

    at[0] = after_ht
    m.gate_up = put("gate_up", [P, TILES, HK])
    m.glr_raw = put("glr_raw", [P, DC * RANK])
    m.glr_hi = put("glr_hi", [P, DC * RANK], F32R)
    m.glr_lo = put("glr_lo", [P, DC * RANK], F32R)
    m.glr = put("glr", [P, TILES * RANK])
    m.glr_t = put("glr_t", [P, P])
    m.bgate = put("bgate", [P, HK])
    m.z = put("z", [P, 2, HK])
    m.zexp = put("zexp", [P, 2, HK])
    m.logsig = put("logsig", [P, 2, HK])
    at[0] = after_ht
    m.dec = put("dec", [P, TILES, DK])
    m.q_t = put("q_t", [P, SEQ])
    m.kd = put("kd", [P, TILES, DK])
    m.v = put("v", [P, TILES, DV])
    m.o = put("o", [P, TILES, DV])
    m.rg = put("rg", [P, 2, DV])
    m.state = put("state", [P, 2, DV])
    m.head_g = put("head_g", [P, DV])
    m.e_now = put("e_now", [P, CHUNKS])
    m.junk = put("junk", [P, DV])
    m.oss = put("oss", [P, TILES])
    m.ostd = put("ostd", [P, TILES])
    m.orstd = put("orstd", [P, TILES])
    at_o = at[0]
    at[0] = after_ht + 4 * 1024
    m.ot_hi = put("ot_hi", [P, TILES, DV], F32R)
    m.ot_lo = put("ot_lo", [P, TILES, DV], F32R)
    at[0] = top - 256 - 32
    m.e_end = put("e_end", [P, HEADS * CHUNKS])
    assert at_o <= top - 256 - 32

    at[0] = after_ht
    m.v_out = put("v_out", [P, 2, TILES, SLICE])
    at[0] = after_ht
    m.gt_hi = put("gt_hi", [P, 2, SEQ], F32R)
    m.gt_lo = put("gt_lo", [P, 2, SEQ], F32R)
    m.v_s = put("v_s", [P, TILES, SLICE])
    m.ut = put("ut", [P, 2, BANK])
    m.mix = put("mix", [P, BANK])
    m.ln_g = put("ln_g", [P, SLICE])
    m.ln_b = put("ln_b", [P, SLICE])
    m.ws_t = put("ws_t", [P, SG * P])
    m.bs = put("bs", [P, SG * P])
    m.stats = put("stats", [P, TILES, SLICES * 6])
    m.mv = put("mv", [P, TILES, 2])
    m.lstd = put("lstd", [P, TILES])
    m.lrstd = put("lrstd", [P, TILES])
    m.lshift = put("lshift", [P, TILES])
    at[0] = after_norm
    m.ws = put("ws", [P, SG, P])

    at[0] = after_norm
    m.r_raw = put("r_raw", [P, DC, ROUTES])
    m.r_hi = put("r_hi", [P, DC, ROUTES], F32R)
    m.r_lo = put("r_lo", [P, DC, ROUTES], F32R)
    m.r_bias = put("r_bias", [P, ROUTES])
    m.logit = put("logit", [P, TILES, ROUTES])
    m.glog = put("glog", [P, TILES, 8])
    m.gmax = put("gmax", [P, TILES, 8])
    m.gidx = put("gidx", [P, TILES, 8], U32)
    m.gsel = put("gsel", [P, TILES])
    m.gexp = put("gexp", [P, TILES, NG])
    m.gw = put("gw", [P, TILES])
    m.goh = put("goh", [P, TILES, NG])
    m.sel = put("sel", [P, TILES, NG, NE])
    m.chosen = put("chosen", [P, TILES, NE])
    m.cmax = put("cmax", [P, TILES, 8])
    m.cidx = put("cidx", [P, TILES, 8], U32)
    m.csel = put("csel", [P, TILES, TOP])
    m.e2 = put("e2", [P, TILES])
    m.gate = put("gate", [P, TOP, TILES])
    m.eid = put("eid", [P, TOP, TILES])
    m.eoh = put("eoh", [P, TOP * TILES, EXPERTS])
    m.emask = put("emask", [P, TILES, EXPERTS])
    m.pre = put("pre", [P, TILES + 1, EXPERTS])
    m.rank = put("rank", [P, TILES, EXPERTS])
    m.pick = put("pick", [P, TOP * TILES, EXPERTS])
    m.rk = put("rk", [P, TOP * TILES])
    m.nov = put("nov", [P, EXPERTS])
    m.inc = put("inc", [P, 2, EXPERTS])
    m.ovb = put("ovb", [P, EXPERTS])
    m.q = put("q", [P, TOP * TILES])
    m.ovk = put("ovk", [P, TOP * TILES])
    m.t1 = put("t1", [P, TOP * TILES])
    m.tab = put("tab", [P, 3, COLS])
    m.tok_idx = put("tok_idx", [P, COLS], U32)
    m.dst_idx = put("dst_idx", [P, COLS], U32)
    m.ovx = put("ovx", [P, OV, EXPERTS])
    m.ovf = put("ovf", [P, OV + 1])
    m.ov_tab = put("ov_tab", [P, OV + 1], I32)
    at[0] = after_ht
    m.rowoh = put("rowoh", [P, TOP * TILES, P])
    m.coloh = put("coloh", [P, TOP * TILES, COLS])
    at[0] = region
    m.xg = put("xg", [P, 2, D])
    m.xt_hi = put("xt_hi", [P, 2, DC, P], F32R)
    m.xt_lo = put("xt_lo", [P, 2, DC, P], F32R)
    m.sil = put("sil", [P, FF])
    m.hid = put("hid", [P, FF])
    m.hidt_hi = put("hidt_hi", [P, FF], F32R)
    m.hidt_lo = put("hidt_lo", [P, FF], F32R)
    m.y = put("y", [P, 2, D])
    m.tok_col = put("tok_col", [P, 2, 8], U32)
    m.dst_col = put("dst_col", [P, 2, 8], U32)
    at[0] = region
    m.pair = put("pair", [P, 4, TOP, D])
    m.o_out = put("o_out", [P, 2, D])

    m.tr = [ctx.enter_context(nc.psum_tensor(f"ps_tr{k}", [P, 2 * BANK], F32)) for k in range(2)]
    m.pj = [ctx.enter_context(nc.psum_tensor(f"ps_pj{k}", [P, BANK], F32)) for k in range(2)]
    m.ps = [ctx.enter_context(nc.psum_tensor(f"ps_aux{k}", [P, BANK], F32)) for k in range(2)]
    return m


def semaphores(nc, ctx):
    def sem(name):
        return ctx.enter_context(nc.semaphore(name))

    def stream(tag):
        q = Names()
        q.full = [sem(f"{tag}_raw_full{k}") for k in range(RAW)]
        q.hi, q.split = sem(f"{tag}_hi_done"), sem(f"{tag}_split_done")
        return q

    def experts(tag, ring):
        names = ("used", "tok_col", "dst_col", "xt_tr", "xt_hi", "xt_lo", "sil", "hid", "ht_tr", "ht_hi",
                 "ht_lo", "y_act", "y_dve")
        q = Names()
        q.ring = ring
        q.xg_full = [sem(f"{tag}_xg_full{k}") for k in range(ring)]
        q.y_out, q.y_free, q.go = sem(f"{tag}_y_out"), sem(f"{tag}_y_free"), sem(f"{tag}_dma_go")
        (q.used, q.tok_col, q.dst_col, q.xt_tr, q.xt_hi, q.xt_lo, q.sil, q.hid, q.ht_tr, q.ht_hi, q.ht_lo,
         q.y_act, q.y_dve) = [sem(f"{tag}_{n}") for n in names]
        return q

    s = Names()
    s.w = stream("w")
    s.ov = [stream(f"ov{k}") for k in range(2)]
    s.e = experts("e", 2)
    s.oe = [experts(f"oe{k}", 1) for k in range(2)]
    s.meet = [sem(f"met_{n}") for n in ("pool", "act", "dve", "pe")]
    s.const = sem("const_ready")
    s.const_step = sem("const_step")
    s.x_in = [sem(f"x_in{k}") for k in range(2)]
    s.gain = sem("gain_in")
    s.sq, s.std, s.h, s.n_tr, s.n_hi, s.n_lo = [sem(n) for n in (
        "norm_squares", "norm_std", "norm_h", "norm_turned", "norm_hi", "norm_lo")]
    s.h_free = sem("h_slot_free")
    s.h_out = [sem(f"h_out{k}") for k in range(2)]
    s.step = sem("dve_step")
    s.given_back = sem("raw_given_back")
    s.routed = sem("routed")
    s.pj_full, s.pj_act, s.pj_dve = sem("group_full"), sem("group_by_act"), sem("group_by_dve")
    s.gin, s.gup = sem("gate_in"), sem("gate_up_in")
    s.z_mm, s.z_dve, s.z_act, s.z_g, s.dec_mm, s.dec_act = [sem(n) for n in (
        "z_made", "z_biased", "z_logged", "log_decay", "decay_summed", "decay_exp")]
    s.dec_out = [sem(f"decay_out{k}") for k in range(2)]
    s.head_in, s.e_now, s.e_std = sem("head_in"), sem("e_now_ready"), sem("o_rstd")
    s.u_full, s.s_upd, s.o_mm, s.o_evac, s.o_std, s.og, s.ot_tr, s.ot_hi, s.ot_lo, s.rgh = [sem(n) for n in (
        "update_made", "state_ready", "o_made", "o_out", "o_std", "o_gated", "o_turned", "o_hi", "o_lo", "r_gained")]
    s.ws_in, s.bn, s.v_in = sem("ws_in"), sem("v_stats"), sem("v_in")
    s.ws_tr, s.ws_masked, s.lvar, s.v_free = sem("ws_turned"), sem("ws_masked"), sem("v_variance"), sem("v_slot_free")
    s.v_st = sem("v_stored")
    s.mix_full, s.mix_used, s.ln_hat, s.vn, s.gt, s.gt_hi, s.gt_lo = [sem(n) for n in (
        "mix_made", "mix_read", "v_normed", "v_ready", "g_ready", "g_hi", "g_lo")]
    s.r_in, s.r_hi, s.r_lo, s.r_mm, s.r_act = [sem(n) for n in (
        "router_in", "router_hi", "router_lo", "route_product", "route_exp")]
    s.masked, s.cleared = sem("route_one_hot"), sem("cleared")
    s.pair_in = [sem(f"pair_in{k}") for k in range(4)]
    s.sum = sem("rows_summed")
    s.fin, s.out = sem("row_final"), [sem(f"out{k}") for k in range(2)]
    return s



class Chain:

    def __init__(self, engine, sem, at=0):
        self.engine, self.sem, self.at = engine, sem, at

    def __call__(self, instruction):
        self.at += 1
        instruction.then_inc(self.sem, 1)
        self.engine.wait_ge(self.sem, self.at)


def meet(s, engine, me, n):
    engine.drain().then_inc(s.meet[me], 1)
    for other in range(4):
        if other != me:
            engine.wait_ge(s.meet[other], n)


def split_hi(act, m, st, b, landed, used=None):
    act.wait_ge(st.full[b % RAW], landed)
    if used is not None:
        act.wait_ge(*used)
    act.activation(m.w_hi[:, b % SPLIT, :], m.raw[:, b % RAW, :], ACT.Copy).then_inc(st.hi, 1)


def split_lo(dve, m, st, b, n):
    dve.wait_ge(st.hi, n + 1)
    dve.tensor_tensor(m.w_lo[:, b % SPLIT, :], m.raw[:, b % RAW, :], m.w_hi[:, b % SPLIT, :].bitcast(F32),
                      ALU.subtract).then_inc(st.split, 1)


def wait_split(pe, st, n):
    pe.wait_ge(st.split, n + 1 + RAW)


def raw_count(i, a, b):
    return i * (a // RAW * LANDED) + (b // RAW + 1) * LANDED


def ov_count(j, b):
    uses = 2 if b % RAW < BLOCK - RAW else 1
    return j * (uses * LANDED) + (b // RAW + 1) * LANDED


def group_wait(pe, s, who, base, i, g):
    n = len(who)
    owner = who[g - 2]
    done = sum(w == owner for w in who[:g - 1]) if g >= 2 else -sum(w == owner for w in who[n - 1 + g:])
    sem = s.pj_act if owner == "A" else s.pj_dve
    pe.wait_ge(sem, i * sum(w == owner for w in who) + base[owner] + done + G_CREDIT)


B_GLA = {"F": 0, "A": 0, "D": 0}
B_V = {"F": HEADS * len(G_HEAD), "A": HEADS * G_HEAD.count("A"), "D": HEADS * G_HEAD.count("D")}
B_U = {"F": B_V["F"] + SLICES * 8, "A": B_V["A"] + SLICES * 8, "D": B_V["D"]}


def three(pe, out, hi_l, lo_l, hi_r, lo_r, first, last):
    pe.matmul(out, hi_l, hi_r, start=first, stop=False)
    pe.matmul(out, hi_l, lo_r, start=False, stop=False)
    return pe.matmul(out, lo_l, hi_r, start=False, stop=last)



def sp_program(sp, m, s, d):
    for k in range(2):
        rows = d.x[0, k * SEQ // 2:(k + 1) * SEQ // 2, :].rearrange("(t p) n -> p t n", p=P)
        sp.dma_start(m.x[:, k * TILES // 2:(k + 1) * TILES // 2, :], rows).then_inc(s.x_in[k], 16)

    def slot_free(n):
        sp.wait_ge(s.w.split, n + 1)

    w_in = d.gla_w_in[0].rearrange("(p c) n -> p c n", c=DC)
    with sp.Fori(0, HEADS) as h:
        qk = m.raw[:, 0, :].rearrange("p (c n) -> p c n", c=DC)
        slot_free(h * 4 + GLA_AT)
        for part in range(2):
            sp.dma_start(qk[:, :, part * DK:(part + 1) * DK],
                         w_in[:, :, bass.ds(h * DK + part * HK, DK)]).then_inc(s.w.full[0], 16)
        for k in range(2):
            slot_free(h * 4 + GLA_AT + k + 1)
            sp.dma_start(m.raw[:, k + 1, :].rearrange("p (c n) -> p c n", c=DC),
                         w_in[:, :, bass.ds(h * DV + 2 * HK + k * HV, DV)]).then_inc(s.w.full[k + 1], LANDED)
        slot_free(h * 4 + GLA_AT + 3)
        rows = d.gla_w_out[0][bass.ds(h * DV, DV), :]
        sp.dma_start(m.raw[:, 3, :], rows.rearrange("(p c) n -> p (c n)", c=2)).then_inc(s.w.full[3], LANDED)

    sp_experts(sp, m, s, d, 0)

    s_in = d.sgu_w_in[0].rearrange("(p c) n -> p c n", c=DC)
    with sp.Fori(0, SLICES // RAW) as i:
        for k in range(RAW):
            slot_free(i * RAW + SGU_V_AT + k)
            sp.dma_start(m.raw[:, k, :].rearrange("p (c n) -> p c n", c=DC),
                         s_in[:, :, bass.ds(i * (RAW * SLICE) + HALF + k * SLICE, SLICE)]).then_inc(s.w.full[k], LANDED)
    with sp.Fori(0, SLICES // 2) as i:
        for k in range(2):
            slot_free(i * RAW + SGU_U_AT + 2 * k)
            sp.dma_start(m.raw[:, 2 * k, :].rearrange("p (c n) -> p c n", c=DC),
                         s_in[:, :, bass.ds(i * (2 * SLICE) + k * SLICE, SLICE)]).then_inc(s.w.full[2 * k], LANDED)
            slot_free(i * RAW + SGU_U_AT + 2 * k + 1)
            rows = d.sgu_w_out[0][bass.ds(i * (2 * SLICE) + k * SLICE, SLICE), :]
            sp.dma_start(m.raw[:, 2 * k + 1, :], rows.rearrange("(p c) n -> p (c n)", c=2)) \
              .then_inc(s.w.full[2 * k + 1], LANDED)

    sp_experts(sp, m, s, d, 1)
    for k in range(2):
        sp.wait_ge(s.out[k], 16 * TILES // 2)


def expert_piece(d, layer, e, b):
    w, c = ((d.moe_w1, DC), (d.moe_w3, DC), (d.moe_w2, FC))[b // 2]
    rows = w[layer][bass.ds(e, 1)].rearrange("o (p c) n -> p (o c n)", c=c)
    return rows[:, (b % 2) * PIECE:(b % 2 + 1) * PIECE]


def sp_experts(sp, m, s, d, layer):
    with sp.Fori(0, EXPERTS // 2) as i:
        for b in range(2 * BLOCK):
            sp.wait_ge(s.w.split, i * (2 * BLOCK) + MOE_AT[layer] + b + 1)
            sp.dma_start(m.raw[:, b % RAW, :], expert_piece(d, layer, i * 2 + b // BLOCK, b % BLOCK)) \
              .then_inc(s.w.full[b % RAW], LANDED)
    ov = s.ov[layer]
    sp.wait_ge(s.routed, layer + 1)
    blocks = sp.value_load(m.ov_tab[0:1, OV:OV + 1], min_val=0, max_val=OV)
    with sp.If(blocks > 0):
        sp.wait_ge(s.w.split, MOE_AT[layer] + EXPERTS * BLOCK + RAW)
        with sp.Fori(0, blocks) as j:
            e = sp.value_load(m.ov_tab[0:1, bass.ds(j, 1)], min_val=0, max_val=EXPERTS - 1)
            for b in range(BLOCK):
                sp.wait_ge(ov.split, j * BLOCK + max(b + 1, RAW))
                sp.dma_start(m.raw[:, b % RAW, :], expert_piece(d, layer, e, b)).then_inc(ov.full[b % RAW], LANDED)
        sp.wait_ge(ov.split, blocks * BLOCK + RAW)
        sp.sem_inc(s.given_back, 1)



def norm_pool(pool, m, s, d, n, gain, stored=None):
    pool.dma_start(m.gain[:], gain.partition_broadcast(P)).then_inc(s.gain, 16)
    if stored is not None:
        for t in range(TILES + 1):
            if t < TILES:
                pool.wait_ge(s.h, n * TILES + t + 1)
                pool.dma_start(d.h[t * P:(t + 1) * P, :], m.h[:, t % 2, :]).then_inc(s.h_out[t % 2], 16)
            if t >= 1:
                pool.wait_ge(s.h_out[(t - 1) % 2], 16 * (stored * TILES // 2 + (t - 1) // 2 + 1))
                pool.sem_inc(s.h_free, 1)


def norm_std(act, m, s, n):
    for t in range(TILES):
        if n == 0 and t % (TILES // 2) == 0:
            act.wait_ge(s.x_in[t // (TILES // 2)], 16)
        if t > 0:
            act.wait_ge(s.sq, n * TILES + t)
        act.activation(m.h[:, 0, :], m.x[:, t, :], ACT.Square, accum_out=m.ss[:, t:t + 1]).then_inc(s.sq, 1)
    act.wait_ge(s.sq, (n + 1) * TILES)
    act.activation(m.std[:], m.ss[:], ACT.Sqrt, scale=1.0 / D, bias=m.eps[:, 0:1]).then_inc(s.std, 1)


def norm_act(act, m, s, n):
    norm_std(act, m, s, n)
    with act.Fori(0, TILES // 2) as i:
        for b in range(2):
            act.wait_ge(s.n_tr, i * 2 + n * TILES + b + 3)
            act.activation(m.ht_hi[:, :, bass.ds(i * (2 * P) + b * P, P)],
                           m.tr[b][:].rearrange("p (c n) -> p c n", c=DC), ACT.Copy).then_inc(s.n_hi, 1)


def norm_dve(dve, m, s, n, step, stored=None):
    dve.wait_ge(s.std, n + 1)
    dve.wait_ge(s.gain, 16 * (n + 1))
    step(dve.reciprocal(m.rstd[:], m.std[:]))
    with dve.Fori(0, TILES // 2) as i:
        for b in range(2):
            t = i * 2 + b
            dve.wait_ge(s.n_tr, i * 2 + n * TILES + b + 1)
            if stored is not None:
                dve.wait_ge(s.h_free, i * 2 + stored * TILES + b + 1)
            dve.scalar_tensor_tensor(m.h[:, b, :], m.x[:, bass.ds(t, 1), :].rearrange("p o n -> p (o n)"),
                                     m.rstd[:, bass.ds(t, 1)], m.gain[:], ALU.mult, ALU.mult).then_inc(s.h, 1)
        for b in range(2):
            dve.wait_ge(s.n_hi, i * 2 + n * TILES + b + 1)
            cols = bass.ds(i * (2 * P) + b * P, P)
            dve.tensor_tensor(m.ht_lo[:, :, cols], m.tr[b][:].rearrange("p (c n) -> p c n", c=DC),
                              m.ht_hi[:, :, cols].bitcast(F32), ALU.subtract).then_inc(s.n_lo, 1)


def norm_pe(pe, m, s, n):
    with pe.Fori(0, TILES // 2) as i:
        for b in range(2):
            pe.wait_ge(s.h, i * 2 + n * TILES + b + 1)
            pe.wait_ge(s.n_lo, i * 2 + n * TILES + b + 1)
            rows = m.h[:, b, :].rearrange("p (n c) -> p c n", c=DC)
            for c in range(DC):
                last = pe.transpose(m.tr[b][:, c * P:(c + 1) * P], rows[:, c, :], m.ident[:])
            last.then_inc(s.n_tr, 1)
    pe.wait_ge(s.n_lo, (n + 1) * TILES + 2)


def project(pe, m, s, i, base, g, who, out, stationary, moving, wait=True):
    group_wait(pe, s, who, base, i, g)
    for c in range(DC):
        last = three(pe, out, stationary(c, 0), stationary(c, 1), moving(c, 0), moving(c, 1), c == 0, c == DC - 1)
    last.then_inc(s.pj_full, 1)



def gates_pool(pool, m, s, d):
    pool.dma_start(m.glr_raw[:].rearrange("p (c r) -> p c r", c=DC),
                   d.gla_w_in[0].rearrange("(p c) n -> p c n", c=DC)[:, :, 2 * HK + 2 * HV:]).then_inc(s.gin, 16)
    pool.dma_start(m.bgate[:], d.gla_b_gate[0].partition_broadcast(P)).then_inc(s.gin, 16)
    pool.wait_ge(s.n_tr, TILES + 2)
    pool.memset(m.gate_up[:], 0.0).then_inc(s.cleared, 1)
    pool.wait_ge(s.cleared, 1)
    for t in range(TILES):
        pool.dma_start(m.gate_up[t * RANK:(t + 1) * RANK, t, :], d.gla_w_gate_up[0]).then_inc(s.gup, 16)
    with pool.Fori(0, TILES // 2) as i:
        for b in range(2):
            pool.wait_ge(s.dec_act, i * 2 + b + 1)
            pool.dma_start(d.dec[bass.ds(i * (2 * P) + b * P, P), :], m.z[:, b, :]).then_inc(s.dec_out[b], 16)


def gates_pe(pe, m, s):
    pe.wait_ge(s.z_g, 1)
    for t in range(TILES):
        for c in range(DC):
            r = slice(c * RANK, (c + 1) * RANK)
            last = three(pe, m.ps[0][:, t * RANK:(t + 1) * RANK], m.ht_hi[:, c, t * P:(t + 1) * P],
                         m.ht_lo[:, c, t * P:(t + 1) * P], m.glr_hi[:, r], m.glr_lo[:, r], c == 0, c == DC - 1)
    last.then_inc(s.z_mm, 1)
    pe.wait_ge(s.z_act, 1)
    pe.transpose(m.ps[1][:, 0:P], m.glr[:], m.ident[:]).then_inc(s.z_mm, 1)
    pe.wait_ge(s.z_act, 2)
    pe.wait_ge(s.gup, 16 * TILES)
    for t in range(TILES + 1):
        if t < TILES:
            if t >= 2:
                pe.wait_ge(s.z_dve, 2 * t - 3)
            pe.matmul(m.pj[t % 2][:], m.glr_t[:], m.gate_up[:, t, :], start=True, stop=True).then_inc(s.z_mm, 1)
        if t >= 1:
            u = t - 1
            pe.wait_ge(s.z_g, u + 2)
            if u >= 2:
                pe.wait_ge(s.dec_act, u - 1)
            pe.matmul(m.ps[u % 2][:], m.after[:], m.logsig[:, u % 2, :], start=True, stop=True)
            for h in range(HEADS):
                last = pe.matmul(m.tr[0][:, h * CHUNKS + 2 * u:h * CHUNKS + 2 * u + 2],
                                 m.logsig[:, u % 2, h * DK:(h + 1) * DK], m.halves[:], start=True, stop=True)
            last.then_inc(s.dec_mm, 1)


def gates_act(act, m, s):
    act.wait_ge(s.z_mm, 1)
    act.activation(m.glr[:], m.ps[0][:, 0:P], ACT.Copy).then_inc(s.z_act, 1)
    act.wait_ge(s.z_mm, 2)
    act.activation(m.glr_t[:], m.ps[1][:, 0:P], ACT.Copy).then_inc(s.z_act, 1)
    for t in range(TILES):
        act.wait_ge(s.z_dve, 2 * t + 2)
        act.activation(m.zexp[:, t % 2, :], m.zexp[:, t % 2, :], ACT.Exp).then_inc(s.z_act, 1)
        act.wait_ge(s.z_act, 2 * t + 3)
        act.activation(m.zexp[:, t % 2, :], m.zexp[:, t % 2, :], ACT.Ln, bias=m.one[:, 0:1]).then_inc(s.z_act, 1)
        if t >= 1:
            decay_exp(act, m, s, t - 1)
    decay_exp(act, m, s, TILES - 1)
    act.activation(m.e_end[:], m.tr[0][:, 0:HEADS * CHUNKS], ACT.Exp, scale=1.0 / TAU)


def decay_exp(act, m, s, t):
    act.wait_ge(s.dec_mm, t + 1)
    act.activation(m.z[:, t % 2, :], m.ps[t % 2][:], ACT.Exp, scale=1.0 / TAU).then_inc(s.dec_act, 1)


def gates_dve(dve, m, s, step):
    dve.wait_ge(s.gin, 32)
    step(dve.tensor_copy(m.glr_hi[:], m.glr_raw[:]))
    dve.tensor_tensor(m.glr_lo[:], m.glr_raw[:], m.glr_hi[:].bitcast(F32), ALU.subtract).then_inc(s.z_g, 1)
    for t in range(TILES):
        z, e = m.z[:, t % 2, :], m.zexp[:, t % 2, :]
        dve.wait_ge(s.z_mm, t + 3)
        if t >= 2:
            dve.wait_ge(s.dec_out[t % 2], 16 * (t // 2))
        dve.tensor_tensor(z, m.pj[t % 2][:], m.bgate[:], ALU.add).then_inc(s.z_dve, 1)
        dve.wait_ge(s.z_dve, 2 * t + 1)
        dve.scalar_tensor_tensor(e, z, -1.0, z, ALU.mult, ALU.min).then_inc(s.z_dve, 1)
        dve.wait_ge(s.z_act, 2 * t + 4)
        if t >= 2:
            dve.wait_ge(s.dec_mm, t - 1)
        dve.scalar_tensor_tensor(m.logsig[:, t % 2, :], z, 0.0, e, ALU.min, ALU.subtract).then_inc(s.z_g, 1)



def heads_pool(pool, m, s, d):
    def load(h):
        pool.dma_start(m.head_g[:], d.gla_head_g[0][bass.ds(h, 1), :].partition_broadcast(P)
                       .rearrange("q o n -> q (o n)")).then_inc(s.head_in, 16)
        pool.dma_start(m.dec[:], d.dec[:, bass.ds(h * DK, DK)].rearrange("(t p) k -> p t k", p=P)).then_inc(s.head_in, 16)

    for b in range(2):
        pool.wait_ge(s.dec_out[b], 16 * TILES // 2)
    load(0)
    with pool.Fori(1, HEADS) as h:
        pool.wait_ge(s.og, h * TILES + 2)
        load(h)


def heads_pe(pe, m, s):
    with pe.Fori(0, HEADS) as h:
        w = [m.w_hi, m.w_lo]
        ht = [m.ht_hi, m.ht_lo]
        wait_split(pe, s.w, h * 4 + GLA_AT)
        for g in range(2):
            project(pe, m, s, h, B_GLA, g, G_HEAD, m.pj[g % 2][:],
                    lambda c, part: w[part][:, 0, c * SLICE:c * SLICE + DK],
                    lambda c, part: ht[part][:, c, g * BANK:(g + 1) * BANK])
        for t in range(TILES):
            project(pe, m, s, h, B_GLA, 2 + t, G_HEAD, m.pj[t % 2][:, 0:DK],
                    lambda c, part: ht[part][:, c, t * P:(t + 1) * P],
                    lambda c, part: w[part][:, 0, c * SLICE + DK:(c + 1) * SLICE])
        wait_split(pe, s.w, h * 4 + GLA_AT + 1)
        for t in range(TILES):
            project(pe, m, s, h, B_GLA, 10 + t, G_HEAD, m.pj[t % 2][:, 0:DV],
                    lambda c, part: ht[part][:, c, t * P:(t + 1) * P],
                    lambda c, part: w[part][:, 1, c * SLICE:(c + 1) * SLICE])
        pe.wait_ge(s.pj_dve, h * G_HEAD.count("D") + TILES + G_CREDIT)
        pe.wait_ge(s.pj_act, h * G_HEAD.count("A") + 2 + TILES + G_CREDIT)
        for c in range(CHUNKS + 1):
            if c < CHUNKS:
                rows = slice(c % 2 * CHUNK, (c % 2 + 1) * CHUNK)
                pe.wait_ge(s.s_upd, h * CHUNKS + c + 1)
                pe.matmul(m.ps[c % 2][:, 0:DV], m.kd[rows, c // 2, :], m.v[rows, c // 2, :],
                          start=True, stop=True).then_inc(s.u_full, 1)
            if c >= 1:
                u = c - 1
                pe.wait_ge(s.s_upd, h * CHUNKS + u + 3)
                if u % 2 == 0:
                    pe.wait_ge(s.o_evac, h * TILES + u // 2 + 1)
                pe.matmul(m.tr[u // 2 % 2][u % 2 * CHUNK:(u % 2 + 1) * CHUNK, 0:DV],
                          m.q_t[:, u * CHUNK:(u + 1) * CHUNK], m.state[:, u % 2, :],
                          start=True, stop=True).then_inc(s.o_mm, 1)
        wait_split(pe, s.w, h * 4 + GLA_AT + 2)

        def turn(t):
            pe.wait_ge(s.og, h * TILES + t + 3)
            pe.wait_ge(s.ot_lo, h * TILES + t + 1)
            rows = m.o[:, t, :].rearrange("p (n c) -> p c n", c=2)
            for c in range(2):
                last = pe.transpose(m.tr[t % 2][:, c * P:(c + 1) * P], rows[:, c, :], m.ident[:])
            last.then_inc(s.ot_tr, 1)

        for t in range(TILES):
            project(pe, m, s, h, B_GLA, 18 + t, G_HEAD, m.pj[t % 2][:, 0:DV],
                    lambda c, part: ht[part][:, c, t * P:(t + 1) * P],
                    lambda c, part: w[part][:, 0, c * SLICE:(c + 1) * SLICE])
            if t >= 1:
                turn(t - 1)
        turn(TILES - 1)
        wait_split(pe, s.w, h * 4 + GLA_AT + 3)
        ot = [m.ot_hi, m.ot_lo]
        for t in range(TILES):
            pe.wait_ge(s.ot_lo, h * TILES + t + 3)
            for half in range(2):
                out_group(pe, m, s, h, B_GLA, 26 + 2 * t + half, G_HEAD, half,
                          lambda c, part: ot[part][:, t, c * P:(c + 1) * P])


def out_group(pe, m, s, i, base, g, who, half, stationary):
    group_wait(pe, s, who, base, i, g)
    for c in range(2):
        at = c * D + half * BANK
        last = three(pe, m.pj[g % 2][:], stationary(c, 0), stationary(c, 1), m.w_hi[:, 1, at:at + BANK],
                     m.w_lo[:, 1, at:at + BANK], c == 0, c == 1)
    last.then_inc(s.pj_full, 1)


def heads_act(act, m, s):
    with act.Fori(0, HEADS) as h:
        def full(g):
            act.wait_ge(s.pj_full, h * len(G_HEAD) + g + 1)

        def after(g):
            return s.pj_full, h * len(G_HEAD) + g + 1

        for g in range(2):
            full(g)
            act.activation(m.q_t[:, g * BANK:(g + 1) * BANK], m.pj[g][:], ACT.Copy, scale=DK ** -0.5).then_inc(s.pj_act, 1)
        split_hi(act, m, s.w, 2, raw_count(h, 4, 2), after(9))
        for t in range(TILES):
            full(10 + t)
            act.activation(m.v[:, t, :], m.pj[t % 2][:, 0:DV], ACT.Copy).then_inc(s.pj_act, 1)
        split_hi(act, m, s.w, 3, raw_count(h, 4, 3), after(17))
        for t in range(TILES):
            act.wait_ge(s.o_mm, h * CHUNKS + 2 * t + 4)
            act.activation(m.o[:, t, :], m.tr[t % 2][:, 0:DV], ACT.Copy)
            act.wait_ge(s.o_evac, h * TILES + t + 2)
            act.activation(m.junk[:], m.tr[t % 2][:, 0:DV], ACT.Square, accum_out=m.oss[:, t:t + 1]).then_inc(s.o_evac, 1)
        act.wait_ge(s.o_evac, h * TILES + TILES + 2)
        act.activation(m.ostd[:], m.oss[:], ACT.Sqrt, scale=1.0 / DV, bias=m.eps[:, 0:1]).then_inc(s.o_std, 1)
        for t in range(TILES + 1):
            if t < TILES:
                full(18 + t)
                act.wait_ge(s.og, h * TILES + t + 1)
                act.activation(m.rg[:, t % 2, :], m.pj[t % 2][:, 0:DV], ACT.Silu).then_inc(s.pj_act, 1)
            if t >= 1:
                act.wait_ge(s.ot_tr, h * TILES + t)
                act.activation(m.ot_hi[:, t - 1, :], m.tr[(t - 1) % 2][:, 0:DV], ACT.Copy).then_inc(s.ot_hi, 1)
        split_hi(act, m, s.w, 4, raw_count(h, 4, 4), after(25))
        split_hi(act, m, s.w, 5, raw_count(h, 4, 5), after(41))


def heads_dve(dve, m, s):
    with dve.Fori(0, HEADS) as h:
        dve.wait_ge(s.head_in, h * 32 + 32)
        dve.tensor_copy(m.e_now[:], m.e_end[:, bass.ds(h * CHUNKS, CHUNKS)]).then_inc(s.e_now, 1)
        for t in range(TILES):
            dve.wait_ge(s.pj_full, h * len(G_HEAD) + t + 3)
            dve.tensor_tensor(m.kd[:, t, :], m.pj[t % 2][:, 0:DK], m.dec[:, t, :], ALU.mult).then_inc(s.pj_dve, 1)
        split_lo(dve, m, s.w, 2, h * 4 + GLA_AT + 2)
        dve.wait_ge(s.e_now, h + 1)
        for c in range(CHUNKS):
            dve.wait_ge(s.u_full, h * CHUNKS + c + 1)
            dve.wait_ge(s.o_mm, h * CHUNKS + c + 1)
            if c == 0:
                dve.tensor_copy(m.state[:, 0, :], m.ps[0][:, 0:DV]).then_inc(s.s_upd, 1)
            else:
                dve.wait_ge(s.s_upd, h * CHUNKS + c + 2)
                dve.scalar_tensor_tensor(m.state[:, c % 2, :], m.state[:, (c - 1) % 2, :], m.e_now[:, c:c + 1],
                                         m.ps[c % 2][:, 0:DV], ALU.mult, ALU.add).then_inc(s.s_upd, 1)
        split_lo(dve, m, s.w, 3, h * 4 + GLA_AT + 3)
        dve.wait_ge(s.o_std, h + 1)
        dve.reciprocal(m.orstd[:], m.ostd[:]).then_inc(s.e_std, 1)
        dve.wait_ge(s.e_std, h + 1)
        for t in range(TILES + 1):
            if t < TILES:
                dve.wait_ge(s.pj_act, h * G_HEAD.count("A") + 11 + t + G_CREDIT)
                dve.tensor_tensor(m.rg[:, t % 2, :], m.rg[:, t % 2, :], m.head_g[:], ALU.mult).then_inc(s.rgh, 1)
                dve.wait_ge(s.rgh, h * TILES + t + 1)
                dve.scalar_tensor_tensor(m.o[:, t, :], m.o[:, t, :], m.orstd[:, t:t + 1], m.rg[:, t % 2, :],
                                         ALU.mult, ALU.mult).then_inc(s.og, 1)
            if t >= 1:
                dve.wait_ge(s.ot_hi, h * TILES + t)
                dve.tensor_tensor(m.ot_lo[:, t - 1, :], m.tr[(t - 1) % 2][:, 0:DV],
                                  m.ot_hi[:, t - 1, :].bitcast(F32), ALU.subtract).then_inc(s.ot_lo, 1)
        split_lo(dve, m, s.w, 4, h * 4 + GLA_AT + 4)
        for g in range(2 * TILES):
            dve.wait_ge(s.pj_full, h * len(G_HEAD) + 27 + g)
            add_rows(dve, m, s, g, g % 2)
        split_lo(dve, m, s.w, 5, h * 4 + GLA_AT + 5)


def add_rows(dve, m, s, g, bank):
    part = m.x[:, g // 2, g % 2 * BANK:(g % 2 + 1) * BANK]
    dve.tensor_tensor(part, part, m.pj[bank][:], ALU.add).then_inc(s.pj_dve, 1)



def sgu_pool(pool, m, s, d):
    pool.dma_start(m.ws[:], d.sgu_w_s[0].rearrange("g t q -> t g q")).then_inc(s.ws_in, 16)
    with pool.Fori(0, SLICES // RAW) as i:
        for b in range(RAW):
            pool.wait_ge(s.pj_act, i * (RAW * 8) + B_V["A"] + 8 * (b + 1) + G_CREDIT)
            pool.dma_start(d.v[:, bass.ds(i * (RAW * SLICE) + b * SLICE, SLICE)].rearrange("(t p) c -> p t c", p=P),
                           m.v_out[:, b % 2, :, :]).then_inc(s.v_st, 16)
            pool.wait_ge(s.v_st, i * (16 * RAW) + 16 * (b + 1))
            pool.sem_inc(s.v_free, 1)
    pool.dma_start(m.bs[:], d.sgu_b_s[0].rearrange("g t -> (g t)").partition_broadcast(P)).then_inc(s.ws_in, 16)

    def load(j):
        cols = bass.ds(j * SLICE, SLICE)
        pool.dma_start(m.v_s[:], d.v[:, cols].rearrange("(t p) c -> p t c", p=P)).then_inc(s.v_in, 16)
        pool.dma_start(m.ln_g[:], d.sgu_ln_g[0][cols].partition_broadcast(P)).then_inc(s.v_in, 16)
        pool.dma_start(m.ln_b[:], d.sgu_ln_b[0][cols].partition_broadcast(P)).then_inc(s.v_in, 16)

    def scale(j):
        pool.wait_ge(s.ln_hat, j + 2)
        gain = m.ln_g[:].unsqueeze(1).to_broadcast([P, TILES, SLICE])
        shift = m.ln_b[:].unsqueeze(1).to_broadcast([P, TILES, SLICE])
        pool.tensor_tensor(m.v_s[:], m.v_s[:], gain, ALU.mult).then_inc(s.vn, 1)
        pool.wait_ge(s.vn, j * 2 + 1)
        pool.tensor_tensor(m.v_s[:], m.v_s[:], shift, ALU.add).then_inc(s.vn, 1)

    load(0)
    scale(0)
    with pool.Fori(1, SLICES) as j:
        pool.wait_ge(s.mix_full, j * 4)
        load(j)
        scale(j)


def sgu_pe(pe, m, s):
    ht = [m.ht_hi, m.ht_lo]
    w = [m.w_hi, m.w_lo]
    pe.wait_ge(s.ws_masked, 1)
    for g in range(SG):
        last = pe.transpose(m.ps[0][:, g * P:(g + 1) * P], m.ws[:, g, :], m.ident[:])
    last.then_inc(s.ws_tr, 1)
    with pe.Fori(0, SLICES // RAW) as i:
        for b in range(RAW):
            wait_split(pe, s.w, i * RAW + SGU_V_AT + b)
            for t in range(TILES):
                pe.wait_ge(s.pj_act, i * (RAW * 8) + B_V["A"] + b * 8 + t - 1 + G_CREDIT)
                for c in range(DC):
                    cols = slice(c * SLICE, (c + 1) * SLICE)
                    rows = slice(t * P, (t + 1) * P)
                    last = three(pe, m.pj[t % 2][:, 0:SLICE], ht[0][:, c, rows], ht[1][:, c, rows],
                                 w[0][:, b % 2, cols], w[1][:, b % 2, cols], c == 0, c == DC - 1)
                last.then_inc(s.pj_full, 1)
    gt = [m.gt_hi, m.gt_lo]
    with pe.Fori(0, SLICES // 2) as i:
        for b in range(2):
            pe.wait_ge(s.vn, i * 4 + 2 * b + 2)
            wait_split(pe, s.w, i * RAW + SGU_U_AT + 2 * b)
            vt = m.v_s[:].rearrange("p t (n c) -> p t c n", c=2)
            for q in range(4):
                half, c = q // 2, q % 2
                pe.wait_ge(s.mix_used, i * 8 + 4 * b + q + 1)
                for k in range(4):
                    last = pe.matmul(m.ps[q % 2][:, k * P:(k + 1) * P], vt[:, half * 4 + k, c, :],
                                     m.ws_t[:, bass.ds(i * P, P)], start=True, stop=True)
                last.then_inc(s.mix_full, 1)
                sgu_group_wait(pe, s, i, b, q)
                for k in range(DC):
                    cols = [w[part][:, 0, k * SLICE:(k + 1) * SLICE].rearrange("p (n c) -> p c n", c=2)[:, c, :]
                            for part in range(2)]
                    last = three(pe, m.pj[q % 2][:], cols[0], cols[1], ht[0][:, k, half * BANK:(half + 1) * BANK],
                                 ht[1][:, k, half * BANK:(half + 1) * BANK], k == 0, k == DC - 1)
                last.then_inc(s.pj_full, 1)
            wait_split(pe, s.w, i * RAW + SGU_U_AT + 2 * b + 1)
            for t in range(TILES):
                if t % 4 == 0:
                    pe.wait_ge(s.gt_lo, i * 8 + 4 * b + t // 4 * 2 + 4)
                for half in range(2):
                    g = 4 + 2 * t + half
                    sgu_group_wait(pe, s, i, b, g)
                    for c in range(2):
                        at = c * D + half * BANK
                        last = three(pe, m.pj[g % 2][:], gt[0][:, c, t * P:(t + 1) * P], gt[1][:, c, t * P:(t + 1) * P],
                                     w[0][:, 1, at:at + BANK], w[1][:, 1, at:at + BANK], c == 0, c == 1)
                    last.then_inc(s.pj_full, 1)


def sgu_group_wait(pe, s, i, b, g):
    owner = G_U[g - 2]
    done = G_U[:g - 1].count(owner) if g >= 2 else g - 1
    per = G_U.count(owner)
    sem = s.pj_act if owner == "A" else s.pj_dve
    pe.wait_ge(sem, i * (2 * per) + b * per + B_U[owner] + done + G_CREDIT)


def sgu_act(act, m, s):
    split_hi(act, m, s.w, SGU_V_AT, raw_count(0, 4, SGU_V_AT))
    split_hi(act, m, s.w, SGU_V_AT + 1, raw_count(0, 4, SGU_V_AT + 1))
    act.wait_ge(s.ws_tr, 1)
    act.activation(m.ws_t[:], m.ps[0][:], ACT.Copy)
    with act.Fori(0, SLICES // RAW) as i:
        for b in range(RAW):
            act.wait_ge(s.v_free, i * RAW + b + 1)
            for t in range(TILES):
                act.wait_ge(s.pj_full, i * (RAW * 8) + B_V["F"] + 8 * b + t + 1)
                act.wait_ge(s.bn, i * (RAW * 8) + 8 * b + t + 1)
                act.activation(m.v_out[:, b % 2, t, :], m.pj[t % 2][:, 0:SLICE], ACT.Gelu).then_inc(s.pj_act, 1)
            split_hi(act, m, s.w, SGU_V_AT + b + 2, raw_count(i, 4, SGU_V_AT + b + 2))
    act.wait_ge(s.lvar, 1)
    act.activation(m.lstd[:], m.mv[:, :, 1], ACT.Sqrt, bias=m.eps[:, 0:1]).then_inc(s.lvar, 1)
    with act.Fori(0, SLICES // 2) as i:
        for b in range(2):
            for q in range(4):
                half, c = q // 2, q % 2
                act.wait_ge(s.pj_full, i * 40 + B_U["F"] + 20 * b + q + 1)
                act.wait_ge(s.gt_lo, i * 8 + 4 * b + q + 1)
                act.activation(m.ut[:, q % 2, :], m.pj[q % 2][:], ACT.Gelu).then_inc(s.pj_act, 1)
                act.wait_ge(s.gt, i * 8 + 4 * b + q + 1)
                act.activation(m.gt_hi[:, c, half * BANK:(half + 1) * BANK], m.ut[:, q % 2, :], ACT.Copy).then_inc(s.gt_hi, 1)
            split_hi(act, m, s.w, SGU_U_AT + 2 * b + 2, raw_count(i, 4, SGU_U_AT + 2 * b + 2))
            split_hi(act, m, s.w, SGU_U_AT + 2 * b + 3, raw_count(i, 4, SGU_U_AT + 2 * b + 3),
                     (s.pj_full, i * 40 + B_U["F"] + 20 * (b + 1)))


def sgu_dve(dve, m, s, step):
    split_lo(dve, m, s.w, SGU_V_AT, SGU_V_AT)
    split_lo(dve, m, s.w, SGU_V_AT + 1, SGU_V_AT + 1)
    dve.wait_ge(s.ws_in, 16)
    dve.memset(m.ws[0:CHUNK, :, CHUNK:P], 0.0).then_inc(s.ws_masked, 1)
    with dve.Fori(0, SLICES // RAW) as i:
        for b in range(RAW):
            for t in range(TILES):
                dve.wait_ge(s.pj_act, i * (RAW * 8) + B_V["A"] + 8 * b + t + 1 + G_CREDIT)
                dve.bn_stats(m.stats[:, t, bass.ds(i * (RAW * 6) + b * 6, 6)], m.v_out[:, b % 2, t, :]).then_inc(s.bn, 1)
            split_lo(dve, m, s.w, SGU_V_AT + b + 2, i * RAW + SGU_V_AT + b + 2)
    dve.wait_ge(s.bn, SLICES * TILES + 16)
    for t in range(TILES):
        last = dve.bn_aggr(m.mv[:, t, :], m.stats[:, t, :])
    last.then_inc(s.lvar, 1)
    dve.wait_ge(s.ws_in, 32)
    dve.wait_ge(s.lvar, 2)
    step(dve.reciprocal(m.lrstd[:], m.lstd[:]))
    step(dve.scalar_tensor_tensor(m.lshift[:], m.mv[:, :, 0], -1.0, m.lrstd[:], ALU.mult, ALU.mult))
    dve.drain().then_inc(s.ln_hat, 1)

    def normalise(j):
        dve.wait_ge(s.v_in, j * 48 + 48)
        for t in range(TILES):
            last = dve.tensor_scalar(m.v_s[:, t, :], m.v_s[:, t, :], m.lrstd[:, t:t + 1], m.lshift[:, t:t + 1],
                                     ALU.mult, ALU.add)
        last.then_inc(s.ln_hat, 1)

    def slice_(i, b, last):
        for q in range(4):
            half, c = q // 2, q % 2
            dve.wait_ge(s.mix_full, i * 8 + 4 * b + q + 1)
            bias = m.bs[:, bass.ds(i * P, P)].unsqueeze(1).to_broadcast([P, 4, P])
            dve.tensor_tensor(m.mix[:].rearrange("p (k t) -> p k t", k=4),
                              m.ps[q % 2][:].rearrange("p (k t) -> p k t", k=4), bias, ALU.add).then_inc(s.mix_used, 1)
            dve.wait_ge(s.mix_used, i * 8 + 4 * b + q + 3)
            dve.wait_ge(s.pj_act, i * 8 + B_U["A"] + 4 * b + q + 1 + G_CREDIT)
            dve.tensor_tensor(m.ut[:, q % 2, :], m.ut[:, q % 2, :], m.mix[:], ALU.mult).then_inc(s.gt, 1)
            dve.wait_ge(s.gt_hi, i * 8 + 4 * b + q + 1)
            cols = slice(half * BANK, (half + 1) * BANK)
            dve.tensor_tensor(m.gt_lo[:, c, cols], m.ut[:, q % 2, :], m.gt_hi[:, c, cols].bitcast(F32),
                              ALU.subtract).then_inc(s.gt_lo, 1)
        split_lo(dve, m, s.w, SGU_U_AT + 2 * b + 2, i * RAW + SGU_U_AT + 2 * b + 2)
        for g in range(2 * TILES):
            dve.wait_ge(s.pj_full, i * 40 + B_U["F"] + 20 * b + 5 + g)
            add_rows(dve, m, s, g, g % 2)
            if g == 3 and not last:
                normalise(i * 2 + b + 1)
        split_lo(dve, m, s.w, SGU_U_AT + 2 * b + 3, i * RAW + SGU_U_AT + 2 * b + 3)

    normalise(0)
    with dve.Fori(0, SLICES // 2 - 1) as i:
        slice_(i, 0, False)
        slice_(i, 1, False)
    slice_(SLICES // 2 - 1, 0, False)
    slice_(SLICES // 2 - 1, 1, True)



def route_pool(pool, m, s, d, layer):
    pool.dma_start(m.r_raw[:, :, 0:NG], d.moe_w_group[layer].rearrange("(p c) g -> p c g", c=DC)).then_inc(s.r_in, 16)
    for g in range(NG):
        at = NG + g * NE
        pool.dma_start(m.r_raw[:, :, at:at + NE], d.moe_w_sub[layer][g].rearrange("(p c) e -> p c e", c=DC)).then_inc(s.r_in, 16)
    pool.dma_start(m.r_bias[:, 0:NG], d.moe_b_group[layer].partition_broadcast(P)).then_inc(s.r_in, 16)
    pool.dma_start(m.r_bias[:, NG:ROUTES], d.moe_b_sub[layer].rearrange("g e -> (g e)").partition_broadcast(P)).then_inc(s.r_in, 16)


ROUTER_LOADS = 16 * (NG + 3)


def route_pe(pe, m, s, layer):
    pe.wait_ge(s.r_lo, layer + 1)
    for t in range(TILES):
        rows = slice(t * P, (t + 1) * P)
        for c in range(DC):
            last = three(pe, m.ps[0][:, t * ROUTES:(t + 1) * ROUTES], m.ht_hi[:, c, rows], m.ht_lo[:, c, rows],
                         m.r_hi[:, c, :], m.r_lo[:, c, :], c == 0, c == DC - 1)
    last.then_inc(s.r_mm, 1)
    pe.wait_ge(s.masked, layer * 2 + 1)
    flat = m.emask[:].rearrange("p t e -> p (t e)")
    pe.matmul(m.ps[1][:, 0:TILES * EXPERTS], m.before[:], flat, start=True, stop=True)
    pe.matmul(m.ps[0][:, 0:TILES * EXPERTS], m.ones[:], flat, start=True, stop=True).then_inc(s.r_mm, 1)
    pe.wait_ge(s.masked, layer * 2 + 2)
    for a in range(TOP * TILES):
        last = pe.matmul(m.ps[1][:, 0:COLS], m.rowoh[:, a, :], m.coloh[:, a, :], start=(a == 0), stop=(a == TOP * TILES - 1))
    last.then_inc(s.r_mm, 1)


def route_act(act, m, s, layer):
    act.wait_ge(s.r_act, layer * 4 + 1)
    act.activation(m.gexp[:], m.gexp[:], ACT.Exp).then_inc(s.r_act, 1)
    act.wait_ge(s.r_act, layer * 4 + 3)
    act.activation(m.e2[:], m.e2[:], ACT.Exp).then_inc(s.r_act, 1)


def route_dve(dve, m, s, layer, step):
    def tiles(ap, *shape):
        return ap.to_broadcast([P, *shape])

    dve.wait_ge(s.r_in, (layer + 1) * ROUTER_LOADS)
    step(dve.tensor_copy(m.r_hi[:], m.r_raw[:]))
    dve.tensor_tensor(m.r_lo[:], m.r_raw[:], m.r_hi[:].bitcast(F32), ALU.subtract).then_inc(s.r_lo, 1)
    step(dve.memset(m.glog[:], -3.0e38))
    dve.wait_ge(s.r_mm, layer * 3 + 1)
    step(dve.tensor_tensor(m.logit[:], m.ps[0][:, 0:TILES * ROUTES].rearrange("p (t r) -> p t r", t=TILES),
                           tiles(m.r_bias[:].unsqueeze(1), TILES, ROUTES), ALU.add))
    step(dve.tensor_copy(m.glog[:, :, 0:NG], m.logit[:, :, 0:NG]))
    for t in range(TILES):
        last = dve.max(m.gmax[:, t, :], m.glog[:, t, :])
    step(last)
    for t in range(TILES):
        last = dve.max_index(m.gidx[:, t, :], m.gmax[:, t, :], m.glog[:, t, :])
    step(last)
    dve.tensor_tensor(m.gexp[:], m.glog[:, :, 0:NG], tiles(m.gmax[:, :, 0:1], TILES, NG), ALU.subtract).then_inc(s.r_act, 1)
    step(dve.tensor_copy(m.gsel[:], m.gidx[:, :, 0]))
    step(dve.tensor_tensor(m.goh[:], tiles(m.count[:, 0:NG].unsqueeze(1), TILES, NG),
                           tiles(m.gsel[:].unsqueeze(2), TILES, NG), ALU.is_equal))
    for g in range(NG):
        at = NG + g * NE
        last = dve.tensor_tensor(m.sel[:, :, g, :], m.logit[:, :, at:at + NE],
                                 tiles(m.goh[:, :, g:g + 1], TILES, NE), ALU.mult)
    step(last)
    step(dve.tensor_reduce(m.chosen[:], m.sel[:].rearrange("p t g e -> p t e g"), AX_X, ALU.add))
    for t in range(TILES):
        last = dve.max(m.cmax[:, t, :], m.chosen[:, t, :])
    step(last)
    for t in range(TILES):
        last = dve.max_index(m.cidx[:, t, :], m.cmax[:, t, :], m.chosen[:, t, :])
    step(last)
    dve.wait_ge(s.r_act, layer * 4 + 2)
    dve.tensor_tensor(m.e2[:], m.cmax[:, :, 1], m.cmax[:, :, 0], ALU.subtract).then_inc(s.r_act, 1)
    step(dve.tensor_reduce(m.gw[:], m.gexp[:], AX_X, ALU.add))
    step(dve.reciprocal(m.gw[:], m.gw[:]))
    step(dve.tensor_copy(m.csel[:], m.cidx[:, :, 0:TOP]))
    for k in range(TOP):
        last = dve.scalar_tensor_tensor(m.eid[:, k, :], m.gsel[:], float(NE), m.csel[:, :, k], ALU.mult, ALU.add)
    step(last)
    eid = m.eid[:].rearrange("p k t -> p (k t)")
    n = TOP * TILES
    step(dve.tensor_tensor(m.eoh[:], tiles(m.count[:, 0:EXPERTS].unsqueeze(1), n, EXPERTS),
                           tiles(eid.unsqueeze(2), n, EXPERTS), ALU.is_equal))
    dve.tensor_tensor(m.emask[:], m.eoh[:, 0:TILES, :], m.eoh[:, TILES:, :], ALU.add).then_inc(s.masked, 1)
    dve.wait_ge(s.r_act, layer * 4 + 4)
    step(dve.tensor_scalar(m.gate[:, 0, :], m.e2[:], 1.0, None, ALU.add))
    step(dve.reciprocal(m.gate[:, 0, :], m.gate[:, 0, :]))
    step(dve.tensor_tensor(m.gate[:, 0, :], m.gate[:, 0, :], m.gw[:], ALU.mult))
    step(dve.tensor_tensor(m.gate[:, 1, :], m.gate[:, 0, :], m.e2[:], ALU.mult))
    step(dve.memset(m.pre[:, 0, :], 0.0))
    dve.wait_ge(s.r_mm, layer * 3 + 2)
    for t in range(TILES):
        step(dve.tensor_tensor(m.pre[:, t + 1, :], m.pre[:, t, :], m.ps[0][:, t * EXPERTS:(t + 1) * EXPERTS], ALU.add))
    step(dve.tensor_tensor(m.rank[:], m.ps[1][:, 0:TILES * EXPERTS].rearrange("p (t e) -> p t e", t=TILES),
                           m.pre[:, 0:TILES, :], ALU.add))
    for k in range(TOP):
        last = dve.tensor_tensor(m.pick[:, k * TILES:(k + 1) * TILES, :], m.eoh[:, k * TILES:(k + 1) * TILES, :],
                                 m.rank[:], ALU.mult)
    step(last)
    step(dve.tensor_reduce(m.rk[:], m.pick[:], AX_X, ALU.add))
    count = m.pre[:, TILES, :]
    step(dve.tensor_scalar(m.nov[:], count, float(P), None, ALU.is_gt))
    for k in range(2, SEQ // P):
        step(dve.scalar_tensor_tensor(m.nov[:], count, float(k * P), m.nov[:], ALU.is_gt, ALU.add))
    step(dve.tensor_copy(m.inc[:, 0, :], m.nov[:]))
    k, now = 1, 0
    while k < EXPERTS:
        dve.tensor_copy(m.inc[:, 1 - now, 0:k], m.inc[:, now, 0:k])
        step(dve.tensor_tensor(m.inc[:, 1 - now, k:], m.inc[:, now, k:], m.inc[:, now, 0:EXPERTS - k], ALU.add))
        k, now = 2 * k, 1 - now
    inc = m.inc[:, now, :]
    step(dve.tensor_tensor(m.ovb[:], inc, m.nov[:], ALU.subtract))
    step(dve.tensor_tensor(m.ovx[:], tiles(inc.unsqueeze(1), OV, EXPERTS),
                           tiles(m.count[:, 0:OV].unsqueeze(2), OV, EXPERTS), ALU.is_le))
    dve.tensor_copy(m.ovf[:, OV:OV + 1], inc[:, EXPERTS - 1:EXPERTS])
    step(dve.tensor_reduce(m.ovf[:, 0:OV], m.ovx[:], AX_X, ALU.add))
    step(dve.tensor_scalar(m.ovf[:, 0:OV], m.ovf[:, 0:OV], float(EXPERTS - 1), None, ALU.min))
    step(dve.tensor_copy(m.ov_tab[:], m.ovf[:]))
    step(dve.tensor_scalar(m.q[:], m.rk[:], float(P), None, ALU.is_ge))
    for k in range(2, SEQ // P):
        step(dve.scalar_tensor_tensor(m.q[:], m.rk[:], float(k * P), m.q[:], ALU.is_ge, ALU.add))
    step(dve.scalar_tensor_tensor(m.rk[:], m.q[:], -float(P), m.rk[:], ALU.mult, ALU.add))
    step(dve.tensor_tensor(m.pick[:], m.eoh[:], tiles(m.ovb[:].unsqueeze(1), n, EXPERTS), ALU.mult))
    step(dve.tensor_reduce(m.ovk[:], m.pick[:], AX_X, ALU.add))
    step(dve.scalar_tensor_tensor(m.ovk[:], m.ovk[:], float(EXPERTS - 1), m.q[:], ALU.add, ALU.add))
    step(dve.tensor_tensor(m.ovk[:], m.ovk[:], eid, ALU.subtract))
    step(dve.tensor_scalar(m.t1[:], m.q[:], 0.0, None, ALU.is_gt))
    step(dve.tensor_tensor(m.ovk[:], m.ovk[:], m.t1[:], ALU.mult))
    step(dve.tensor_tensor(m.ovk[:], m.ovk[:], eid, ALU.add))
    dve.wait_ge(s.h_free, (layer + 1) * TILES + 2)
    dve.tensor_tensor(m.rowoh[:], tiles(m.count[:].unsqueeze(1), n, P), tiles(m.rk[:].unsqueeze(2), n, P), ALU.is_equal)
    step(dve.tensor_tensor(m.coloh[:], tiles(m.count[:, 0:COLS].unsqueeze(1), n, COLS),
                           tiles(m.ovk[:].unsqueeze(2), n, COLS), ALU.is_equal))
    dve.tensor_tensor(m.coloh[:], m.coloh[:], tiles(m.label[:].unsqueeze(2), n, COLS), ALU.mult).then_inc(s.masked, 1)
    dve.wait_ge(s.r_mm, layer * 3 + 3)
    empty, dst, tok = m.tab[:, 0, :], m.tab[:, 1, :], m.tab[:, 2, :]
    step(dve.tensor_scalar(empty, m.ps[1][:, 0:COLS], 0.0, float(NOWHERE), ALU.is_equal, ALU.mult))
    step(dve.scalar_tensor_tensor(dst, m.ps[1][:, 0:COLS], -1.0, empty, ALU.add, ALU.add))
    step(dve.tensor_scalar(tok, dst, float(SEQ), -float(SEQ), ALU.is_ge, ALU.mult))
    step(dve.tensor_tensor(tok, tok, dst, ALU.add))
    step(dve.tensor_copy(m.tok_idx[:], tok))
    step(dve.tensor_copy(m.dst_idx[:], dst))
    dve.drain().then_inc(s.routed, 1)



def gather(pool, m, q, d, i, a, b, col):
    slot = b % q.ring
    pool.wait_ge(q.xt_tr, i * a + b + 1)
    pool.tensor_copy(m.tok_col[:, slot, 0:1], m.tok_idx[:, bass.ds(col, 1)]).then_inc(q.tok_col, 1)
    pool.wait_ge(q.tok_col, i * a + b + 1)
    pool.sem_inc(q.go, 1)
    pool.indirect_dma_start(out=m.xg[:, slot, :], out_offset=None, in_=d.h[:, :],
                            in_offset=bass.IndirectOffsetOnAxis(ap=m.tok_col[:, slot, 0:1], axis=0),
                            bounds_check=SEQ - 1, oob_is_err=False).then_inc(q.xg_full[slot], 16)


def uses(i, a, b, ring):
    return i * (a // ring) + (b // ring + 1)


def scatter(pool, m, q, d, i, a, b, col):
    slot = b % q.ring
    pool.tensor_copy(m.dst_col[:, slot, 0:1], m.dst_idx[:, bass.ds(col, 1)]).then_inc(q.dst_col, 1)
    pool.wait_ge(q.dst_col, i * a + b + 1)
    pool.wait_ge(q.y_act, i * a + b + 2)
    pool.wait_ge(q.y_dve, i * a + b + 2)
    pool.sem_inc(q.go, 1)
    pool.indirect_dma_start(out=d.y[:, :], out_offset=bass.IndirectOffsetOnAxis(ap=m.dst_col[:, slot, 0:1], axis=0),
                            in_=m.y[:, slot, :], in_offset=None,
                            bounds_check=ASSIGN - 1, oob_is_err=False).then_inc(q.y_out, 16)
    pool.wait_ge(q.y_out, i * (16 * a) + 16 * (b + 1))
    pool.sem_inc(q.y_free, 1)


def turn_rows(pe, m, q, i, a, b):
    slot = b % q.ring
    pe.wait_ge(q.xg_full[slot], uses(i, a, b, q.ring) * 16)
    pe.wait_ge(q.xt_lo, i * a + b + 1)
    rows = m.xg[:, slot, :].rearrange("p (n c) -> p c n", c=DC)
    for c in range(DC):
        last = pe.transpose(m.tr[0][:, c * P:(c + 1) * P], rows[:, c, :], m.ident[:])
    last.then_inc(q.xt_tr, 1)


def block_pe(pe, m, q, st, i, a, b, first_piece, next_block):
    slot = b % q.ring
    n = i * (a * BLOCK) + b * BLOCK
    pe.wait_ge(q.xt_lo, i * a + b + 2)
    for k in range(4):
        if k == 0:
            pe.wait_ge(q.sil, i * a + b + 1)
        if k == 2:
            pe.wait_ge(q.hid, i * a + b + 1)
        wait_split(pe, st, n + first_piece + k)
        for c in range(4):
            row = k % 2 * 4 + c
            cols = slice(c * FF, (c + 1) * FF)
            last = three(pe, m.pj[k // 2][:], m.xt_hi[:, slot, row, :], m.xt_lo[:, slot, row, :],
                         m.w_hi[:, k % 2, cols], m.w_lo[:, k % 2, cols], row == 0, row == DC - 1)
        last.then_inc(q.used, 1)
    if next_block:
        turn_rows(pe, m, q, i, a, b + 1)
    pe.wait_ge(q.hid, i * a + b + 2)
    pe.wait_ge(q.ht_lo, i * a + b + 1)
    hid = m.hid[:].rearrange("p (n c) -> p c n", c=FC)
    for c in range(FC):
        last = pe.transpose(m.ps[0][:, c * P:(c + 1) * P], hid[:, c, :], m.ident[:])
    last.then_inc(q.ht_tr, 1)
    pe.wait_ge(q.ht_lo, i * a + b + 2)
    pe.wait_ge(q.y_act, i * a + b + 1)
    pe.wait_ge(q.y_dve, i * a + b + 1)
    for k in range(2):
        wait_split(pe, st, n + first_piece + 4 + k)
        for half in range(2):
            for c in range(2):
                row = 2 * k + c
                at = c * D + half * BANK
                rows = slice(row * P, (row + 1) * P)
                last = three(pe, m.tr[1][:, half * BANK:(half + 1) * BANK], m.hidt_hi[:, rows], m.hidt_lo[:, rows],
                             m.w_hi[:, k, at:at + BANK], m.w_lo[:, k, at:at + BANK], row == 0, row == FC - 1)
        last.then_inc(q.used, 1)


def rows_hi(act, m, q, i, a, b):
    slot = b % q.ring
    act.wait_ge(q.xt_tr, i * a + b + 1 + q.ring)
    act.activation(m.xt_hi[:, slot], m.tr[0][:].rearrange("p (c n) -> p c n", c=DC), ACT.Copy).then_inc(q.xt_hi, 1)


def rows_lo(dve, m, q, i, a, b):
    slot = b % q.ring
    dve.wait_ge(q.xt_hi, i * a + b + 1)
    dve.tensor_tensor(m.xt_lo[:, slot], m.tr[0][:].rearrange("p (c n) -> p c n", c=DC),
                      m.xt_hi[:, slot].bitcast(F32), ALU.subtract).then_inc(q.xt_lo, 1)


def block_act(act, m, q, st, i, a, b, landed, next_block):
    n = i * (a * BLOCK) + b * BLOCK

    def hi(k):
        split_hi(act, m, st, b % q.ring * BLOCK + k, landed(k), (q.used, n + k - 1))

    hi(2)
    hi(3)
    act.wait_ge(q.used, n + 2)
    act.activation(m.sil[:], m.pj[0][:], ACT.Silu).then_inc(q.sil, 1)
    hi(4)
    act.wait_ge(q.ht_tr, i * a + b + 1)
    act.activation(m.hidt_hi[:], m.ps[0][:], ACT.Copy).then_inc(q.ht_hi, 1)
    hi(5)
    if next_block:
        rows_hi(act, m, q, i, a, b + 1)
        hi(6)
        hi(7)
    act.wait_ge(q.used, n + BLOCK)
    slot = b % q.ring
    act.wait_ge(q.y_free, i * a + b + 1)
    act.activation(m.y[:, slot, 0:BANK], m.tr[1][:, 0:BANK], ACT.Copy).then_inc(q.y_act, 1)


def block_dve(dve, m, q, st, i, a, b, first_piece, next_block):
    n = i * (a * BLOCK) + b * BLOCK

    def lo(k):
        split_lo(dve, m, st, b % q.ring * BLOCK + k, n + first_piece + k)

    lo(2)
    lo(3)
    lo(4)
    dve.wait_ge(q.sil, i * a + b + 2)
    dve.wait_ge(q.used, n + 4)
    dve.tensor_tensor(m.hid[:], m.sil[:], m.pj[1][:], ALU.mult).then_inc(q.hid, 1)
    dve.wait_ge(q.ht_hi, i * a + b + 1)
    dve.tensor_tensor(m.hidt_lo[:], m.ps[0][:], m.hidt_hi[:].bitcast(F32), ALU.subtract).then_inc(q.ht_lo, 1)
    lo(5)
    if next_block:
        rows_lo(dve, m, q, i, a, b + 1)
        lo(6)
        lo(7)
    dve.wait_ge(q.used, n + BLOCK)
    slot = b % q.ring
    dve.wait_ge(q.y_free, i * a + b + 1)
    dve.tensor_copy(m.y[:, slot, BANK:], m.tr[1][:, BANK:]).then_inc(q.y_dve, 1)


def overflow(engine, m, body):
    blocks = engine.value_load(m.ov_tab[0:1, OV:OV + 1], min_val=0, max_val=OV)
    with engine.If(blocks > 0):
        with engine.Fori(0, blocks) as j:
            body(j)


def experts_pool(pool, m, s, d, layer):
    q, at = s.e, layer * EXPERTS
    last = EXPERTS // 2 - 1
    pool.memset(m.xg[:], 0.0).then_inc(s.cleared, 1)
    pool.wait_ge(s.cleared, layer + 2)
    for b in range(2):
        gather(pool, m, q, d, 0, 2, at + b, b)
    with pool.Fori(0, last) as i:
        for b in range(2):
            gather(pool, m, q, d, i, 2, at + b + 2, i * 2 + b + 2)
            scatter(pool, m, q, d, i, 2, at + b, i * 2 + b)
    for b in range(2):
        scatter(pool, m, q, d, last, 2, at + b, last * 2 + b)
    oq = s.oe[layer]

    def body(j):
        gather(pool, m, oq, d, j, 1, 0, j + EXPERTS)
        scatter(pool, m, oq, d, j, 1, 0, j + EXPERTS)

    overflow(pool, m, body)


def experts_pe(pe, m, s, layer):
    at, piece = layer * EXPERTS, MOE_AT[layer] - layer * EXPERTS * BLOCK
    last = EXPERTS // 2 - 1
    turn_rows(pe, m, s.e, 0, 2, at)
    with pe.Fori(0, last) as i:
        for b in range(2):
            block_pe(pe, m, s.e, s.w, i, 2, at + b, piece, True)
    block_pe(pe, m, s.e, s.w, last, 2, at, piece, True)
    block_pe(pe, m, s.e, s.w, last, 2, at + 1, piece, False)

    def body(j):
        pe.wait_ge(s.e.y_act, (layer + 1) * EXPERTS + 1)
        pe.wait_ge(s.e.y_dve, (layer + 1) * EXPERTS + 1)
        turn_rows(pe, m, s.oe[layer], j, 1, 0)
        block_pe(pe, m, s.oe[layer], s.ov[layer], j, 1, 0, 0, False)

    overflow(pe, m, body)


def experts_act(act, m, s, layer):
    at, piece = layer * EXPERTS, MOE_AT[layer] - layer * EXPERTS * BLOCK
    last = EXPERTS // 2 - 1

    def landed(i, b):
        return lambda k: raw_count(i, 2 * BLOCK, MOE_AT[layer] + b * BLOCK + k)

    rows_hi(act, m, s.e, 0, 2, at)
    with act.Fori(0, last) as i:
        for b in range(2):
            block_act(act, m, s.e, s.w, i, 2, at + b, landed(i, b), True)
    block_act(act, m, s.e, s.w, last, 2, at, landed(last, 0), True)
    block_act(act, m, s.e, s.w, last, 2, at + 1, landed(last, 1), False)

    def body(j):
        act.wait_ge(s.e.used, (layer + 1) * EXPERTS * BLOCK)
        act.wait_ge(s.e.y_free, (layer + 1) * EXPERTS + 2)
        q, st = s.oe[layer], s.ov[layer]
        for k in range(2):
            split_hi(act, m, st, k, ov_count(j, k), (q.y_dve, j + 1))
        rows_hi(act, m, q, j, 1, 0)
        block_act(act, m, q, st, j, 1, 0, lambda k: ov_count(j, k), False)

    overflow(act, m, body)


def experts_dve(dve, m, s, layer):
    at, piece = layer * EXPERTS, MOE_AT[layer] - layer * EXPERTS * BLOCK
    last = EXPERTS // 2 - 1
    rows_lo(dve, m, s.e, 0, 2, at)
    with dve.Fori(0, last) as i:
        for b in range(2):
            block_dve(dve, m, s.e, s.w, i, 2, at + b, piece, True)
    block_dve(dve, m, s.e, s.w, last, 2, at, piece, True)
    block_dve(dve, m, s.e, s.w, last, 2, at + 1, piece, False)

    def body(j):
        dve.wait_ge(s.e.y_free, (layer + 1) * EXPERTS + 2)
        q, st = s.oe[layer], s.ov[layer]
        for k in range(2):
            split_lo(dve, m, st, k, j * BLOCK + k)
        rows_lo(dve, m, q, j, 1, 0)
        block_dve(dve, m, q, st, j, 1, 0, 0, False)

    overflow(dve, m, body)



PAIRS = 4


def sum_pool(pool, m, s, d, layer):
    for t in range(TILES):
        if t >= PAIRS:
            pool.wait_ge(s.sum, (layer * TILES + t - PAIRS + 1) * TOP)
        pool.dma_start(m.pair[:, t % PAIRS, :, :], d.y.rearrange("(k t p) n -> t p k n", k=TOP, p=P)[t]) \
            .then_inc(s.pair_in[t % PAIRS], 16)


def sum_dve(dve, m, s, layer):
    for t in range(TILES):
        dve.wait_ge(s.pair_in[t % PAIRS], 16 * (layer * TILES // PAIRS + t // PAIRS + 1))
        for k in range(TOP):
            dve.scalar_tensor_tensor(m.x[:, t, :], m.pair[:, t % PAIRS, k, :], m.gate[:, k, t:t + 1], m.x[:, t, :],
                                     ALU.mult, ALU.add).then_inc(s.sum, 1)
            dve.wait_ge(s.sum, (layer * TILES + t) * TOP + k + 1)



def pool_program(pool, m, s, d):
    pool.sem_inc(s.h_free, 2)
    pool.sem_inc(s.v_free, 2)
    for q in (s.e, *s.oe):
        pool.sem_inc(q.y_free, q.ring)
    step = Chain(pool, s.const_step)
    for t in (m.ident, m.halves):
        step(pool.memset(t[:], 0.0))
    for t in (m.ones, m.before, m.after, m.one):
        step(pool.memset(t[:], 1.0))
    step(pool.memset(m.eps[:], EPS))
    step(pool.affine_select(out=m.ident[:], in_=m.ident[:], compare_op=ALU.not_equal, fill=1.0, base=0,
                            pattern=[[-1, P]], channel_multiplier=1))
    step(pool.memset(m.halves[0:CHUNK, 0:1], 1.0))
    step(pool.memset(m.halves[CHUNK:P, 1:2], 1.0))
    step(pool.affine_select(out=m.before[:], in_=m.before[:], compare_op=ALU.is_ge, fill=0.0, base=-1,
                            pattern=[[1, P]], channel_multiplier=-1))
    step(pool.affine_select(out=m.after[:], in_=m.after[:], compare_op=ALU.is_ge, fill=0.0, base=-1,
                            pattern=[[-1, P]], channel_multiplier=1))
    step(pool.memset(m.after[CHUNK:P, 0:CHUNK], 0.0))
    step(pool.iota(m.count_i[:], pattern=[[1, P]], base=0, channel_multiplier=0))
    step(pool.iota(m.label_i[:], pattern=[[SEQ, TOP], [P, TILES]], base=1, channel_multiplier=1))
    step(pool.tensor_copy(m.count[:], m.count_i[:]))
    pool.tensor_copy(m.label[:], m.label_i[:]).then_inc(s.const, 1)

    norm_pool(pool, m, s, d, 0, d.gla_norm[0])
    gates_pool(pool, m, s, d)
    meet(s, pool, 0, 1)
    heads_pool(pool, m, s, d)
    meet(s, pool, 0, 2)
    moe_pool(pool, m, s, d, 0, 1, 2)
    norm_pool(pool, m, s, d, 2, d.sgu_norm[0])
    meet(s, pool, 0, 6)
    sgu_pool(pool, m, s, d)
    meet(s, pool, 0, 7)
    moe_pool(pool, m, s, d, 1, 3, 7)
    pool.dma_start(m.gain[:], d.final_norm.partition_broadcast(P)).then_inc(s.gain, 16)
    for t in range(TILES):
        pool.wait_ge(s.fin, t + 1)
        pool.dma_start(d.out[0, t * P:(t + 1) * P, :], m.o_out[:, t % 2, :]).then_inc(s.out[t % 2], 16)
    for k in range(2):
        pool.wait_ge(s.out[k], 16 * TILES // 2)


def moe_pool(pool, m, s, d, layer, n, met):
    route_pool(pool, m, s, d, layer)
    norm_pool(pool, m, s, d, n, d.moe_norm[layer], layer)
    meet(s, pool, 0, met + 1)
    experts_pool(pool, m, s, d, layer)
    meet(s, pool, 0, met + 2)
    sum_pool(pool, m, s, d, layer)
    meet(s, pool, 0, met + 3)


def pe_program(pe, m, s, d):
    pe.sem_inc(s.n_tr, 2)
    pe.sem_inc(s.o_mm, 2)
    pe.sem_inc(s.e.xt_tr, 2)
    for k in range(2):
        pe.sem_inc(s.oe[k].xt_tr, 1)
    pe.wait_ge(s.const, 1)
    norm_pe(pe, m, s, 0)
    gates_pe(pe, m, s)
    meet(s, pe, 3, 1)
    heads_pe(pe, m, s)
    meet(s, pe, 3, 2)
    moe_pe(pe, m, s, 0, 1, 2)
    norm_pe(pe, m, s, 2)
    meet(s, pe, 3, 6)
    sgu_pe(pe, m, s)
    meet(s, pe, 3, 7)
    moe_pe(pe, m, s, 1, 3, 7)


def moe_pe(pe, m, s, layer, n, met):
    norm_pe(pe, m, s, n)
    route_pe(pe, m, s, layer)
    meet(s, pe, 3, met + 1)
    experts_pe(pe, m, s, layer)
    meet(s, pe, 3, met + 2)
    meet(s, pe, 3, met + 3)


def act_program(act, m, s, d):
    act.sem_inc(s.pj_act, G_CREDIT)
    act.sem_inc(s.o_evac, 2)
    act.sem_inc(s.e.sil, 1)
    act.sem_inc(s.e.y_act, 1)
    for k in range(2):
        act.sem_inc(s.oe[k].sil, 1)
        act.sem_inc(s.oe[k].y_act, 1)
    act.wait_ge(s.const, 1)
    norm_act(act, m, s, 0)
    for k in range(2):
        split_hi(act, m, s.w, k, raw_count(0, 4, k))
    gates_act(act, m, s)
    meet(s, act, 1, 1)
    heads_act(act, m, s)
    meet(s, act, 1, 2)
    moe_act(act, m, s, 0, 1, 2)
    norm_act(act, m, s, 2)
    meet(s, act, 1, 6)
    sgu_act(act, m, s)
    meet(s, act, 1, 7)
    moe_act(act, m, s, 1, 3, 7)
    norm_std(act, m, s, 4)


def moe_act(act, m, s, layer, n, met):
    norm_act(act, m, s, n)
    route_act(act, m, s, layer)
    meet(s, act, 1, met + 1)
    experts_act(act, m, s, layer)
    meet(s, act, 1, met + 2)
    meet(s, act, 1, met + 3)


def dve_program(dve, m, s, d):
    step = Chain(dve, s.step)
    dve.sem_inc(s.w.split, RAW)
    dve.sem_inc(s.pj_dve, G_CREDIT)
    for sem in (s.n_lo, s.s_upd, s.og, s.ot_lo, s.mix_used, s.gt_lo):
        dve.sem_inc(sem, 2)
    dve.sem_inc(s.bn, 16)
    for q in (s.e, *s.oe):
        for sem in (q.xt_lo, q.hid, q.ht_lo, q.y_dve):
            dve.sem_inc(sem, 1)
    for k in range(2):
        dve.sem_inc(s.ov[k].split, RAW)
    dve.wait_ge(s.const, 1)
    norm_dve(dve, m, s, 0, step)
    for k in range(2):
        split_lo(dve, m, s.w, k, k)
    gates_dve(dve, m, s, step)
    meet(s, dve, 2, 1)
    heads_dve(dve, m, s)
    meet(s, dve, 2, 2)
    moe_dve(dve, m, s, step, 0, 1, 2)
    norm_dve(dve, m, s, 2, step)
    meet(s, dve, 2, 6)
    sgu_dve(dve, m, s, step)
    meet(s, dve, 2, 7)
    moe_dve(dve, m, s, step, 1, 3, 7)
    dve.wait_ge(s.std, 5)
    dve.wait_ge(s.gain, 16 * 5)
    step(dve.reciprocal(m.rstd[:], m.std[:]))
    for t in range(TILES):
        if t >= 2:
            dve.wait_ge(s.out[t % 2], 16 * (t // 2))
        dve.scalar_tensor_tensor(m.o_out[:, t % 2, :], m.x[:, t, :], m.rstd[:, t:t + 1], m.gain[:],
                                 ALU.mult, ALU.mult).then_inc(s.fin, 1)


def moe_dve(dve, m, s, step, layer, n, met):
    norm_dve(dve, m, s, n, step, layer)
    route_dve(dve, m, s, layer, step)
    meet(s, dve, 2, met + 1)
    experts_dve(dve, m, s, layer)
    meet(s, dve, 2, met + 2)
    sum_dve(dve, m, s, layer)
    meet(s, dve, 2, met + 3)


_INS = ["x", "gla_norm", "gla_w_in", "gla_w_gate_up", "gla_b_gate", "gla_head_g", "gla_w_out", "sgu_norm",
        "sgu_w_in", "sgu_ln_g", "sgu_ln_b", "sgu_w_s", "sgu_b_s", "sgu_w_out", "moe_norm", "moe_w_group",
        "moe_b_group", "moe_w_sub", "moe_b_sub", "moe_w1", "moe_w3", "moe_w2", "final_norm"]


def kernel(**inputs):
    import numpy as np
    import concourse.bacc as bacc
    from concourse.bass_utils import run_bass_kernel_spmd

    nc = bacc.Bacc("TRN2", target_bir_lowering=False, num_devices=1)
    arrays, args = {}, []
    for name in _INS:
        a = np.ascontiguousarray(inputs[name])
        arrays[f"in_{name}_dram"] = a
        args.append(nc.dram_tensor(f"in_{name}_dram", a.shape, mybir.dt.from_np(a.dtype), kind="ExternalInput").ap())
    args.append(nc.dram_tensor("out_dram", (1, SEQ, D), F32, kind="ExternalOutput").ap())
    build(nc, *args)
    r = run_bass_kernel_spmd(nc, [arrays], core_ids=[0])
    return r.results[0]["out_dram"]
```

```python
from contextlib import ExitStack

import concourse.bass as bass
from concourse import mybir

F32 = mybir.dt.float32
F32R = mybir.dt.float32r
I32 = mybir.dt.int32
U32 = mybir.dt.uint32
ALU = mybir.AluOpType
ACT = mybir.ActivationFunctionType
AX_X = mybir.AxisListType.X

P = 128
D = 1024
SEQ = 1024
TILES = SEQ // P
DC = D // P
EPS = 1e-6

HEADS = 4
DK = 128
DV = 256
HK = HEADS * DK
HV = HEADS * DV
RANK = 16
TAU = 16.0
CHUNK = 64
CHUNKS = SEQ // CHUNK

HALF = 2048
SG = 4
SLICE = 256
SLICES = HALF // SLICE

NG = 4
NE = 8
EXPERTS = NG * NE
TOP = 2
FF = 512
FC = FF // P
ROUTES = NG + EXPERTS
ASSIGN = SEQ * TOP
OV = ASSIGN // P - 1
COLS = EXPERTS + OV + 1
NOWHERE = 1 << 20

PIECE = 2048
RAW = 4
SPLIT = 2
MOE_SPLIT = 4
BLOCK = 6
AHEAD = 2
GLA_AT = 0
MOE_AT = [HEADS * 4, HEADS * 4 + EXPERTS * BLOCK + SLICES * 3]
SGU_V_AT = MOE_AT[0] + EXPERTS * BLOCK
SGU_U_AT = SGU_V_AT + SLICES

HALF_BANK = 256
BANK = 512

G_HEAD = ["A"] * 2 + ["D"] * 8 + ["A"] * 16 + ["D"] * 16
G_V = ["A"] * 8
G_U = ["A"] * 4 + ["D"] * 16
G_CREDIT = 3
LANDED = 32


class Names:
    pass


def build(nc, x, gla_norm, gla_w_in, gla_w_gate_up, gla_b_gate, gla_head_g, gla_w_out,
          sgu_norm, sgu_w_in, sgu_ln_g, sgu_ln_b, sgu_w_s, sgu_b_s, sgu_w_out,
          moe_norm, moe_w_group, moe_b_group, moe_w_sub, moe_b_sub, moe_w1, moe_w3, moe_w2,
          final_norm, out):
    with ExitStack() as ctx:
        m = memory(nc, ctx)
        s = semaphores(nc, ctx)
        d = Names()
        d.h = nc.dram_tensor("h_rows", (SEQ, D), F32, kind="Internal").ap()
        d.y = nc.dram_tensor("y_rows", (ASSIGN, D), F32, kind="Internal").ap()
        d.dec = nc.dram_tensor("decay_rows", (SEQ, HK), F32, kind="Internal").ap()
        d.v = nc.dram_tensor("v_rows", (SEQ, HALF), F32, kind="Internal").ap()
        d.x, d.gla_norm, d.gla_w_in, d.gla_w_gate_up, d.gla_b_gate = x, gla_norm, gla_w_in, gla_w_gate_up, gla_b_gate
        d.gla_head_g, d.gla_w_out, d.sgu_norm, d.sgu_w_in = gla_head_g, gla_w_out, sgu_norm, sgu_w_in
        d.sgu_ln_g, d.sgu_ln_b, d.sgu_w_s, d.sgu_b_s, d.sgu_w_out = sgu_ln_g, sgu_ln_b, sgu_w_s, sgu_b_s, sgu_w_out
        d.moe_norm, d.moe_w_group, d.moe_b_group = moe_norm, moe_w_group, moe_b_group
        d.moe_w_sub, d.moe_b_sub, d.moe_w1, d.moe_w3, d.moe_w2 = moe_w_sub, moe_b_sub, moe_w1, moe_w3, moe_w2
        d.final_norm, d.out = final_norm, out
        block = ctx.enter_context(nc.Block())

        @block.sync
        def _(sp):
            sp_program(sp, m, s, d)

        @block.gpsimd
        def _(pool):
            pool_program(pool, m, s, d)

        @block.scalar
        def _(act):
            act_program(act, m, s, d)

        @block.vector
        def _(dve):
            dve_program(dve, m, s, d)

        @block.tensor
        def _(pe):
            pe_program(pe, m, s, d)



def memory(nc, ctx):
    base = (nc.sbuf_base + 63) // 64 * 64
    top = nc.sbuf_usable_end // 32 * 32
    ctx.enter_context(nc.sbuf_tensor("slab", [P, (top - nc.sbuf_base) // 4 - 8], F32))
    at = [base]

    def put(name, shape, dt=F32):
        size = 4
        for n in shape[1:]:
            size *= n
        t = nc.alloc_sbuf_tensor_at(name, list(shape), dt, offset=at[0])
        at[0] += (size + 31) // 32 * 32
        assert at[0] <= top, (name, at[0] - top)
        return t

    m = Names()
    m.x = put("x_sb", [P, TILES, D])
    m.raw = put("raw", [P, RAW, PIECE])
    m.w_hi = [put(f"w_hi{k}", [P, PIECE], F32R) for k in range(SPLIT)]
    m.w_lo = [put(f"w_lo{k}", [P, PIECE], F32R) for k in range(SPLIT)]
    m.ident = put("ident", [P, P])
    m.ones = put("ones", [P, P])
    m.before = put("before", [P, P])
    m.after = put("after", [P, P])
    m.halves = put("halves", [P, 2])
    m.count_i = put("count_i", [P, P], I32)
    m.count = put("count", [P, P])
    m.label_i = put("label_i", [P, TOP * TILES], I32)
    m.label = put("label", [P, TOP * TILES])
    m.eps = put("eps", [P, 1])
    m.one = put("one", [P, 1])
    m.ss = put("ss", [P, TILES])
    m.std = put("std", [P, TILES])
    m.rstd = put("rstd", [P, TILES])
    region = at[0]

    m.ht_hi = put("ht_hi", [P, DC, SEQ], F32R)
    m.ht_lo = put("ht_lo", [P, DC, SEQ], F32R)
    after_ht = at[0]
    m.h = put("h", [P, 2, D])
    m.gain = put("gain", [P, D])
    after_norm = at[0]

    at[0] = after_ht
    m.gate_up = put("gate_up", [P, TILES, HK])
    m.glr_raw = put("glr_raw", [P, DC * RANK])
    m.glr_hi = put("glr_hi", [P, DC * RANK], F32R)
    m.glr_lo = put("glr_lo", [P, DC * RANK], F32R)
    m.glr = put("glr", [P, TILES * RANK])
    m.glr_t = put("glr_t", [P, P])
    m.bgate = put("bgate", [P, HK])
    m.z = put("z", [P, 2, HK])
    m.zexp = put("zexp", [P, 2, HK])
    m.logsig = put("logsig", [P, 2, HK])
    at[0] = after_ht
    m.dec = put("dec", [P, TILES, DK])
    m.q_t = put("q_t", [P, SEQ])
    m.kd = put("kd", [P, TILES, DK])
    m.v = put("v", [P, TILES, DV])
    m.o = put("o", [P, TILES, DV])
    m.rg = put("rg", [P, 2, DV])
    m.state = put("state", [P, 2, DV])
    m.head_g = put("head_g", [P, DV])
    m.e_now = put("e_now", [P, CHUNKS])
    m.junk = put("junk", [P, DV])
    m.oss = put("oss", [P, TILES])
    m.ostd = put("ostd", [P, TILES])
    m.orstd = put("orstd", [P, TILES])
    at_o = at[0]
    at[0] = after_ht + 4 * 1024
    m.ot_hi = put("ot_hi", [P, TILES, DV], F32R)
    m.ot_lo = put("ot_lo", [P, TILES, DV], F32R)
    at[0] = top - 256 - 32
    m.e_end = put("e_end", [P, HEADS * CHUNKS])
    assert at_o <= top - 256 - 32

    at[0] = after_ht
    m.v_out = put("v_out", [P, 2, TILES, SLICE])
    at[0] = after_ht
    m.gt_hi = put("gt_hi", [P, 2, SEQ], F32R)
    m.gt_lo = put("gt_lo", [P, 2, SEQ], F32R)
    m.v_s = put("v_s", [P, TILES, SLICE])
    m.ut = put("ut", [P, 2, BANK])
    m.mix = put("mix", [P, BANK])
    m.ln_g = put("ln_g", [P, SLICE])
    m.ln_b = put("ln_b", [P, SLICE])
    m.ws_t = put("ws_t", [P, SG * P])
    m.bs = put("bs", [P, SG * P])
    m.stats = put("stats", [P, TILES, SLICES * 6])
    m.mv = put("mv", [P, TILES, 2])
    m.lstd = put("lstd", [P, TILES])
    m.lrstd = put("lrstd", [P, TILES])
    m.lshift = put("lshift", [P, TILES])
    at[0] = after_norm
    m.ws = put("ws", [P, SG, P])

    at[0] = after_norm
    m.r_raw = put("r_raw", [P, DC, ROUTES])
    m.r_hi = put("r_hi", [P, DC, ROUTES], F32R)
    m.r_lo = put("r_lo", [P, DC, ROUTES], F32R)
    m.r_bias = put("r_bias", [P, ROUTES])
    m.logit = put("logit", [P, TILES, ROUTES])
    m.glog = put("glog", [P, TILES, 8])
    m.gmax = put("gmax", [P, TILES, 8])
    m.gidx = put("gidx", [P, TILES, 8], U32)
    m.gsel = put("gsel", [P, TILES])
    m.gexp = put("gexp", [P, TILES, NG])
    m.gw = put("gw", [P, TILES])
    m.goh = put("goh", [P, TILES, NG])
    m.sel = put("sel", [P, TILES, NG, NE])
    m.chosen = put("chosen", [P, TILES, NE])
    m.cmax = put("cmax", [P, TILES, 8])
    m.cidx = put("cidx", [P, TILES, 8], U32)
    m.csel = put("csel", [P, TILES, TOP])
    m.e2 = put("e2", [P, TILES])
    m.gate = put("gate", [P, TOP, TILES])
    m.eid = put("eid", [P, TOP, TILES])
    m.eoh = put("eoh", [P, TOP * TILES, EXPERTS])
    m.emask = put("emask", [P, TILES, EXPERTS])
    m.pre = put("pre", [P, TILES + 1, EXPERTS])
    m.rank = put("rank", [P, TILES, EXPERTS])
    m.pick = put("pick", [P, TOP * TILES, EXPERTS])
    m.rk = put("rk", [P, TOP * TILES])
    m.nov = put("nov", [P, EXPERTS])
    m.inc = put("inc", [P, 2, EXPERTS])
    m.ovb = put("ovb", [P, EXPERTS])
    m.q = put("q", [P, TOP * TILES])
    m.ovk = put("ovk", [P, TOP * TILES])
    m.t1 = put("t1", [P, TOP * TILES])
    m.tab = put("tab", [P, 3, COLS])
    m.tok_idx = put("tok_idx", [P, COLS], U32)
    m.dst_idx = put("dst_idx", [P, COLS], U32)
    m.ovx = put("ovx", [P, OV, EXPERTS])
    m.ovf = put("ovf", [P, OV + 1])
    m.ov_tab = put("ov_tab", [P, OV + 1], I32)
    at[0] = after_ht
    m.rowoh = put("rowoh", [P, TOP * TILES, P])
    m.coloh = put("coloh", [P, TOP * TILES, COLS])
    at[0] = region
    m.xg = put("xg", [P, 2, D])
    m.xt_hi = put("xt_hi", [P, 2, DC, P], F32R)
    m.xt_lo = put("xt_lo", [P, 2, DC, P], F32R)
    m.sil = put("sil", [P, FF])
    m.hid = put("hid", [P, FF])
    m.hidt_hi = put("hidt_hi", [P, FF], F32R)
    m.hidt_lo = put("hidt_lo", [P, FF], F32R)
    m.y = put("y", [P, 2, D])
    m.tok_col = put("tok_col", [P, 2, 8], U32)
    m.dst_col = put("dst_col", [P, 2, 8], U32)
    m.w_hi += [put(f"w_hi{k}", [P, PIECE], F32R) for k in range(SPLIT, MOE_SPLIT)]
    m.w_lo += [put(f"w_lo{k}", [P, PIECE], F32R) for k in range(SPLIT, MOE_SPLIT)]
    assert at[0] <= after_norm
    at[0] = region
    m.pair = put("pair", [P, 4, TOP, D])
    m.o_out = put("o_out", [P, 2, D])

    m.tr = [ctx.enter_context(nc.psum_tensor(f"ps_tr{k}", [P, 2 * BANK], F32)) for k in range(2)]
    m.pj = [ctx.enter_context(nc.psum_tensor(f"ps_pj{k}", [P, BANK], F32)) for k in range(2)]
    m.ps = [ctx.enter_context(nc.psum_tensor(f"ps_aux{k}", [P, BANK], F32)) for k in range(2)]
    return m


def semaphores(nc, ctx):
    def sem(name):
        return ctx.enter_context(nc.semaphore(name))

    def stream(tag):
        q = Names()
        q.full = [sem(f"{tag}_raw_full{k}") for k in range(RAW)]
        q.hi, q.split = sem(f"{tag}_hi_done"), sem(f"{tag}_split_done")
        return q

    def experts(tag, ring):
        names = ("used", "tok_col", "dst_col", "xt_tr", "xt_hi", "xt_lo", "sil", "hid", "ht_tr", "ht_hi",
                 "ht_lo", "y_act")
        q = Names()
        q.ring = ring
        q.xg_full = [sem(f"{tag}_xg_full{k}") for k in range(ring)]
        q.y_out, q.y_free, q.go = sem(f"{tag}_y_out"), sem(f"{tag}_y_free"), sem(f"{tag}_dma_go")
        (q.used, q.tok_col, q.dst_col, q.xt_tr, q.xt_hi, q.xt_lo, q.sil, q.hid, q.ht_tr, q.ht_hi, q.ht_lo,
         q.y_act) = [sem(f"{tag}_{n}") for n in names]
        return q

    s = Names()
    s.w = stream("w")
    s.ov = [stream(f"ov{k}") for k in range(2)]
    s.e = experts("e", 2)
    s.oe = [experts(f"oe{k}", 1) for k in range(2)]
    s.meet = [sem(f"met_{n}") for n in ("pool", "act", "dve", "pe")]
    s.const = sem("const_ready")
    s.const_step = sem("const_step")
    s.x_in = [sem(f"x_in{k}") for k in range(2)]
    s.gain = sem("gain_in")
    s.sq, s.std, s.h, s.n_tr, s.n_hi, s.n_lo = [sem(n) for n in (
        "norm_squares", "norm_std", "norm_h", "norm_turned", "norm_hi", "norm_lo")]
    s.h_free = sem("h_slot_free")
    s.h_out = [sem(f"h_out{k}") for k in range(2)]
    s.step = sem("dve_step")
    s.given_back = sem("raw_given_back")
    s.routed = sem("routed")
    s.pj_full, s.pj_act, s.pj_dve = sem("group_full"), sem("group_by_act"), sem("group_by_dve")
    s.gin, s.gup = sem("gate_in"), sem("gate_up_in")
    s.z_mm, s.z_dve, s.z_act, s.z_g, s.dec_mm, s.dec_act = [sem(n) for n in (
        "z_made", "z_biased", "z_logged", "log_decay", "decay_summed", "decay_exp")]
    s.dec_out = [sem(f"decay_out{k}") for k in range(2)]
    s.head_in, s.e_now, s.e_std = sem("head_in"), sem("e_now_ready"), sem("o_rstd")
    s.u_full, s.s_upd, s.o_mm, s.o_evac, s.o_std, s.og, s.ot_tr, s.ot_hi, s.ot_lo, s.rgh = [sem(n) for n in (
        "update_made", "state_ready", "o_made", "o_out", "o_std", "o_gated", "o_turned", "o_hi", "o_lo", "r_gained")]
    s.ws_in, s.bn, s.v_in = sem("ws_in"), sem("v_stats"), sem("v_in")
    s.ws_tr, s.ws_masked, s.lvar, s.v_free = sem("ws_turned"), sem("ws_masked"), sem("v_variance"), sem("v_slot_free")
    s.v_st = sem("v_stored")
    s.mix_full, s.mix_used, s.ln_hat, s.vn, s.gt, s.gt_hi, s.gt_lo = [sem(n) for n in (
        "mix_made", "mix_read", "v_normed", "v_ready", "g_ready", "g_hi", "g_lo")]
    s.r_in, s.r_hi, s.r_lo, s.r_mm, s.r_act = [sem(n) for n in (
        "router_in", "router_hi", "router_lo", "route_product", "route_exp")]
    s.masked, s.cleared = sem("route_one_hot"), sem("cleared")
    s.pair_in = [sem(f"pair_in{k}") for k in range(4)]
    s.sum = sem("rows_summed")
    s.fin, s.out = sem("row_final"), [sem(f"out{k}") for k in range(2)]
    return s



class Chain:

    def __init__(self, engine, sem, at=0):
        self.engine, self.sem, self.at = engine, sem, at

    def __call__(self, instruction):
        self.at += 1
        instruction.then_inc(self.sem, 1)
        self.engine.wait_ge(self.sem, self.at)


def meet(s, engine, me, n):
    engine.drain().then_inc(s.meet[me], 1)
    for other in range(4):
        if other != me:
            engine.wait_ge(s.meet[other], n)


def split_hi(act, m, st, b, landed, used=None, ring=SPLIT):
    act.wait_ge(st.full[b % RAW], landed)
    if used is not None:
        act.wait_ge(*used)
    act.activation(m.w_hi[b % ring][:], m.raw[:, b % RAW, :], ACT.Copy).then_inc(st.hi, 1)


def split_lo(dve, m, st, b, n, ring=SPLIT):
    dve.wait_ge(st.hi, n + 1)
    dve.tensor_tensor(m.w_lo[b % ring][:], m.raw[:, b % RAW, :], m.w_hi[b % ring][:].bitcast(F32),
                      ALU.subtract).then_inc(st.split, 1)


def wait_split(pe, st, n):
    pe.wait_ge(st.split, n + 1 + RAW)


def raw_count(i, a, b):
    return i * (a // RAW * LANDED) + (b // RAW + 1) * LANDED


def ov_count(j, b):
    uses = 2 if b % RAW < BLOCK - RAW else 1
    return j * (uses * LANDED) + (b // RAW + 1) * LANDED


def group_wait(pe, s, who, base, i, g):
    n = len(who)
    owner = who[g - 2]
    done = sum(w == owner for w in who[:g - 1]) if g >= 2 else -sum(w == owner for w in who[n - 1 + g:])
    sem = s.pj_act if owner == "A" else s.pj_dve
    pe.wait_ge(sem, i * sum(w == owner for w in who) + base[owner] + done + G_CREDIT)


B_GLA = {"F": 0, "A": 0, "D": 0}
B_V = {"F": HEADS * len(G_HEAD), "A": HEADS * G_HEAD.count("A"), "D": HEADS * G_HEAD.count("D")}
B_U = {"F": B_V["F"] + SLICES * 8, "A": B_V["A"] + SLICES * 8, "D": B_V["D"]}


def three(pe, out, hi_l, lo_l, hi_r, lo_r, first, last):
    pe.matmul(out, hi_l, hi_r, start=first, stop=False)
    pe.matmul(out, hi_l, lo_r, start=False, stop=False)
    return pe.matmul(out, lo_l, hi_r, start=False, stop=last)



def sp_program(sp, m, s, d):
    for k in range(2):
        rows = d.x[0, k * SEQ // 2:(k + 1) * SEQ // 2, :].rearrange("(t p) n -> p t n", p=P)
        sp.dma_start(m.x[:, k * TILES // 2:(k + 1) * TILES // 2, :], rows).then_inc(s.x_in[k], 16)

    def slot_free(n):
        sp.wait_ge(s.w.split, n + 1)

    w_in = d.gla_w_in[0].rearrange("(p c) n -> p c n", c=DC)
    with sp.Fori(0, HEADS) as h:
        qk = m.raw[:, 0, :].rearrange("p (c n) -> p c n", c=DC)
        slot_free(h * 4 + GLA_AT)
        for part in range(2):
            sp.dma_start(qk[:, :, part * DK:(part + 1) * DK],
                         w_in[:, :, bass.ds(h * DK + part * HK, DK)]).then_inc(s.w.full[0], 16)
        for k in range(2):
            slot_free(h * 4 + GLA_AT + k + 1)
            sp.dma_start(m.raw[:, k + 1, :].rearrange("p (c n) -> p c n", c=DC),
                         w_in[:, :, bass.ds(h * DV + 2 * HK + k * HV, DV)]).then_inc(s.w.full[k + 1], LANDED)
        slot_free(h * 4 + GLA_AT + 3)
        rows = d.gla_w_out[0][bass.ds(h * DV, DV), :]
        sp.dma_start(m.raw[:, 3, :], rows.rearrange("(p c) n -> p (c n)", c=2)).then_inc(s.w.full[3], LANDED)

    sp_experts(sp, m, s, d, 0)

    s_in = d.sgu_w_in[0].rearrange("(p c) n -> p c n", c=DC)
    with sp.Fori(0, SLICES // RAW) as i:
        for k in range(RAW):
            slot_free(i * RAW + SGU_V_AT + k)
            sp.dma_start(m.raw[:, k, :].rearrange("p (c n) -> p c n", c=DC),
                         s_in[:, :, bass.ds(i * (RAW * SLICE) + HALF + k * SLICE, SLICE)]).then_inc(s.w.full[k], LANDED)
    with sp.Fori(0, SLICES // 2) as i:
        for k in range(2):
            slot_free(i * RAW + SGU_U_AT + 2 * k)
            sp.dma_start(m.raw[:, 2 * k, :].rearrange("p (c n) -> p c n", c=DC),
                         s_in[:, :, bass.ds(i * (2 * SLICE) + k * SLICE, SLICE)]).then_inc(s.w.full[2 * k], LANDED)
            slot_free(i * RAW + SGU_U_AT + 2 * k + 1)
            rows = d.sgu_w_out[0][bass.ds(i * (2 * SLICE) + k * SLICE, SLICE), :]
            sp.dma_start(m.raw[:, 2 * k + 1, :], rows.rearrange("(p c) n -> p (c n)", c=2)) \
              .then_inc(s.w.full[2 * k + 1], LANDED)

    sp_experts(sp, m, s, d, 1)
    for k in range(2):
        sp.wait_ge(s.out[k], 16 * TILES // 2)


def expert_piece(d, layer, e, b):
    w, c = ((d.moe_w1, DC), (d.moe_w3, DC), (d.moe_w2, FC))[b // 2]
    rows = w[layer][bass.ds(e, 1)].rearrange("o (p c) n -> p (o c n)", c=c)
    return rows[:, (b % 2) * PIECE:(b % 2 + 1) * PIECE]


def sp_experts(sp, m, s, d, layer):
    def load(i, n, e, b):
        sp.wait_ge(s.w.split, i * (2 * BLOCK) + MOE_AT[layer] + n + 1)
        sp.dma_start(m.raw[:, n % RAW, :], expert_piece(d, layer, e, b)).then_inc(s.w.full[n % RAW], LANDED)

    def expert(i, b):
        first = AHEAD + b * BLOCK
        for k in range(2):
            load(i, first + k, i * 2 + b, 2 + k)
        for k in range(2):
            load(i, first + 2 + k, i * 2 + b + 1, k)
        for k in range(2):
            load(i, first + 4 + k, i * 2 + b, 4 + k)

    last = EXPERTS // 2 - 1
    for k in range(AHEAD):
        load(0, k, 0, k)
    with sp.Fori(0, last) as i:
        for b in range(2):
            expert(i, b)
    expert(last, 0)
    for k in range(4):
        load(last, AHEAD + BLOCK + k, EXPERTS - 1, 2 + k)
    ov = s.ov[layer]
    sp.wait_ge(s.routed, layer + 1)
    blocks = sp.value_load(m.ov_tab[0:1, OV:OV + 1], min_val=0, max_val=OV)
    with sp.If(blocks > 0):
        sp.wait_ge(s.w.split, MOE_AT[layer] + EXPERTS * BLOCK + RAW)
        with sp.Fori(0, blocks) as j:
            e = sp.value_load(m.ov_tab[0:1, bass.ds(j, 1)], min_val=0, max_val=EXPERTS - 1)
            for b in range(BLOCK):
                sp.wait_ge(ov.split, j * BLOCK + max(b + 1, RAW))
                sp.dma_start(m.raw[:, b % RAW, :], expert_piece(d, layer, e, b)).then_inc(ov.full[b % RAW], LANDED)
        sp.wait_ge(ov.split, blocks * BLOCK + RAW)
        sp.sem_inc(s.given_back, 1)



def norm_pool(pool, m, s, d, n, gain, stored=None):
    pool.dma_start(m.gain[:], gain.partition_broadcast(P)).then_inc(s.gain, 16)
    if stored is not None:
        for t in range(TILES + 1):
            if t < TILES:
                pool.wait_ge(s.h, n * TILES + t + 1)
                pool.dma_start(d.h[t * P:(t + 1) * P, :], m.h[:, t % 2, :]).then_inc(s.h_out[t % 2], 16)
            if t >= 1:
                pool.wait_ge(s.h_out[(t - 1) % 2], 16 * (stored * TILES // 2 + (t - 1) // 2 + 1))
                pool.sem_inc(s.h_free, 1)


def norm_std(act, m, s, n):
    for t in range(TILES):
        if n == 0 and t % (TILES // 2) == 0:
            act.wait_ge(s.x_in[t // (TILES // 2)], 16)
        if t > 0:
            act.wait_ge(s.sq, n * TILES + t)
        act.activation(m.h[:, 0, :], m.x[:, t, :], ACT.Square, accum_out=m.ss[:, t:t + 1]).then_inc(s.sq, 1)
    act.wait_ge(s.sq, (n + 1) * TILES)
    act.activation(m.std[:], m.ss[:], ACT.Sqrt, scale=1.0 / D, bias=m.eps[:, 0:1]).then_inc(s.std, 1)


def norm_act(act, m, s, n):
    norm_std(act, m, s, n)
    with act.Fori(0, TILES // 2) as i:
        for b in range(2):
            act.wait_ge(s.n_tr, i * 2 + n * TILES + b + 3)
            act.activation(m.ht_hi[:, :, bass.ds(i * (2 * P) + b * P, P)],
                           m.tr[b][:].rearrange("p (c n) -> p c n", c=DC), ACT.Copy).then_inc(s.n_hi, 1)


def norm_dve(dve, m, s, n, step, stored=None):
    dve.wait_ge(s.std, n + 1)
    dve.wait_ge(s.gain, 16 * (n + 1))
    step(dve.reciprocal(m.rstd[:], m.std[:]))
    with dve.Fori(0, TILES // 2) as i:
        for b in range(2):
            t = i * 2 + b
            dve.wait_ge(s.n_tr, i * 2 + n * TILES + b + 1)
            if stored is not None:
                dve.wait_ge(s.h_free, i * 2 + stored * TILES + b + 1)
            dve.scalar_tensor_tensor(m.h[:, b, :], m.x[:, bass.ds(t, 1), :].rearrange("p o n -> p (o n)"),
                                     m.rstd[:, bass.ds(t, 1)], m.gain[:], ALU.mult, ALU.mult).then_inc(s.h, 1)
        for b in range(2):
            dve.wait_ge(s.n_hi, i * 2 + n * TILES + b + 1)
            cols = bass.ds(i * (2 * P) + b * P, P)
            dve.tensor_tensor(m.ht_lo[:, :, cols], m.tr[b][:].rearrange("p (c n) -> p c n", c=DC),
                              m.ht_hi[:, :, cols].bitcast(F32), ALU.subtract).then_inc(s.n_lo, 1)


def norm_pe(pe, m, s, n):
    with pe.Fori(0, TILES // 2) as i:
        for b in range(2):
            pe.wait_ge(s.h, i * 2 + n * TILES + b + 1)
            pe.wait_ge(s.n_lo, i * 2 + n * TILES + b + 1)
            rows = m.h[:, b, :].rearrange("p (n c) -> p c n", c=DC)
            for c in range(DC):
                last = pe.transpose(m.tr[b][:, c * P:(c + 1) * P], rows[:, c, :], m.ident[:])
            last.then_inc(s.n_tr, 1)
    pe.wait_ge(s.n_lo, (n + 1) * TILES + 2)


def project(pe, m, s, i, base, g, who, out, stationary, moving, wait=True):
    group_wait(pe, s, who, base, i, g)
    for c in range(DC):
        last = three(pe, out, stationary(c, 0), stationary(c, 1), moving(c, 0), moving(c, 1), c == 0, c == DC - 1)
    last.then_inc(s.pj_full, 1)



def gates_pool(pool, m, s, d):
    pool.dma_start(m.glr_raw[:].rearrange("p (c r) -> p c r", c=DC),
                   d.gla_w_in[0].rearrange("(p c) n -> p c n", c=DC)[:, :, 2 * HK + 2 * HV:]).then_inc(s.gin, 16)
    pool.dma_start(m.bgate[:], d.gla_b_gate[0].partition_broadcast(P)).then_inc(s.gin, 16)
    pool.wait_ge(s.n_tr, TILES + 2)
    pool.memset(m.gate_up[:], 0.0).then_inc(s.cleared, 1)
    pool.wait_ge(s.cleared, 1)
    for t in range(TILES):
        pool.dma_start(m.gate_up[t * RANK:(t + 1) * RANK, t, :], d.gla_w_gate_up[0]).then_inc(s.gup, 16)
    with pool.Fori(0, TILES // 2) as i:
        for b in range(2):
            pool.wait_ge(s.dec_act, i * 2 + b + 1)
            pool.dma_start(d.dec[bass.ds(i * (2 * P) + b * P, P), :], m.z[:, b, :]).then_inc(s.dec_out[b], 16)


def gates_pe(pe, m, s):
    pe.wait_ge(s.z_g, 1)
    for t in range(TILES):
        for c in range(DC):
            r = slice(c * RANK, (c + 1) * RANK)
            last = three(pe, m.ps[0][:, t * RANK:(t + 1) * RANK], m.ht_hi[:, c, t * P:(t + 1) * P],
                         m.ht_lo[:, c, t * P:(t + 1) * P], m.glr_hi[:, r], m.glr_lo[:, r], c == 0, c == DC - 1)
    last.then_inc(s.z_mm, 1)
    pe.wait_ge(s.z_act, 1)
    pe.transpose(m.ps[1][:, 0:P], m.glr[:], m.ident[:]).then_inc(s.z_mm, 1)
    pe.wait_ge(s.z_act, 2)
    pe.wait_ge(s.gup, 16 * TILES)
    for t in range(TILES + 1):
        if t < TILES:
            if t >= 2:
                pe.wait_ge(s.z_dve, 2 * t - 3)
            pe.matmul(m.pj[t % 2][:], m.glr_t[:], m.gate_up[:, t, :], start=True, stop=True).then_inc(s.z_mm, 1)
        if t >= 1:
            u = t - 1
            pe.wait_ge(s.z_g, u + 2)
            if u >= 2:
                pe.wait_ge(s.dec_act, u - 1)
            pe.matmul(m.ps[u % 2][:], m.after[:], m.logsig[:, u % 2, :], start=True, stop=True)
            for h in range(HEADS):
                last = pe.matmul(m.tr[0][:, h * CHUNKS + 2 * u:h * CHUNKS + 2 * u + 2],
                                 m.logsig[:, u % 2, h * DK:(h + 1) * DK], m.halves[:], start=True, stop=True)
            last.then_inc(s.dec_mm, 1)


def gates_act(act, m, s):
    act.wait_ge(s.z_mm, 1)
    act.activation(m.glr[:], m.ps[0][:, 0:P], ACT.Copy).then_inc(s.z_act, 1)
    act.wait_ge(s.z_mm, 2)
    act.activation(m.glr_t[:], m.ps[1][:, 0:P], ACT.Copy).then_inc(s.z_act, 1)
    for t in range(TILES):
        act.wait_ge(s.z_dve, 2 * t + 2)
        act.activation(m.zexp[:, t % 2, :], m.zexp[:, t % 2, :], ACT.Exp).then_inc(s.z_act, 1)
        act.wait_ge(s.z_act, 2 * t + 3)
        act.activation(m.zexp[:, t % 2, :], m.zexp[:, t % 2, :], ACT.Ln, bias=m.one[:, 0:1]).then_inc(s.z_act, 1)
        if t >= 1:
            decay_exp(act, m, s, t - 1)
    decay_exp(act, m, s, TILES - 1)
    act.activation(m.e_end[:], m.tr[0][:, 0:HEADS * CHUNKS], ACT.Exp, scale=1.0 / TAU)


def decay_exp(act, m, s, t):
    act.wait_ge(s.dec_mm, t + 1)
    act.activation(m.z[:, t % 2, :], m.ps[t % 2][:], ACT.Exp, scale=1.0 / TAU).then_inc(s.dec_act, 1)


def gates_dve(dve, m, s, step):
    dve.wait_ge(s.gin, 32)
    step(dve.tensor_copy(m.glr_hi[:], m.glr_raw[:]))
    dve.tensor_tensor(m.glr_lo[:], m.glr_raw[:], m.glr_hi[:].bitcast(F32), ALU.subtract).then_inc(s.z_g, 1)
    for t in range(TILES):
        z, e = m.z[:, t % 2, :], m.zexp[:, t % 2, :]
        dve.wait_ge(s.z_mm, t + 3)
        if t >= 2:
            dve.wait_ge(s.dec_out[t % 2], 16 * (t // 2))
        dve.tensor_tensor(z, m.pj[t % 2][:], m.bgate[:], ALU.add).then_inc(s.z_dve, 1)
        dve.wait_ge(s.z_dve, 2 * t + 1)
        dve.scalar_tensor_tensor(e, z, -1.0, z, ALU.mult, ALU.min).then_inc(s.z_dve, 1)
        dve.wait_ge(s.z_act, 2 * t + 4)
        if t >= 2:
            dve.wait_ge(s.dec_mm, t - 1)
        dve.scalar_tensor_tensor(m.logsig[:, t % 2, :], z, 0.0, e, ALU.min, ALU.subtract).then_inc(s.z_g, 1)



def heads_pool(pool, m, s, d):
    def load(h):
        pool.dma_start(m.head_g[:], d.gla_head_g[0][bass.ds(h, 1), :].partition_broadcast(P)
                       .rearrange("q o n -> q (o n)")).then_inc(s.head_in, 16)
        pool.dma_start(m.dec[:], d.dec[:, bass.ds(h * DK, DK)].rearrange("(t p) k -> p t k", p=P)).then_inc(s.head_in, 16)

    for b in range(2):
        pool.wait_ge(s.dec_out[b], 16 * TILES // 2)
    load(0)
    with pool.Fori(1, HEADS) as h:
        pool.wait_ge(s.og, h * TILES + 2)
        load(h)


def heads_pe(pe, m, s):
    with pe.Fori(0, HEADS) as h:
        w = [m.w_hi, m.w_lo]
        ht = [m.ht_hi, m.ht_lo]
        wait_split(pe, s.w, h * 4 + GLA_AT)
        for g in range(2):
            project(pe, m, s, h, B_GLA, g, G_HEAD, m.pj[g % 2][:],
                    lambda c, part: w[part][0][:, c * SLICE:c * SLICE + DK],
                    lambda c, part: ht[part][:, c, g * BANK:(g + 1) * BANK])
        for t in range(TILES):
            project(pe, m, s, h, B_GLA, 2 + t, G_HEAD, m.pj[t % 2][:, 0:DK],
                    lambda c, part: ht[part][:, c, t * P:(t + 1) * P],
                    lambda c, part: w[part][0][:, c * SLICE + DK:(c + 1) * SLICE])
        wait_split(pe, s.w, h * 4 + GLA_AT + 1)
        for t in range(TILES):
            project(pe, m, s, h, B_GLA, 10 + t, G_HEAD, m.pj[t % 2][:, 0:DV],
                    lambda c, part: ht[part][:, c, t * P:(t + 1) * P],
                    lambda c, part: w[part][1][:, c * SLICE:(c + 1) * SLICE])
        pe.wait_ge(s.pj_dve, h * G_HEAD.count("D") + TILES + G_CREDIT)
        pe.wait_ge(s.pj_act, h * G_HEAD.count("A") + 2 + TILES + G_CREDIT)
        for c in range(CHUNKS + 1):
            if c < CHUNKS:
                rows = slice(c % 2 * CHUNK, (c % 2 + 1) * CHUNK)
                pe.wait_ge(s.s_upd, h * CHUNKS + c + 1)
                pe.matmul(m.ps[c % 2][:, 0:DV], m.kd[rows, c // 2, :], m.v[rows, c // 2, :],
                          start=True, stop=True).then_inc(s.u_full, 1)
            if c >= 1:
                u = c - 1
                pe.wait_ge(s.s_upd, h * CHUNKS + u + 3)
                if u % 2 == 0:
                    pe.wait_ge(s.o_evac, h * TILES + u // 2 + 1)
                pe.matmul(m.tr[u // 2 % 2][u % 2 * CHUNK:(u % 2 + 1) * CHUNK, 0:DV],
                          m.q_t[:, u * CHUNK:(u + 1) * CHUNK], m.state[:, u % 2, :],
                          start=True, stop=True).then_inc(s.o_mm, 1)
        wait_split(pe, s.w, h * 4 + GLA_AT + 2)

        def turn(t):
            pe.wait_ge(s.og, h * TILES + t + 3)
            pe.wait_ge(s.ot_lo, h * TILES + t + 1)
            rows = m.o[:, t, :].rearrange("p (n c) -> p c n", c=2)
            for c in range(2):
                last = pe.transpose(m.tr[t % 2][:, c * P:(c + 1) * P], rows[:, c, :], m.ident[:])
            last.then_inc(s.ot_tr, 1)

        for t in range(TILES):
            project(pe, m, s, h, B_GLA, 18 + t, G_HEAD, m.pj[t % 2][:, 0:DV],
                    lambda c, part: ht[part][:, c, t * P:(t + 1) * P],
                    lambda c, part: w[part][0][:, c * SLICE:(c + 1) * SLICE])
            if t >= 1:
                turn(t - 1)
        turn(TILES - 1)
        wait_split(pe, s.w, h * 4 + GLA_AT + 3)
        ot = [m.ot_hi, m.ot_lo]
        for t in range(TILES):
            pe.wait_ge(s.ot_lo, h * TILES + t + 3)
            for half in range(2):
                out_group(pe, m, s, h, B_GLA, 26 + 2 * t + half, G_HEAD, half,
                          lambda c, part: ot[part][:, t, c * P:(c + 1) * P])


def out_group(pe, m, s, i, base, g, who, half, stationary):
    group_wait(pe, s, who, base, i, g)
    for c in range(2):
        at = c * D + half * BANK
        last = three(pe, m.pj[g % 2][:], stationary(c, 0), stationary(c, 1), m.w_hi[1][:, at:at + BANK],
                     m.w_lo[1][:, at:at + BANK], c == 0, c == 1)
    last.then_inc(s.pj_full, 1)


def heads_act(act, m, s):
    with act.Fori(0, HEADS) as h:
        def full(g):
            act.wait_ge(s.pj_full, h * len(G_HEAD) + g + 1)

        def after(g):
            return s.pj_full, h * len(G_HEAD) + g + 1

        for g in range(2):
            full(g)
            act.activation(m.q_t[:, g * BANK:(g + 1) * BANK], m.pj[g][:], ACT.Copy, scale=DK ** -0.5).then_inc(s.pj_act, 1)
        split_hi(act, m, s.w, 2, raw_count(h, 4, 2), after(9))
        for t in range(TILES):
            full(10 + t)
            act.activation(m.v[:, t, :], m.pj[t % 2][:, 0:DV], ACT.Copy).then_inc(s.pj_act, 1)
        split_hi(act, m, s.w, 3, raw_count(h, 4, 3), after(17))
        for t in range(TILES):
            act.wait_ge(s.o_mm, h * CHUNKS + 2 * t + 4)
            act.activation(m.o[:, t, :], m.tr[t % 2][:, 0:DV], ACT.Copy)
            act.wait_ge(s.o_evac, h * TILES + t + 2)
            act.activation(m.junk[:], m.tr[t % 2][:, 0:DV], ACT.Square, accum_out=m.oss[:, t:t + 1]).then_inc(s.o_evac, 1)
        act.wait_ge(s.o_evac, h * TILES + TILES + 2)
        act.activation(m.ostd[:], m.oss[:], ACT.Sqrt, scale=1.0 / DV, bias=m.eps[:, 0:1]).then_inc(s.o_std, 1)
        for t in range(TILES + 1):
            if t < TILES:
                full(18 + t)
                act.wait_ge(s.og, h * TILES + t + 1)
                act.activation(m.rg[:, t % 2, :], m.pj[t % 2][:, 0:DV], ACT.Silu).then_inc(s.pj_act, 1)
            if t >= 1:
                act.wait_ge(s.ot_tr, h * TILES + t)
                act.activation(m.ot_hi[:, t - 1, :], m.tr[(t - 1) % 2][:, 0:DV], ACT.Copy).then_inc(s.ot_hi, 1)
        split_hi(act, m, s.w, 4, raw_count(h, 4, 4), after(25))
        split_hi(act, m, s.w, 5, raw_count(h, 4, 5), after(41))


def heads_dve(dve, m, s):
    with dve.Fori(0, HEADS) as h:
        dve.wait_ge(s.head_in, h * 32 + 32)
        dve.tensor_copy(m.e_now[:], m.e_end[:, bass.ds(h * CHUNKS, CHUNKS)]).then_inc(s.e_now, 1)
        for t in range(TILES):
            dve.wait_ge(s.pj_full, h * len(G_HEAD) + t + 3)
            dve.tensor_tensor(m.kd[:, t, :], m.pj[t % 2][:, 0:DK], m.dec[:, t, :], ALU.mult).then_inc(s.pj_dve, 1)
        split_lo(dve, m, s.w, 2, h * 4 + GLA_AT + 2)
        dve.wait_ge(s.e_now, h + 1)
        for c in range(CHUNKS):
            dve.wait_ge(s.u_full, h * CHUNKS + c + 1)
            dve.wait_ge(s.o_mm, h * CHUNKS + c + 1)
            if c == 0:
                dve.tensor_copy(m.state[:, 0, :], m.ps[0][:, 0:DV]).then_inc(s.s_upd, 1)
            else:
                dve.wait_ge(s.s_upd, h * CHUNKS + c + 2)
                dve.scalar_tensor_tensor(m.state[:, c % 2, :], m.state[:, (c - 1) % 2, :], m.e_now[:, c:c + 1],
                                         m.ps[c % 2][:, 0:DV], ALU.mult, ALU.add).then_inc(s.s_upd, 1)
        split_lo(dve, m, s.w, 3, h * 4 + GLA_AT + 3)
        dve.wait_ge(s.o_std, h + 1)
        dve.reciprocal(m.orstd[:], m.ostd[:]).then_inc(s.e_std, 1)
        dve.wait_ge(s.e_std, h + 1)
        for t in range(TILES + 1):
            if t < TILES:
                dve.wait_ge(s.pj_act, h * G_HEAD.count("A") + 11 + t + G_CREDIT)
                dve.tensor_tensor(m.rg[:, t % 2, :], m.rg[:, t % 2, :], m.head_g[:], ALU.mult).then_inc(s.rgh, 1)
                dve.wait_ge(s.rgh, h * TILES + t + 1)
                dve.scalar_tensor_tensor(m.o[:, t, :], m.o[:, t, :], m.orstd[:, t:t + 1], m.rg[:, t % 2, :],
                                         ALU.mult, ALU.mult).then_inc(s.og, 1)
            if t >= 1:
                dve.wait_ge(s.ot_hi, h * TILES + t)
                dve.tensor_tensor(m.ot_lo[:, t - 1, :], m.tr[(t - 1) % 2][:, 0:DV],
                                  m.ot_hi[:, t - 1, :].bitcast(F32), ALU.subtract).then_inc(s.ot_lo, 1)
        split_lo(dve, m, s.w, 4, h * 4 + GLA_AT + 4)
        for g in range(2 * TILES):
            dve.wait_ge(s.pj_full, h * len(G_HEAD) + 27 + g)
            add_rows(dve, m, s, g, g % 2)
        split_lo(dve, m, s.w, 5, h * 4 + GLA_AT + 5)


def add_rows(dve, m, s, g, bank):
    part = m.x[:, g // 2, g % 2 * BANK:(g % 2 + 1) * BANK]
    dve.tensor_tensor(part, part, m.pj[bank][:], ALU.add).then_inc(s.pj_dve, 1)



def sgu_pool(pool, m, s, d):
    pool.dma_start(m.ws[:], d.sgu_w_s[0].rearrange("g t q -> t g q")).then_inc(s.ws_in, 16)
    with pool.Fori(0, SLICES // RAW) as i:
        for b in range(RAW):
            pool.wait_ge(s.pj_act, i * (RAW * 8) + B_V["A"] + 8 * (b + 1) + G_CREDIT)
            pool.dma_start(d.v[:, bass.ds(i * (RAW * SLICE) + b * SLICE, SLICE)].rearrange("(t p) c -> p t c", p=P),
                           m.v_out[:, b % 2, :, :]).then_inc(s.v_st, 16)
            pool.wait_ge(s.v_st, i * (16 * RAW) + 16 * (b + 1))
            pool.sem_inc(s.v_free, 1)
    pool.dma_start(m.bs[:], d.sgu_b_s[0].rearrange("g t -> (g t)").partition_broadcast(P)).then_inc(s.ws_in, 16)

    def load(j):
        cols = bass.ds(j * SLICE, SLICE)
        pool.dma_start(m.v_s[:], d.v[:, cols].rearrange("(t p) c -> p t c", p=P)).then_inc(s.v_in, 16)
        pool.dma_start(m.ln_g[:], d.sgu_ln_g[0][cols].partition_broadcast(P)).then_inc(s.v_in, 16)
        pool.dma_start(m.ln_b[:], d.sgu_ln_b[0][cols].partition_broadcast(P)).then_inc(s.v_in, 16)

    def scale(j):
        pool.wait_ge(s.ln_hat, j + 2)
        gain = m.ln_g[:].unsqueeze(1).to_broadcast([P, TILES, SLICE])
        shift = m.ln_b[:].unsqueeze(1).to_broadcast([P, TILES, SLICE])
        pool.tensor_tensor(m.v_s[:], m.v_s[:], gain, ALU.mult).then_inc(s.vn, 1)
        pool.wait_ge(s.vn, j * 2 + 1)
        pool.tensor_tensor(m.v_s[:], m.v_s[:], shift, ALU.add).then_inc(s.vn, 1)

    load(0)
    scale(0)
    with pool.Fori(1, SLICES) as j:
        pool.wait_ge(s.mix_full, j * 4)
        load(j)
        scale(j)


def sgu_pe(pe, m, s):
    ht = [m.ht_hi, m.ht_lo]
    w = [m.w_hi, m.w_lo]
    pe.wait_ge(s.ws_masked, 1)
    for g in range(SG):
        last = pe.transpose(m.ps[0][:, g * P:(g + 1) * P], m.ws[:, g, :], m.ident[:])
    last.then_inc(s.ws_tr, 1)
    with pe.Fori(0, SLICES // RAW) as i:
        for b in range(RAW):
            wait_split(pe, s.w, i * RAW + SGU_V_AT + b)
            for t in range(TILES):
                pe.wait_ge(s.pj_act, i * (RAW * 8) + B_V["A"] + b * 8 + t - 1 + G_CREDIT)
                for c in range(DC):
                    cols = slice(c * SLICE, (c + 1) * SLICE)
                    rows = slice(t * P, (t + 1) * P)
                    last = three(pe, m.pj[t % 2][:, 0:SLICE], ht[0][:, c, rows], ht[1][:, c, rows],
                                 w[0][b % 2][:, cols], w[1][b % 2][:, cols], c == 0, c == DC - 1)
                last.then_inc(s.pj_full, 1)
    gt = [m.gt_hi, m.gt_lo]
    with pe.Fori(0, SLICES // 2) as i:
        for b in range(2):
            pe.wait_ge(s.vn, i * 4 + 2 * b + 2)
            wait_split(pe, s.w, i * RAW + SGU_U_AT + 2 * b)
            vt = m.v_s[:].rearrange("p t (n c) -> p t c n", c=2)
            for q in range(4):
                half, c = q // 2, q % 2
                pe.wait_ge(s.mix_used, i * 8 + 4 * b + q + 1)
                for k in range(4):
                    last = pe.matmul(m.ps[q % 2][:, k * P:(k + 1) * P], vt[:, half * 4 + k, c, :],
                                     m.ws_t[:, bass.ds(i * P, P)], start=True, stop=True)
                last.then_inc(s.mix_full, 1)
                sgu_group_wait(pe, s, i, b, q)
                for k in range(DC):
                    cols = [w[part][0][:, k * SLICE:(k + 1) * SLICE].rearrange("p (n c) -> p c n", c=2)[:, c, :]
                            for part in range(2)]
                    last = three(pe, m.pj[q % 2][:], cols[0], cols[1], ht[0][:, k, half * BANK:(half + 1) * BANK],
                                 ht[1][:, k, half * BANK:(half + 1) * BANK], k == 0, k == DC - 1)
                last.then_inc(s.pj_full, 1)
            wait_split(pe, s.w, i * RAW + SGU_U_AT + 2 * b + 1)
            for t in range(TILES):
                if t % 4 == 0:
                    pe.wait_ge(s.gt_lo, i * 8 + 4 * b + t // 4 * 2 + 4)
                for half in range(2):
                    g = 4 + 2 * t + half
                    sgu_group_wait(pe, s, i, b, g)
                    for c in range(2):
                        at = c * D + half * BANK
                        last = three(pe, m.pj[g % 2][:], gt[0][:, c, t * P:(t + 1) * P], gt[1][:, c, t * P:(t + 1) * P],
                                     w[0][1][:, at:at + BANK], w[1][1][:, at:at + BANK], c == 0, c == 1)
                    last.then_inc(s.pj_full, 1)


def sgu_group_wait(pe, s, i, b, g):
    owner = G_U[g - 2]
    done = G_U[:g - 1].count(owner) if g >= 2 else g - 1
    per = G_U.count(owner)
    sem = s.pj_act if owner == "A" else s.pj_dve
    pe.wait_ge(sem, i * (2 * per) + b * per + B_U[owner] + done + G_CREDIT)


def sgu_act(act, m, s):
    split_hi(act, m, s.w, SGU_V_AT, raw_count(0, 4, SGU_V_AT))
    split_hi(act, m, s.w, SGU_V_AT + 1, raw_count(0, 4, SGU_V_AT + 1))
    act.wait_ge(s.ws_tr, 1)
    act.activation(m.ws_t[:], m.ps[0][:], ACT.Copy)
    with act.Fori(0, SLICES // RAW) as i:
        for b in range(RAW):
            act.wait_ge(s.v_free, i * RAW + b + 1)
            for t in range(TILES):
                act.wait_ge(s.pj_full, i * (RAW * 8) + B_V["F"] + 8 * b + t + 1)
                act.wait_ge(s.bn, i * (RAW * 8) + 8 * b + t + 1)
                act.activation(m.v_out[:, b % 2, t, :], m.pj[t % 2][:, 0:SLICE], ACT.Gelu).then_inc(s.pj_act, 1)
            split_hi(act, m, s.w, SGU_V_AT + b + 2, raw_count(i, 4, SGU_V_AT + b + 2))
    act.wait_ge(s.lvar, 1)
    act.activation(m.lstd[:], m.mv[:, :, 1], ACT.Sqrt, bias=m.eps[:, 0:1]).then_inc(s.lvar, 1)
    with act.Fori(0, SLICES // 2) as i:
        for b in range(2):
            for q in range(4):
                half, c = q // 2, q % 2
                act.wait_ge(s.pj_full, i * 40 + B_U["F"] + 20 * b + q + 1)
                act.wait_ge(s.gt_lo, i * 8 + 4 * b + q + 1)
                act.activation(m.ut[:, q % 2, :], m.pj[q % 2][:], ACT.Gelu).then_inc(s.pj_act, 1)
                act.wait_ge(s.gt, i * 8 + 4 * b + q + 1)
                act.activation(m.gt_hi[:, c, half * BANK:(half + 1) * BANK], m.ut[:, q % 2, :], ACT.Copy).then_inc(s.gt_hi, 1)
            split_hi(act, m, s.w, SGU_U_AT + 2 * b + 2, raw_count(i, 4, SGU_U_AT + 2 * b + 2))
            split_hi(act, m, s.w, SGU_U_AT + 2 * b + 3, raw_count(i, 4, SGU_U_AT + 2 * b + 3),
                     (s.pj_full, i * 40 + B_U["F"] + 20 * (b + 1)))


def sgu_dve(dve, m, s, step):
    split_lo(dve, m, s.w, SGU_V_AT, SGU_V_AT)
    split_lo(dve, m, s.w, SGU_V_AT + 1, SGU_V_AT + 1)
    dve.wait_ge(s.ws_in, 16)
    dve.memset(m.ws[0:CHUNK, :, CHUNK:P], 0.0).then_inc(s.ws_masked, 1)
    with dve.Fori(0, SLICES // RAW) as i:
        for b in range(RAW):
            for t in range(TILES):
                dve.wait_ge(s.pj_act, i * (RAW * 8) + B_V["A"] + 8 * b + t + 1 + G_CREDIT)
                dve.bn_stats(m.stats[:, t, bass.ds(i * (RAW * 6) + b * 6, 6)], m.v_out[:, b % 2, t, :]).then_inc(s.bn, 1)
            split_lo(dve, m, s.w, SGU_V_AT + b + 2, i * RAW + SGU_V_AT + b + 2)
    dve.wait_ge(s.bn, SLICES * TILES + 16)
    for t in range(TILES):
        last = dve.bn_aggr(m.mv[:, t, :], m.stats[:, t, :])
    last.then_inc(s.lvar, 1)
    dve.wait_ge(s.ws_in, 32)
    dve.wait_ge(s.lvar, 2)
    step(dve.reciprocal(m.lrstd[:], m.lstd[:]))
    step(dve.scalar_tensor_tensor(m.lshift[:], m.mv[:, :, 0], -1.0, m.lrstd[:], ALU.mult, ALU.mult))
    dve.drain().then_inc(s.ln_hat, 1)

    def normalise(j):
        dve.wait_ge(s.v_in, j * 48 + 48)
        for t in range(TILES):
            last = dve.tensor_scalar(m.v_s[:, t, :], m.v_s[:, t, :], m.lrstd[:, t:t + 1], m.lshift[:, t:t + 1],
                                     ALU.mult, ALU.add)
        last.then_inc(s.ln_hat, 1)

    def slice_(i, b, last):
        for q in range(4):
            half, c = q // 2, q % 2
            dve.wait_ge(s.mix_full, i * 8 + 4 * b + q + 1)
            bias = m.bs[:, bass.ds(i * P, P)].unsqueeze(1).to_broadcast([P, 4, P])
            dve.tensor_tensor(m.mix[:].rearrange("p (k t) -> p k t", k=4),
                              m.ps[q % 2][:].rearrange("p (k t) -> p k t", k=4), bias, ALU.add).then_inc(s.mix_used, 1)
            dve.wait_ge(s.mix_used, i * 8 + 4 * b + q + 3)
            dve.wait_ge(s.pj_act, i * 8 + B_U["A"] + 4 * b + q + 1 + G_CREDIT)
            dve.tensor_tensor(m.ut[:, q % 2, :], m.ut[:, q % 2, :], m.mix[:], ALU.mult).then_inc(s.gt, 1)
            dve.wait_ge(s.gt_hi, i * 8 + 4 * b + q + 1)
            cols = slice(half * BANK, (half + 1) * BANK)
            dve.tensor_tensor(m.gt_lo[:, c, cols], m.ut[:, q % 2, :], m.gt_hi[:, c, cols].bitcast(F32),
                              ALU.subtract).then_inc(s.gt_lo, 1)
        split_lo(dve, m, s.w, SGU_U_AT + 2 * b + 2, i * RAW + SGU_U_AT + 2 * b + 2)
        for g in range(2 * TILES):
            dve.wait_ge(s.pj_full, i * 40 + B_U["F"] + 20 * b + 5 + g)
            add_rows(dve, m, s, g, g % 2)
            if g == 3 and not last:
                normalise(i * 2 + b + 1)
        split_lo(dve, m, s.w, SGU_U_AT + 2 * b + 3, i * RAW + SGU_U_AT + 2 * b + 3)

    normalise(0)
    with dve.Fori(0, SLICES // 2 - 1) as i:
        slice_(i, 0, False)
        slice_(i, 1, False)
    slice_(SLICES // 2 - 1, 0, False)
    slice_(SLICES // 2 - 1, 1, True)



def route_pool(pool, m, s, d, layer):
    pool.dma_start(m.r_raw[:, :, 0:NG], d.moe_w_group[layer].rearrange("(p c) g -> p c g", c=DC)).then_inc(s.r_in, 16)
    for g in range(NG):
        at = NG + g * NE
        pool.dma_start(m.r_raw[:, :, at:at + NE], d.moe_w_sub[layer][g].rearrange("(p c) e -> p c e", c=DC)).then_inc(s.r_in, 16)
    pool.dma_start(m.r_bias[:, 0:NG], d.moe_b_group[layer].partition_broadcast(P)).then_inc(s.r_in, 16)
    pool.dma_start(m.r_bias[:, NG:ROUTES], d.moe_b_sub[layer].rearrange("g e -> (g e)").partition_broadcast(P)).then_inc(s.r_in, 16)


ROUTER_LOADS = 16 * (NG + 3)


def route_pe(pe, m, s, layer):
    pe.wait_ge(s.r_lo, layer + 1)
    for t in range(TILES):
        rows = slice(t * P, (t + 1) * P)
        for c in range(DC):
            last = three(pe, m.ps[0][:, t * ROUTES:(t + 1) * ROUTES], m.ht_hi[:, c, rows], m.ht_lo[:, c, rows],
                         m.r_hi[:, c, :], m.r_lo[:, c, :], c == 0, c == DC - 1)
    last.then_inc(s.r_mm, 1)
    pe.wait_ge(s.masked, layer * 2 + 1)
    flat = m.emask[:].rearrange("p t e -> p (t e)")
    pe.matmul(m.ps[1][:, 0:TILES * EXPERTS], m.before[:], flat, start=True, stop=True)
    pe.matmul(m.ps[0][:, 0:TILES * EXPERTS], m.ones[:], flat, start=True, stop=True).then_inc(s.r_mm, 1)
    pe.wait_ge(s.masked, layer * 2 + 2)
    for a in range(TOP * TILES):
        last = pe.matmul(m.ps[1][:, 0:COLS], m.rowoh[:, a, :], m.coloh[:, a, :], start=(a == 0), stop=(a == TOP * TILES - 1))
    last.then_inc(s.r_mm, 1)


def route_act(act, m, s, layer):
    act.wait_ge(s.r_act, layer * 4 + 1)
    act.activation(m.gexp[:], m.gexp[:], ACT.Exp).then_inc(s.r_act, 1)
    act.wait_ge(s.r_act, layer * 4 + 3)
    act.activation(m.e2[:], m.e2[:], ACT.Exp).then_inc(s.r_act, 1)


def route_dve(dve, m, s, layer, step):
    def tiles(ap, *shape):
        return ap.to_broadcast([P, *shape])

    dve.wait_ge(s.r_in, (layer + 1) * ROUTER_LOADS)
    step(dve.tensor_copy(m.r_hi[:], m.r_raw[:]))
    dve.tensor_tensor(m.r_lo[:], m.r_raw[:], m.r_hi[:].bitcast(F32), ALU.subtract).then_inc(s.r_lo, 1)
    step(dve.memset(m.glog[:], -3.0e38))
    dve.wait_ge(s.r_mm, layer * 3 + 1)
    step(dve.tensor_tensor(m.logit[:], m.ps[0][:, 0:TILES * ROUTES].rearrange("p (t r) -> p t r", t=TILES),
                           tiles(m.r_bias[:].unsqueeze(1), TILES, ROUTES), ALU.add))
    step(dve.tensor_copy(m.glog[:, :, 0:NG], m.logit[:, :, 0:NG]))
    for t in range(TILES):
        last = dve.max(m.gmax[:, t, :], m.glog[:, t, :])
    step(last)
    for t in range(TILES):
        last = dve.max_index(m.gidx[:, t, :], m.gmax[:, t, :], m.glog[:, t, :])
    step(last)
    dve.tensor_tensor(m.gexp[:], m.glog[:, :, 0:NG], tiles(m.gmax[:, :, 0:1], TILES, NG), ALU.subtract).then_inc(s.r_act, 1)
    step(dve.tensor_copy(m.gsel[:], m.gidx[:, :, 0]))
    step(dve.tensor_tensor(m.goh[:], tiles(m.count[:, 0:NG].unsqueeze(1), TILES, NG),
                           tiles(m.gsel[:].unsqueeze(2), TILES, NG), ALU.is_equal))
    for g in range(NG):
        at = NG + g * NE
        last = dve.tensor_tensor(m.sel[:, :, g, :], m.logit[:, :, at:at + NE],
                                 tiles(m.goh[:, :, g:g + 1], TILES, NE), ALU.mult)
    step(last)
    step(dve.tensor_reduce(m.chosen[:], m.sel[:].rearrange("p t g e -> p t e g"), AX_X, ALU.add))
    for t in range(TILES):
        last = dve.max(m.cmax[:, t, :], m.chosen[:, t, :])
    step(last)
    for t in range(TILES):
        last = dve.max_index(m.cidx[:, t, :], m.cmax[:, t, :], m.chosen[:, t, :])
    step(last)
    dve.wait_ge(s.r_act, layer * 4 + 2)
    dve.tensor_tensor(m.e2[:], m.cmax[:, :, 1], m.cmax[:, :, 0], ALU.subtract).then_inc(s.r_act, 1)
    step(dve.tensor_reduce(m.gw[:], m.gexp[:], AX_X, ALU.add))
    step(dve.reciprocal(m.gw[:], m.gw[:]))
    step(dve.tensor_copy(m.csel[:], m.cidx[:, :, 0:TOP]))
    for k in range(TOP):
        last = dve.scalar_tensor_tensor(m.eid[:, k, :], m.gsel[:], float(NE), m.csel[:, :, k], ALU.mult, ALU.add)
    step(last)
    eid = m.eid[:].rearrange("p k t -> p (k t)")
    n = TOP * TILES
    step(dve.tensor_tensor(m.eoh[:], tiles(m.count[:, 0:EXPERTS].unsqueeze(1), n, EXPERTS),
                           tiles(eid.unsqueeze(2), n, EXPERTS), ALU.is_equal))
    dve.tensor_tensor(m.emask[:], m.eoh[:, 0:TILES, :], m.eoh[:, TILES:, :], ALU.add).then_inc(s.masked, 1)
    dve.wait_ge(s.r_act, layer * 4 + 4)
    step(dve.tensor_scalar(m.gate[:, 0, :], m.e2[:], 1.0, None, ALU.add))
    step(dve.reciprocal(m.gate[:, 0, :], m.gate[:, 0, :]))
    step(dve.tensor_tensor(m.gate[:, 0, :], m.gate[:, 0, :], m.gw[:], ALU.mult))
    step(dve.tensor_tensor(m.gate[:, 1, :], m.gate[:, 0, :], m.e2[:], ALU.mult))
    step(dve.memset(m.pre[:, 0, :], 0.0))
    dve.wait_ge(s.r_mm, layer * 3 + 2)
    for t in range(TILES):
        step(dve.tensor_tensor(m.pre[:, t + 1, :], m.pre[:, t, :], m.ps[0][:, t * EXPERTS:(t + 1) * EXPERTS], ALU.add))
    step(dve.tensor_tensor(m.rank[:], m.ps[1][:, 0:TILES * EXPERTS].rearrange("p (t e) -> p t e", t=TILES),
                           m.pre[:, 0:TILES, :], ALU.add))
    for k in range(TOP):
        last = dve.tensor_tensor(m.pick[:, k * TILES:(k + 1) * TILES, :], m.eoh[:, k * TILES:(k + 1) * TILES, :],
                                 m.rank[:], ALU.mult)
    step(last)
    step(dve.tensor_reduce(m.rk[:], m.pick[:], AX_X, ALU.add))
    count = m.pre[:, TILES, :]
    step(dve.tensor_scalar(m.nov[:], count, float(P), None, ALU.is_gt))
    for k in range(2, SEQ // P):
        step(dve.scalar_tensor_tensor(m.nov[:], count, float(k * P), m.nov[:], ALU.is_gt, ALU.add))
    step(dve.tensor_copy(m.inc[:, 0, :], m.nov[:]))
    k, now = 1, 0
    while k < EXPERTS:
        dve.tensor_copy(m.inc[:, 1 - now, 0:k], m.inc[:, now, 0:k])
        step(dve.tensor_tensor(m.inc[:, 1 - now, k:], m.inc[:, now, k:], m.inc[:, now, 0:EXPERTS - k], ALU.add))
        k, now = 2 * k, 1 - now
    inc = m.inc[:, now, :]
    step(dve.tensor_tensor(m.ovb[:], inc, m.nov[:], ALU.subtract))
    step(dve.tensor_tensor(m.ovx[:], tiles(inc.unsqueeze(1), OV, EXPERTS),
                           tiles(m.count[:, 0:OV].unsqueeze(2), OV, EXPERTS), ALU.is_le))
    dve.tensor_copy(m.ovf[:, OV:OV + 1], inc[:, EXPERTS - 1:EXPERTS])
    step(dve.tensor_reduce(m.ovf[:, 0:OV], m.ovx[:], AX_X, ALU.add))
    step(dve.tensor_scalar(m.ovf[:, 0:OV], m.ovf[:, 0:OV], float(EXPERTS - 1), None, ALU.min))
    step(dve.tensor_copy(m.ov_tab[:], m.ovf[:]))
    step(dve.tensor_scalar(m.q[:], m.rk[:], float(P), None, ALU.is_ge))
    for k in range(2, SEQ // P):
        step(dve.scalar_tensor_tensor(m.q[:], m.rk[:], float(k * P), m.q[:], ALU.is_ge, ALU.add))
    step(dve.scalar_tensor_tensor(m.rk[:], m.q[:], -float(P), m.rk[:], ALU.mult, ALU.add))
    step(dve.tensor_tensor(m.pick[:], m.eoh[:], tiles(m.ovb[:].unsqueeze(1), n, EXPERTS), ALU.mult))
    step(dve.tensor_reduce(m.ovk[:], m.pick[:], AX_X, ALU.add))
    step(dve.scalar_tensor_tensor(m.ovk[:], m.ovk[:], float(EXPERTS - 1), m.q[:], ALU.add, ALU.add))
    step(dve.tensor_tensor(m.ovk[:], m.ovk[:], eid, ALU.subtract))
    step(dve.tensor_scalar(m.t1[:], m.q[:], 0.0, None, ALU.is_gt))
    step(dve.tensor_tensor(m.ovk[:], m.ovk[:], m.t1[:], ALU.mult))
    step(dve.tensor_tensor(m.ovk[:], m.ovk[:], eid, ALU.add))
    dve.wait_ge(s.h_free, (layer + 1) * TILES + 2)
    dve.tensor_tensor(m.rowoh[:], tiles(m.count[:].unsqueeze(1), n, P), tiles(m.rk[:].unsqueeze(2), n, P), ALU.is_equal)
    step(dve.tensor_tensor(m.coloh[:], tiles(m.count[:, 0:COLS].unsqueeze(1), n, COLS),
                           tiles(m.ovk[:].unsqueeze(2), n, COLS), ALU.is_equal))
    dve.tensor_tensor(m.coloh[:], m.coloh[:], tiles(m.label[:].unsqueeze(2), n, COLS), ALU.mult).then_inc(s.masked, 1)
    dve.wait_ge(s.r_mm, layer * 3 + 3)
    empty, dst, tok = m.tab[:, 0, :], m.tab[:, 1, :], m.tab[:, 2, :]
    step(dve.tensor_scalar(empty, m.ps[1][:, 0:COLS], 0.0, float(NOWHERE), ALU.is_equal, ALU.mult))
    step(dve.scalar_tensor_tensor(dst, m.ps[1][:, 0:COLS], -1.0, empty, ALU.add, ALU.add))
    step(dve.tensor_scalar(tok, dst, float(SEQ), -float(SEQ), ALU.is_ge, ALU.mult))
    step(dve.tensor_tensor(tok, tok, dst, ALU.add))
    step(dve.tensor_copy(m.tok_idx[:], tok))
    step(dve.tensor_copy(m.dst_idx[:], dst))
    dve.drain().then_inc(s.routed, 1)



def gather(pool, m, q, d, i, a, b, col):
    slot = b % q.ring
    pool.wait_ge(q.xt_tr, i * a + b + 1)
    pool.tensor_copy(m.tok_col[:, slot, 0:1], m.tok_idx[:, bass.ds(col, 1)]).then_inc(q.tok_col, 1)
    pool.wait_ge(q.tok_col, i * a + b + 1)
    pool.sem_inc(q.go, 1)
    pool.indirect_dma_start(out=m.xg[:, slot, :], out_offset=None, in_=d.h[:, :],
                            in_offset=bass.IndirectOffsetOnAxis(ap=m.tok_col[:, slot, 0:1], axis=0),
                            bounds_check=SEQ - 1, oob_is_err=False).then_inc(q.xg_full[slot], 16)


def uses(i, a, b, ring):
    return i * (a // ring) + (b // ring + 1)


def scatter(pool, m, q, d, i, a, b, col):
    slot = b % q.ring
    pool.tensor_copy(m.dst_col[:, slot, 0:1], m.dst_idx[:, bass.ds(col, 1)]).then_inc(q.dst_col, 1)
    pool.wait_ge(q.dst_col, i * a + b + 1)
    pool.wait_ge(q.y_act, i * a + b + 2)
    pool.sem_inc(q.go, 1)
    pool.indirect_dma_start(out=d.y[:, :], out_offset=bass.IndirectOffsetOnAxis(ap=m.dst_col[:, slot, 0:1], axis=0),
                            in_=m.y[:, slot, :], in_offset=None,
                            bounds_check=ASSIGN - 1, oob_is_err=False).then_inc(q.y_out, 16)
    pool.wait_ge(q.y_out, i * (16 * a) + 16 * (b + 1))
    pool.sem_inc(q.y_free, 1)


def turn_rows(pe, m, q, i, a, b):
    slot = b % q.ring
    pe.wait_ge(q.xg_full[slot], uses(i, a, b, q.ring) * 16)
    pe.wait_ge(q.xt_lo, i * a + b + 1)
    rows = m.xg[:, slot, :].rearrange("p (n c) -> p c n", c=DC)
    for c in range(DC):
        last = pe.transpose(m.tr[0][:, c * P:(c + 1) * P], rows[:, c, :], m.ident[:])
    last.then_inc(q.xt_tr, 1)


def wide(pe, m, q, w_slots, st, n, k, slot, bank, used):
    wait_split(pe, st, n)
    for c in range(4):
        row = k * 4 + c
        cols = slice(c * FF, (c + 1) * FF)
        last = three(pe, m.pj[bank][:], m.xt_hi[:, slot, row, :], m.xt_lo[:, slot, row, :],
                     m.w_hi[w_slots][:, cols], m.w_lo[w_slots][:, cols], row == 0, row == DC - 1)
    last.then_inc(used, 1)


def turn_hid(pe, m, q, i, a, b):
    pe.wait_ge(q.hid, i * a + b + 2)
    pe.wait_ge(q.ht_lo, i * a + b + 1)
    hid = m.hid[:].rearrange("p (n c) -> p c n", c=FC)
    for c in range(FC):
        last = pe.transpose(m.ps[0][:, c * P:(c + 1) * P], hid[:, c, :], m.ident[:])
    last.then_inc(q.ht_tr, 1)


def narrow(pe, m, q, w_slot, st, n, k, used):
    wait_split(pe, st, n)
    for half in range(2):
        for c in range(2):
            row = 2 * k + c
            at = c * D + half * BANK
            rows = slice(row * P, (row + 1) * P)
            last = three(pe, m.tr[1][:, half * BANK:(half + 1) * BANK], m.hidt_hi[:, rows], m.hidt_lo[:, rows],
                         m.w_hi[w_slot][:, at:at + BANK], m.w_lo[w_slot][:, at:at + BANK], row == 0, row == FC - 1)
    last.then_inc(used, 1)


def rows_hi(act, m, q, i, a, b):
    slot = b % q.ring
    act.wait_ge(q.xt_tr, i * a + b + 1 + q.ring)
    act.activation(m.xt_hi[:, slot], m.tr[0][:].rearrange("p (c n) -> p c n", c=DC), ACT.Copy).then_inc(q.xt_hi, 1)


def rows_lo(dve, m, q, i, a, b):
    slot = b % q.ring
    dve.wait_ge(q.xt_hi, i * a + b + 1)
    dve.tensor_tensor(m.xt_lo[:, slot], m.tr[0][:].rearrange("p (c n) -> p c n", c=DC),
                      m.xt_hi[:, slot].bitcast(F32), ALU.subtract).then_inc(q.xt_lo, 1)


def silu(act, m, q, count):
    act.wait_ge(q.used, count)
    act.activation(m.sil[:], m.pj[0][:], ACT.Silu).then_inc(q.sil, 1)


def hid_hi(act, m, q, i, a, b):
    act.wait_ge(q.ht_tr, i * a + b + 1)
    act.activation(m.hidt_hi[:], m.ps[0][:], ACT.Copy).then_inc(q.ht_hi, 1)


def rows_out(act, m, q, i, a, b, count):
    slot = b % q.ring
    act.wait_ge(q.used, count)
    act.wait_ge(q.y_free, i * a + b + 1)
    act.activation(m.y[:, slot, :], m.tr[1][:], ACT.Copy).then_inc(q.y_act, 1)


def gate_hid(dve, m, q, i, a, b, count):
    dve.wait_ge(q.sil, i * a + b + 2)
    dve.wait_ge(q.used, count)
    dve.tensor_tensor(m.hid[:], m.sil[:], m.pj[1][:], ALU.mult).then_inc(q.hid, 1)


def hid_lo(dve, m, q, i, a, b):
    dve.wait_ge(q.ht_hi, i * a + b + 1)
    dve.tensor_tensor(m.hidt_lo[:], m.ps[0][:], m.hidt_hi[:].bitcast(F32), ALU.subtract).then_inc(q.ht_lo, 1)


def overflow(engine, m, body):
    blocks = engine.value_load(m.ov_tab[0:1, OV:OV + 1], min_val=0, max_val=OV)
    with engine.If(blocks > 0):
        with engine.Fori(0, blocks) as j:
            body(j)


def experts_pool(pool, m, s, d, layer):
    q, at = s.e, layer * EXPERTS
    pool.memset(m.xg[:], 0.0).then_inc(s.cleared, 1)
    pool.wait_ge(s.cleared, layer + 2)
    for b in range(3):
        gather(pool, m, q, d, 0, 2, at + b, b)
    loops = (EXPERTS - 3) // 2
    with pool.Fori(0, loops) as i:
        for b in range(2):
            gather(pool, m, q, d, i, 2, at + b + 3, i * 2 + b + 3)
            scatter(pool, m, q, d, i, 2, at + b, i * 2 + b)
    for b in range(EXPERTS - 2 * loops):
        if 2 * loops + b + 3 < EXPERTS:
            gather(pool, m, q, d, loops, 2, at + b + 3, 2 * loops + b + 3)
        scatter(pool, m, q, d, loops, 2, at + b, 2 * loops + b)
    oq = s.oe[layer]

    def body(j):
        gather(pool, m, oq, d, j, 1, 0, j + EXPERTS)
        scatter(pool, m, oq, d, j, 1, 0, j + EXPERTS)

    overflow(pool, m, body)


def experts_pe(pe, m, s, layer):
    q, at = s.e, layer * EXPERTS

    def w_piece(i, n):
        return i * (2 * BLOCK) + MOE_AT[layer] + n, n % MOE_SPLIT

    def x_w1(i, b, k):
        if k == 0:
            pe.wait_ge(q.xt_lo, i * 2 + at + b + 2)
            pe.wait_ge(q.sil, i * 2 + at + b + 1)
        n, slot = w_piece(i, (b - 1) * BLOCK + AHEAD + 2 + k if b > 0 else k)
        wide(pe, m, q, slot, s.w, n, k, b % 2, 0, q.used)

    def expert(i, b, w1=True, turn=True):
        first = AHEAD + b * BLOCK
        pe.wait_ge(q.hid, i * 2 + at + b + 1)
        for k in range(2):
            n, slot = w_piece(i, first + k)
            wide(pe, m, q, slot, s.w, n, k, b % 2, 1, q.used)
        if w1:
            x_w1(i, b + 1, 0)
        turn_hid(pe, m, q, i, 2, at + b)
        if w1:
            x_w1(i, b + 1, 1)
        pe.wait_ge(q.ht_lo, i * 2 + at + b + 2)
        pe.wait_ge(q.y_act, i * 2 + at + b + 1)
        for k in range(2):
            n, slot = w_piece(i, first + (4 if w1 else 2) + k)
            narrow(pe, m, q, slot, s.w, n, k, q.used)
            if turn and k == 0:
                turn_rows(pe, m, q, i, 2, at + b + 2)

    turn_rows(pe, m, q, 0, 2, at)
    x_w1(0, 0, 0)
    x_w1(0, 0, 1)
    turn_rows(pe, m, q, 0, 2, at + 1)
    last = EXPERTS // 2 - 1
    with pe.Fori(0, last) as i:
        for b in range(2):
            expert(i, b)
    expert(last, 0, turn=False)
    expert(last, 1, w1=False, turn=False)

    def body(j):
        oq, st = s.oe[layer], s.ov[layer]
        pe.wait_ge(q.y_act, (layer + 1) * EXPERTS + 1)
        pe.wait_ge(oq.y_act, j + 1)
        turn_rows(pe, m, oq, j, 1, 0)
        pe.wait_ge(oq.xt_lo, j + 2)
        for k in range(4):
            wide(pe, m, oq, k % MOE_SPLIT, st, j * BLOCK + k, k % 2, 0, k // 2, oq.used)
        turn_hid(pe, m, oq, j, 1, 0)
        pe.wait_ge(oq.ht_lo, j + 2)
        for k in range(2):
            narrow(pe, m, oq, k % MOE_SPLIT, st, j * BLOCK + 4 + k, k, oq.used)

    overflow(pe, m, body)


def experts_act(act, m, s, layer):
    q, at = s.e, layer * EXPERTS
    base = layer * EXPERTS * BLOCK

    def used(i, n):
        return i * (2 * BLOCK) + base + n + 1

    def hi(i, n):
        last_use = (q.used, used(i, n - MOE_SPLIT)) if n >= MOE_SPLIT else None
        split_hi(act, m, s.w, n, raw_count(i, 2 * BLOCK, MOE_AT[layer] + n), last_use, MOE_SPLIT)

    def expert(i, b, w1=True, turn=True):
        first = AHEAD + b * BLOCK
        if w1:
            hi(i, first + 4)
            hi(i, first + 5)
        hid_hi(act, m, q, i, 2, at + b)
        if w1:
            hi(i, first + 6)
            hi(i, first + 7)
            silu(act, m, q, used(i, first + 3))
            hi(i, first + 8)
        if turn:
            rows_hi(act, m, q, i, 2, at + b + 2)
        if w1:
            hi(i, first + 9)
        rows_out(act, m, q, i, 2, at + b, used(i, first + (5 if w1 else 3)))

    hi(0, 2)
    rows_hi(act, m, q, 0, 2, at)
    hi(0, 3)
    hi(0, 4)
    silu(act, m, q, used(0, 1))
    hi(0, 5)
    rows_hi(act, m, q, 0, 2, at + 1)
    last = EXPERTS // 2 - 1
    with act.Fori(0, last) as i:
        for b in range(2):
            expert(i, b)
    expert(last, 0, turn=False)
    expert(last, 1, w1=False, turn=False)

    def body(j):
        act.wait_ge(q.used, (layer + 1) * EXPERTS * BLOCK)
        act.wait_ge(q.y_free, (layer + 1) * EXPERTS + 2)
        oq, st = s.oe[layer], s.ov[layer]
        for k in range(MOE_SPLIT):
            split_hi(act, m, st, k, ov_count(j, k), (oq.y_act, j + 1), MOE_SPLIT)
        rows_hi(act, m, oq, j, 1, 0)
        for k in range(MOE_SPLIT, BLOCK):
            split_hi(act, m, st, k, ov_count(j, k), (oq.used, j * BLOCK + k - MOE_SPLIT + 1), MOE_SPLIT)
        silu(act, m, oq, j * BLOCK + 2)
        hid_hi(act, m, oq, j, 1, 0)
        rows_out(act, m, oq, j, 1, 0, (j + 1) * BLOCK)

    overflow(act, m, body)


def experts_dve(dve, m, s, layer):
    q, at = s.e, layer * EXPERTS
    base = layer * EXPERTS * BLOCK

    def lo(i, n):
        split_lo(dve, m, s.w, n, i * (2 * BLOCK) + MOE_AT[layer] + n, MOE_SPLIT)

    def expert(i, b, w1=True, turn=True):
        first = AHEAD + b * BLOCK
        if w1:
            lo(i, first + 4)
        gate_hid(dve, m, q, i, 2, at + b, i * (2 * BLOCK) + base + first + 2)
        if w1:
            lo(i, first + 5)
        hid_lo(dve, m, q, i, 2, at + b)
        if w1:
            lo(i, first + 6)
            lo(i, first + 7)
            lo(i, first + 8)
        if turn:
            rows_lo(dve, m, q, i, 2, at + b + 2)
        if w1:
            lo(i, first + 9)

    lo(0, 2)
    rows_lo(dve, m, q, 0, 2, at)
    lo(0, 3)
    lo(0, 4)
    lo(0, 5)
    rows_lo(dve, m, q, 0, 2, at + 1)
    last = EXPERTS // 2 - 1
    with dve.Fori(0, last) as i:
        for b in range(2):
            expert(i, b)
    expert(last, 0, turn=False)
    expert(last, 1, w1=False, turn=False)

    def body(j):
        oq, st = s.oe[layer], s.ov[layer]
        for k in range(MOE_SPLIT):
            split_lo(dve, m, st, k, j * BLOCK + k, MOE_SPLIT)
        rows_lo(dve, m, oq, j, 1, 0)
        for k in range(MOE_SPLIT, BLOCK):
            split_lo(dve, m, st, k, j * BLOCK + k, MOE_SPLIT)
        gate_hid(dve, m, oq, j, 1, 0, j * BLOCK + 4)
        hid_lo(dve, m, oq, j, 1, 0)

    overflow(dve, m, body)



PAIRS = 4


def sum_pool(pool, m, s, d, layer):
    for t in range(TILES):
        if t >= PAIRS:
            pool.wait_ge(s.sum, (layer * TILES + t - PAIRS + 1) * TOP)
        pool.dma_start(m.pair[:, t % PAIRS, :, :], d.y.rearrange("(k t p) n -> t p k n", k=TOP, p=P)[t]) \
            .then_inc(s.pair_in[t % PAIRS], 16)


def sum_dve(dve, m, s, layer):
    for t in range(TILES):
        dve.wait_ge(s.pair_in[t % PAIRS], 16 * (layer * TILES // PAIRS + t // PAIRS + 1))
        for k in range(TOP):
            dve.scalar_tensor_tensor(m.x[:, t, :], m.pair[:, t % PAIRS, k, :], m.gate[:, k, t:t + 1], m.x[:, t, :],
                                     ALU.mult, ALU.add).then_inc(s.sum, 1)
            dve.wait_ge(s.sum, (layer * TILES + t) * TOP + k + 1)



def pool_program(pool, m, s, d):
    pool.sem_inc(s.h_free, 2)
    pool.sem_inc(s.v_free, 2)
    for q in (s.e, *s.oe):
        pool.sem_inc(q.y_free, q.ring)
    step = Chain(pool, s.const_step)
    for t in (m.ident, m.halves):
        step(pool.memset(t[:], 0.0))
    for t in (m.ones, m.before, m.after, m.one):
        step(pool.memset(t[:], 1.0))
    step(pool.memset(m.eps[:], EPS))
    step(pool.affine_select(out=m.ident[:], in_=m.ident[:], compare_op=ALU.not_equal, fill=1.0, base=0,
                            pattern=[[-1, P]], channel_multiplier=1))
    step(pool.memset(m.halves[0:CHUNK, 0:1], 1.0))
    step(pool.memset(m.halves[CHUNK:P, 1:2], 1.0))
    step(pool.affine_select(out=m.before[:], in_=m.before[:], compare_op=ALU.is_ge, fill=0.0, base=-1,
                            pattern=[[1, P]], channel_multiplier=-1))
    step(pool.affine_select(out=m.after[:], in_=m.after[:], compare_op=ALU.is_ge, fill=0.0, base=-1,
                            pattern=[[-1, P]], channel_multiplier=1))
    step(pool.memset(m.after[CHUNK:P, 0:CHUNK], 0.0))
    step(pool.iota(m.count_i[:], pattern=[[1, P]], base=0, channel_multiplier=0))
    step(pool.iota(m.label_i[:], pattern=[[SEQ, TOP], [P, TILES]], base=1, channel_multiplier=1))
    step(pool.tensor_copy(m.count[:], m.count_i[:]))
    pool.tensor_copy(m.label[:], m.label_i[:]).then_inc(s.const, 1)

    norm_pool(pool, m, s, d, 0, d.gla_norm[0])
    gates_pool(pool, m, s, d)
    meet(s, pool, 0, 1)
    heads_pool(pool, m, s, d)
    meet(s, pool, 0, 2)
    moe_pool(pool, m, s, d, 0, 1, 2)
    norm_pool(pool, m, s, d, 2, d.sgu_norm[0])
    meet(s, pool, 0, 6)
    sgu_pool(pool, m, s, d)
    meet(s, pool, 0, 7)
    moe_pool(pool, m, s, d, 1, 3, 7)
    pool.dma_start(m.gain[:], d.final_norm.partition_broadcast(P)).then_inc(s.gain, 16)
    for t in range(TILES):
        pool.wait_ge(s.fin, t + 1)
        pool.dma_start(d.out[0, t * P:(t + 1) * P, :], m.o_out[:, t % 2, :]).then_inc(s.out[t % 2], 16)
    for k in range(2):
        pool.wait_ge(s.out[k], 16 * TILES // 2)


def moe_pool(pool, m, s, d, layer, n, met):
    route_pool(pool, m, s, d, layer)
    norm_pool(pool, m, s, d, n, d.moe_norm[layer], layer)
    meet(s, pool, 0, met + 1)
    experts_pool(pool, m, s, d, layer)
    meet(s, pool, 0, met + 2)
    sum_pool(pool, m, s, d, layer)
    meet(s, pool, 0, met + 3)


def pe_program(pe, m, s, d):
    pe.sem_inc(s.n_tr, 2)
    pe.sem_inc(s.o_mm, 2)
    pe.sem_inc(s.e.xt_tr, 2)
    for k in range(2):
        pe.sem_inc(s.oe[k].xt_tr, 1)
    pe.wait_ge(s.const, 1)
    norm_pe(pe, m, s, 0)
    gates_pe(pe, m, s)
    meet(s, pe, 3, 1)
    heads_pe(pe, m, s)
    meet(s, pe, 3, 2)
    moe_pe(pe, m, s, 0, 1, 2)
    norm_pe(pe, m, s, 2)
    meet(s, pe, 3, 6)
    sgu_pe(pe, m, s)
    meet(s, pe, 3, 7)
    moe_pe(pe, m, s, 1, 3, 7)


def moe_pe(pe, m, s, layer, n, met):
    norm_pe(pe, m, s, n)
    route_pe(pe, m, s, layer)
    meet(s, pe, 3, met + 1)
    experts_pe(pe, m, s, layer)
    meet(s, pe, 3, met + 2)
    meet(s, pe, 3, met + 3)


def act_program(act, m, s, d):
    act.sem_inc(s.pj_act, G_CREDIT)
    act.sem_inc(s.o_evac, 2)
    act.sem_inc(s.e.sil, 1)
    act.sem_inc(s.e.y_act, 1)
    for k in range(2):
        act.sem_inc(s.oe[k].sil, 1)
        act.sem_inc(s.oe[k].y_act, 1)
    act.wait_ge(s.const, 1)
    norm_act(act, m, s, 0)
    for k in range(2):
        split_hi(act, m, s.w, k, raw_count(0, 4, k))
    gates_act(act, m, s)
    meet(s, act, 1, 1)
    heads_act(act, m, s)
    meet(s, act, 1, 2)
    moe_act(act, m, s, 0, 1, 2)
    norm_act(act, m, s, 2)
    meet(s, act, 1, 6)
    sgu_act(act, m, s)
    meet(s, act, 1, 7)
    moe_act(act, m, s, 1, 3, 7)
    norm_std(act, m, s, 4)


def moe_act(act, m, s, layer, n, met):
    norm_act(act, m, s, n)
    route_act(act, m, s, layer)
    meet(s, act, 1, met + 1)
    experts_act(act, m, s, layer)
    meet(s, act, 1, met + 2)
    meet(s, act, 1, met + 3)


def dve_program(dve, m, s, d):
    step = Chain(dve, s.step)
    dve.sem_inc(s.w.split, RAW)
    dve.sem_inc(s.pj_dve, G_CREDIT)
    for sem in (s.n_lo, s.s_upd, s.og, s.ot_lo, s.mix_used, s.gt_lo):
        dve.sem_inc(sem, 2)
    dve.sem_inc(s.bn, 16)
    for q in (s.e, *s.oe):
        for sem in (q.xt_lo, q.hid, q.ht_lo):
            dve.sem_inc(sem, 1)
    for k in range(2):
        dve.sem_inc(s.ov[k].split, RAW)
    dve.wait_ge(s.const, 1)
    norm_dve(dve, m, s, 0, step)
    for k in range(2):
        split_lo(dve, m, s.w, k, k)
    gates_dve(dve, m, s, step)
    meet(s, dve, 2, 1)
    heads_dve(dve, m, s)
    meet(s, dve, 2, 2)
    moe_dve(dve, m, s, step, 0, 1, 2)
    norm_dve(dve, m, s, 2, step)
    meet(s, dve, 2, 6)
    sgu_dve(dve, m, s, step)
    meet(s, dve, 2, 7)
    moe_dve(dve, m, s, step, 1, 3, 7)
    dve.wait_ge(s.std, 5)
    dve.wait_ge(s.gain, 16 * 5)
    step(dve.reciprocal(m.rstd[:], m.std[:]))
    for t in range(TILES):
        if t >= 2:
            dve.wait_ge(s.out[t % 2], 16 * (t // 2))
        dve.scalar_tensor_tensor(m.o_out[:, t % 2, :], m.x[:, t, :], m.rstd[:, t:t + 1], m.gain[:],
                                 ALU.mult, ALU.mult).then_inc(s.fin, 1)


def moe_dve(dve, m, s, step, layer, n, met):
    norm_dve(dve, m, s, n, step, layer)
    route_dve(dve, m, s, layer, step)
    meet(s, dve, 2, met + 1)
    experts_dve(dve, m, s, layer)
    meet(s, dve, 2, met + 2)
    sum_dve(dve, m, s, layer)
    meet(s, dve, 2, met + 3)


_INS = ["x", "gla_norm", "gla_w_in", "gla_w_gate_up", "gla_b_gate", "gla_head_g", "gla_w_out", "sgu_norm",
        "sgu_w_in", "sgu_ln_g", "sgu_ln_b", "sgu_w_s", "sgu_b_s", "sgu_w_out", "moe_norm", "moe_w_group",
        "moe_b_group", "moe_w_sub", "moe_b_sub", "moe_w1", "moe_w3", "moe_w2", "final_norm"]


def kernel(**inputs):
    import numpy as np
    import concourse.bacc as bacc
    from concourse.bass_utils import run_bass_kernel_spmd

    nc = bacc.Bacc("TRN2", target_bir_lowering=False, num_devices=1)
    arrays, args = {}, []
    for name in _INS:
        a = np.ascontiguousarray(inputs[name])
        arrays[f"in_{name}_dram"] = a
        args.append(nc.dram_tensor(f"in_{name}_dram", a.shape, mybir.dt.from_np(a.dtype), kind="ExternalInput").ap())
    args.append(nc.dram_tensor("out_dram", (1, SEQ, D), F32, kind="ExternalOutput").ap())
    build(nc, *args)
    r = run_bass_kernel_spmd(nc, [arrays], core_ids=[0])
    return r.results[0]["out_dram"]
```

```python
from contextlib import ExitStack

import concourse.bass as bass
from concourse import mybir

F32 = mybir.dt.float32
F32R = mybir.dt.float32r
BF16 = mybir.dt.bfloat16
I32 = mybir.dt.int32
U32 = mybir.dt.uint32
ALU = mybir.AluOpType
ACT = mybir.ActivationFunctionType
AX_X = mybir.AxisListType.X

P = 128
D = 1024
SEQ = 1024
TILES = SEQ // P
DC = D // P
EPS = 1e-6
H_RING = 4
X_LOADS = 4
PAIRS = [2, 6]

HEADS = 4
DK = 128
DV = 256
HK = HEADS * DK
HV = HEADS * DV
RANK = 16
TAU = 16.0
CHUNK = 64
CHUNKS = SEQ // CHUNK
HALVES = 2 * CHUNKS - 2

HALF = 2048
SG = 4
SLICE = 256
SLICES = HALF // SLICE

NG = 4
NE = 8
EXPERTS = NG * NE
TOP = 2
FF = 512
FC = FF // P
ROUTES = NG + EXPERTS
ASSIGN = SEQ * TOP
OV = ASSIGN // P - 1
COLS = EXPERTS + OV + 1
NOWHERE = 1 << 20

PIECE = 2048
RAW = 4
SPLIT = 2
MOE_SPLIT = 4
BLOCK = 6
AHEAD = 2
GLA_AT = 0
MOE_AT = [HEADS * 4, HEADS * 4 + EXPERTS * BLOCK + SLICES * 3]
SGU_V_AT = MOE_AT[0] + EXPERTS * BLOCK
SGU_U_AT = SGU_V_AT + SLICES

BANK = 512
HEAD_GROUPS = 20
GROUPS_AT_V = HEADS * HEAD_GROUPS
GROUPS_AT_U = GROUPS_AT_V + SLICES * TILES
LANDED = 32


class Names:
    pass


def build(nc, x, gla_norm, gla_w_in, gla_w_gate_up, gla_b_gate, gla_head_g, gla_w_out,
          sgu_norm, sgu_w_in, sgu_ln_g, sgu_ln_b, sgu_w_s, sgu_b_s, sgu_w_out,
          moe_norm, moe_w_group, moe_b_group, moe_w_sub, moe_b_sub, moe_w1, moe_w3, moe_w2,
          final_norm, out):
    with ExitStack() as ctx:
        m = memory(nc, ctx)
        s = semaphores(nc, ctx)
        d = Names()
        d.h = nc.dram_tensor("h_rows", (SEQ, D), F32, kind="Internal").ap()
        d.y = nc.dram_tensor("y_rows", (ASSIGN, D), F32, kind="Internal").ap()
        d.dec = nc.dram_tensor("decay_rows", (SEQ, HK), F32, kind="Internal").ap()
        d.v = nc.dram_tensor("v_rows", (SEQ, HALF), F32, kind="Internal").ap()
        d.x, d.gla_norm, d.gla_w_in, d.gla_w_gate_up, d.gla_b_gate = x, gla_norm, gla_w_in, gla_w_gate_up, gla_b_gate
        d.gla_head_g, d.gla_w_out, d.sgu_norm, d.sgu_w_in = gla_head_g, gla_w_out, sgu_norm, sgu_w_in
        d.sgu_ln_g, d.sgu_ln_b, d.sgu_w_s, d.sgu_b_s, d.sgu_w_out = sgu_ln_g, sgu_ln_b, sgu_w_s, sgu_b_s, sgu_w_out
        d.moe_norm, d.moe_w_group, d.moe_b_group = moe_norm, moe_w_group, moe_b_group
        d.moe_w_sub, d.moe_b_sub, d.moe_w1, d.moe_w3, d.moe_w2 = moe_w_sub, moe_b_sub, moe_w1, moe_w3, moe_w2
        d.final_norm, d.out = final_norm, out
        block = ctx.enter_context(nc.Block())

        @block.sync
        def _(sp):
            sp_program(sp, m, s, d)

        @block.gpsimd
        def _(pool):
            pool_program(pool, m, s, d)

        @block.scalar
        def _(act):
            act_program(act, m, s, d)

        @block.vector
        def _(dve):
            dve_program(dve, m, s, d)

        @block.tensor
        def _(pe):
            pe_program(pe, m, s, d)



def memory(nc, ctx):
    base = (nc.sbuf_base + 63) // 64 * 64
    top = nc.sbuf_usable_end // 32 * 32
    ctx.enter_context(nc.sbuf_tensor("slab", [P, (top - nc.sbuf_base) // 4 - 8], F32))
    at = [base]

    def put(name, shape, dt=F32):
        size = 4
        for n in shape[1:]:
            size *= n
        t = nc.alloc_sbuf_tensor_at(name, list(shape), dt, offset=at[0])
        at[0] += (size + 31) // 32 * 32
        assert at[0] <= top, (name, at[0] - top)
        return t

    m = Names()
    m.x = put("x_sb", [P, TILES, D])
    m.raw = put("raw", [P, RAW, PIECE])
    m.w_hi = [put(f"w_hi{k}", [P, PIECE], F32R) for k in range(SPLIT)]
    m.w_lo = [put(f"w_lo{k}", [P, PIECE], F32R) for k in range(SPLIT)]
    m.ident = put("ident", [P, P])
    m.ones = put("ones", [P, P], BF16)
    m.before = put("before", [P, P], BF16)
    m.after_f = put("after_f", [P, P])
    m.halves_f = put("halves_f", [P, HALVES])
    m.after = put("after", [P, P], F32R)
    m.halves = put("halves", [P, HALVES], F32R)
    m.count_i = put("count_i", [P, P], I32)
    m.count = put("count", [P, P])
    m.block_i = put("block_i", [P, TOP * TILES], I32)
    m.block = put("block", [P, TOP * TILES], BF16)
    m.row_i = put("row_i", [P, 1], I32)
    m.row = put("row", [P, 1])
    m.eps = put("eps", [P, 1])
    m.one = put("one", [P, 1])
    m.ss = put("ss", [P, TILES])
    m.std = put("std", [P, TILES])
    m.rstd = put("rstd", [P, TILES])
    m.gain = put("gain", [P, D])
    at[0] -= 4 * D
    m.glr_t = put("glr_t", [P, SEQ])[0:RANK, :]
    m.gate = put("gate", [P, TOP, TILES])
    region = at[0]

    m.ht_hi = put("ht_hi", [P, DC, SEQ], F32R)
    m.ht_lo = put("ht_lo", [P, DC, SEQ], F32R)
    after_ht = at[0]
    m.h = put("h", [P, H_RING, D])
    after_norm = at[0]

    at[0] = after_ht
    m.z = put("z", [P, TILES, HK])
    m.logsig = put("logsig", [P, TILES, HK])
    assert at[0] >= after_norm
    m.total = m.logsig[0:CHUNKS, 0, :]
    m.gate_up = put("gate_up", [RANK, HK])
    m.glr_raw = put("glr_raw", [P, DC * RANK])
    m.glr_hi = put("glr_hi", [P, DC * RANK], F32R)
    m.glr_lo = put("glr_lo", [P, DC * RANK], F32R)
    m.bgate = put("bgate", [P, HK])
    assert at[0] <= top - (4 * HEADS * CHUNKS + 32)
    at[0] = top - (4 * HEADS * CHUNKS + 32)
    end_of_heads = at[0]
    m.e_end = put("e_end", [P, HEADS * CHUNKS])
    at[0] = after_ht
    m.dec = put("dec", [P, TILES, DK])
    m.q_t = put("q_t", [P, SEQ])
    m.kd = put("kd", [P, TILES, DK])
    m.v = put("v", [P, TILES, DV])
    m.k_t = put("k_t", [P, SEQ])
    at[0] -= 4 * SEQ
    m.o = put("o", [P, TILES, DV])
    m.rg = put("rg", [P, TILES, DV])
    m.state = put("state", [P, 2, DV])
    m.head_g = put("head_g", [P, DV])
    m.e_now = put("e_now", [P, CHUNKS])
    m.oss = put("oss", [P, TILES])
    m.ostd = put("ostd", [P, TILES])
    m.orstd = put("orstd", [P, TILES])
    assert at[0] <= end_of_heads
    at[0] = after_ht + 4 * TILES * DK
    m.ot_hi = put("ot_hi", [P, TILES, DV], F32R)
    m.ot_lo = put("ot_lo", [P, TILES, DV], F32R)

    at[0] = after_ht
    m.v_out = put("v_out", [P, 2, TILES, SLICE])
    at[0] = after_ht
    m.gt_hi = put("gt_hi", [P, 2, SEQ], F32R)
    m.gt_lo = put("gt_lo", [P, 2, SEQ], F32R)
    m.v_s = put("v_s", [P, TILES, SLICE])
    m.ut = put("ut", [P, 2, BANK])
    m.mix = put("mix", [P, BANK])
    m.ln_g = put("ln_g", [P, SLICE])
    m.ln_b = put("ln_b", [P, SLICE])
    m.ws_t = put("ws_t", [P, SG * P])
    m.bs = put("bs", [P, SG * P])
    m.stats = put("stats", [P, TILES, SLICES * 6])
    m.mv = put("mv", [P, TILES, 2])
    m.lstd = put("lstd", [P, TILES])
    m.lrstd = put("lrstd", [P, TILES])
    m.lshift = put("lshift", [P, TILES])
    m.ws = put("ws", [P, SG, P])

    at[0] = after_norm
    m.r_raw = put("r_raw", [P, DC, ROUTES])
    m.r_hi = put("r_hi", [P, DC, ROUTES], F32R)
    m.r_lo = put("r_lo", [P, DC, ROUTES], F32R)
    m.r_bias = put("r_bias", [P, ROUTES])
    m.logit_t = put("logit_t", [ROUTES, SEQ])
    m.logit = put("logit", [P, TILES, ROUTES])
    m.glog = put("glog", [P, TILES, 8])
    m.gmax = put("gmax", [P, TILES, 8])
    m.gidx = put("gidx", [P, TILES, 8], U32)
    m.gsel = put("gsel", [P, TILES])
    m.gexp = put("gexp", [P, TILES, NG])
    m.gw = put("gw", [P, TILES])
    m.goh = put("goh", [P, TILES, NG])
    m.sel = put("sel", [P, TILES, NG, NE])
    m.chosen = put("chosen", [P, TILES, NE])
    m.cmax = put("cmax", [P, TILES, 8])
    m.cidx = put("cidx", [P, TILES, 8], U32)
    m.csel = put("csel", [P, TILES, TOP])
    m.e2 = put("e2", [P, TILES])
    m.eid = put("eid", [P, TOP, TILES])
    m.eoh = put("eoh", [P, TOP * TILES, EXPERTS])
    m.emask = put("emask", [P, TILES, EXPERTS], BF16)
    m.pre = put("pre", [P, TILES + 1, EXPERTS])
    m.rank = put("rank", [P, TILES, EXPERTS])
    m.pick = put("pick", [P, TOP * TILES, EXPERTS])
    m.rk = put("rk", [P, TOP * TILES])
    m.nov = put("nov", [P, EXPERTS])
    m.inc = put("inc", [P, 2, EXPERTS])
    m.ovb = put("ovb", [P, EXPERTS])
    m.q = put("q", [P, TOP * TILES])
    m.ovk = put("ovk", [P, TOP * TILES])
    m.t1 = put("t1", [P, TOP * TILES])
    m.tab = put("tab", [P, 3, COLS])
    m.tok_idx = put("tok_idx", [P, COLS], U32)
    m.dst_idx = put("dst_idx", [P, COLS], U32)
    m.ovx = put("ovx", [P, OV, EXPERTS])
    m.ovf = put("ovf", [P, OV + 1])
    m.ov_tab = put("ov_tab", [P, OV + 1], I32)
    at[0] = after_ht
    m.rowoh = put("rowoh", [P, TOP * TILES, P], BF16)
    m.coloh = put("coloh", [P, TOP * TILES, COLS], BF16)
    m.colval = put("colval", [P, TOP * TILES, 2, COLS], BF16)
    at[0] = region
    m.xg = put("xg", [P, 2, D])
    m.xt_hi = put("xt_hi", [P, 2, DC, P], F32R)
    m.xt_lo = put("xt_lo", [P, 2, DC, P], F32R)
    m.sil = put("sil", [P, FF])
    m.hid = put("hid", [P, FF])
    m.hidt_hi = put("hidt_hi", [P, FF], F32R)
    m.hidt_lo = put("hidt_lo", [P, FF], F32R)
    m.y = put("y", [P, 2, D])
    m.tok_col = put("tok_col", [P, 2, 8], U32)
    m.dst_col = put("dst_col", [P, 2, 8], U32)
    m.w_hi += [put(f"w_hi{k}", [P, PIECE], F32R) for k in range(SPLIT, MOE_SPLIT)]
    m.w_lo += [put(f"w_lo{k}", [P, PIECE], F32R) for k in range(SPLIT, MOE_SPLIT)]
    assert at[0] <= after_norm
    at[0] = after_norm
    m.pair = [put("pair0", [P, PAIRS[0], TOP, D])]
    m.squares = put("squares", [P, D])
    at[0] = region
    m.pair.append(put("pair1", [P, PAIRS[1], TOP, D]))
    m.o_out = put("o_out", [P, 4, D])
    assert at[0] <= after_norm

    m.tr = [ctx.enter_context(nc.psum_tensor(f"ps_tr{k}", [P, 2 * BANK], F32)) for k in range(2)]
    m.pj = [ctx.enter_context(nc.psum_tensor(f"ps_pj{k}", [P, BANK], F32)) for k in range(2)]
    m.ps = [ctx.enter_context(nc.psum_tensor(f"ps_aux{k}", [P, BANK], F32)) for k in range(2)]
    return m


def semaphores(nc, ctx):
    def sem(name):
        return ctx.enter_context(nc.semaphore(name))

    def stream(tag):
        q = Names()
        q.full = [sem(f"{tag}_raw_full{k}") for k in range(RAW)]
        q.hi, q.split = sem(f"{tag}_hi_done"), sem(f"{tag}_split_done")
        return q

    def experts(tag, ring):
        names = ("used", "tok_col", "dst_col", "xt_tr", "xt_hi", "xt_lo", "sil", "hid", "ht_tr", "ht_hi",
                 "ht_lo", "y_act")
        q = Names()
        q.ring = ring
        q.xg_full = [sem(f"{tag}_xg_full{k}") for k in range(ring)]
        q.y_out, q.y_free, q.go = sem(f"{tag}_y_out"), sem(f"{tag}_y_free"), sem(f"{tag}_dma_go")
        (q.used, q.tok_col, q.dst_col, q.xt_tr, q.xt_hi, q.xt_lo, q.sil, q.hid, q.ht_tr, q.ht_hi, q.ht_lo,
         q.y_act) = [sem(f"{tag}_{n}") for n in names]
        return q

    s = Names()
    s.w = stream("w")
    s.ov = [stream(f"ov{k}") for k in range(2)]
    s.e = experts("e", 2)
    s.oe = [experts(f"oe{k}", 1) for k in range(2)]
    s.meet = [sem(f"met_{n}") for n in ("pool", "act", "dve", "pe")]
    s.const = sem("const_ready")
    s.const_step = sem("const_step")
    s.x_in = [sem(f"x_in{k}") for k in range(X_LOADS)]
    s.gain = sem("gain_in")
    s.sq, s.std, s.h, s.n_tr, s.n_hi, s.n_lo = [sem(n) for n in (
        "norm_squares", "norm_std", "norm_h", "norm_turned", "norm_hi", "norm_lo")]
    s.h_free = sem("h_slot_free")
    s.h_out = [sem(f"h_out{k}") for k in range(2)]
    s.step = sem("dve_step")
    s.given_back = sem("raw_given_back")
    s.routed = sem("routed")
    s.pj_full, s.pj_act = sem("group_full"), sem("group_read")
    s.y_full, s.y_used = sem("out_tile_full"), sem("out_tile_added")
    s.gin, s.gup = sem("gate_in"), sem("gate_up_in")
    s.z_mm, s.z_dve, s.z_act, s.z_g, s.dec_mm, s.dec_act = [sem(n) for n in (
        "z_made", "z_biased", "z_logged", "log_decay", "decay_summed", "decay_exp")]
    s.dec_out = sem("decay_out")
    s.g_hi, s.g_lo = sem("log_decay_hi"), sem("log_decay_lo")
    s.k_tr, s.kd = sem("k_turned"), sem("k_decayed")
    s.head_in, s.e_now, s.e_std = sem("head_in"), sem("e_now_ready"), sem("o_rstd")
    s.u_full, s.s_upd, s.o_mm, s.o_evac, s.o_std, s.og, s.ot_tr, s.ot_hi, s.ot_lo, s.rgh = [sem(n) for n in (
        "update_made", "state_ready", "o_made", "o_out", "o_std", "o_gated", "o_turned", "o_hi", "o_lo", "r_gained")]
    s.ws_in, s.bn, s.v_in = sem("ws_in"), sem("v_stats"), sem("v_in")
    s.ws_tr, s.ws_masked, s.lvar, s.v_free = sem("ws_turned"), sem("ws_masked"), sem("v_variance"), sem("v_slot_free")
    s.v_st = sem("v_stored")
    s.mix_full, s.mix_used, s.ln_hat, s.vn, s.gt, s.gt_hi, s.gt_lo = [sem(n) for n in (
        "mix_made", "mix_read", "v_normed", "v_ready", "g_ready", "g_hi", "g_lo")]
    s.r_in, s.r_lo, s.r_mm, s.r_act = [sem(n) for n in ("router_in", "router_lo", "route_product", "route_exp")]
    s.r_tr, s.r_copied = sem("logits_turned"), sem("logits_copied")
    s.masked = sem("route_one_hot")
    s.pair_in = [sem(f"pair_in{k}") for k in range(PAIRS[1])]
    s.sum = sem("rows_summed")
    s.fin, s.out = sem("row_final"), [sem(f"out{k}") for k in range(4)]
    return s



class Chain:

    def __init__(self, engine, sem, at=0):
        self.engine, self.sem, self.at = engine, sem, at

    def __call__(self, instruction):
        self.at += 1
        instruction.then_inc(self.sem, 1)
        self.engine.wait_ge(self.sem, self.at)


def meet(s, engine, me, n):
    engine.drain().then_inc(s.meet[me], 1)
    for other in range(4):
        if other != me:
            engine.wait_ge(s.meet[other], n)


def split_hi(act, m, st, b, landed, used=None, ring=SPLIT):
    act.wait_ge(st.full[b % RAW], landed)
    if used is not None:
        act.wait_ge(*used)
    act.activation(m.w_hi[b % ring][:], m.raw[:, b % RAW, :], ACT.Copy).then_inc(st.hi, 1)


def split_lo(dve, m, st, b, n, ring=SPLIT):
    dve.wait_ge(st.hi, n + 1)
    dve.tensor_tensor(m.w_lo[b % ring][:], m.raw[:, b % RAW, :], m.w_hi[b % ring][:].bitcast(F32),
                      ALU.subtract).then_inc(st.split, 1)


def wait_split(pe, st, n):
    pe.wait_ge(st.split, n + 1 + RAW)


def raw_count(i, a, b):
    return i * (a // RAW * LANDED) + (b // RAW + 1) * LANDED


def ov_count(j, b):
    uses = 2 if b % RAW < BLOCK - RAW else 1
    return j * (uses * LANDED) + (b // RAW + 1) * LANDED


def group_free(pe, s, n):
    pe.wait_ge(s.pj_act, n + 1)


def three(pe, out, hi_l, lo_l, hi_r, lo_r, first, last):
    pe.matmul(out, hi_l, hi_r, start=first, stop=False)
    pe.matmul(out, hi_l, lo_r, start=False, stop=False)
    return pe.matmul(out, lo_l, hi_r, start=False, stop=last)



def sp_program(sp, m, s, d):
    for k in range(X_LOADS):
        n = TILES // X_LOADS
        rows = d.x[0, k * n * P:(k + 1) * n * P, :].rearrange("(t p) n -> p t n", p=P)
        sp.dma_start(m.x[:, k * n:(k + 1) * n, :], rows).then_inc(s.x_in[k], 16)

    def slot_free(n):
        sp.wait_ge(s.w.split, n + 1)

    w_in = d.gla_w_in[0].rearrange("(p c) n -> p c n", c=DC)
    with sp.Fori(0, HEADS) as h:
        qk = m.raw[:, 0, :].rearrange("p (c n) -> p c n", c=DC)
        slot_free(h * 4 + GLA_AT)
        for part in range(2):
            sp.dma_start(qk[:, :, part * DK:(part + 1) * DK],
                         w_in[:, :, bass.ds(h * DK + part * HK, DK)]).then_inc(s.w.full[0], 16)
        for k in range(2):
            slot_free(h * 4 + GLA_AT + k + 1)
            sp.dma_start(m.raw[:, k + 1, :].rearrange("p (c n) -> p c n", c=DC),
                         w_in[:, :, bass.ds(h * DV + 2 * HK + k * HV, DV)]).then_inc(s.w.full[k + 1], LANDED)
        slot_free(h * 4 + GLA_AT + 3)
        rows = d.gla_w_out[0][bass.ds(h * DV, DV), :]
        sp.dma_start(m.raw[:, 3, :], rows.rearrange("(p c) n -> p (c n)", c=2)).then_inc(s.w.full[3], LANDED)

    sp_experts(sp, m, s, d, 0)

    s_in = d.sgu_w_in[0].rearrange("(p c) n -> p c n", c=DC)
    with sp.Fori(0, SLICES // RAW) as i:
        for k in range(RAW):
            slot_free(i * RAW + SGU_V_AT + k)
            sp.dma_start(m.raw[:, k, :].rearrange("p (c n) -> p c n", c=DC),
                         s_in[:, :, bass.ds(i * (RAW * SLICE) + HALF + k * SLICE, SLICE)]).then_inc(s.w.full[k], LANDED)
    with sp.Fori(0, SLICES // 2) as i:
        for k in range(2):
            slot_free(i * RAW + SGU_U_AT + 2 * k)
            sp.dma_start(m.raw[:, 2 * k, :].rearrange("p (c n) -> p c n", c=DC),
                         s_in[:, :, bass.ds(i * (2 * SLICE) + k * SLICE, SLICE)]).then_inc(s.w.full[2 * k], LANDED)
            slot_free(i * RAW + SGU_U_AT + 2 * k + 1)
            rows = d.sgu_w_out[0][bass.ds(i * (2 * SLICE) + k * SLICE, SLICE), :]
            sp.dma_start(m.raw[:, 2 * k + 1, :], rows.rearrange("(p c) n -> p (c n)", c=2)) \
              .then_inc(s.w.full[2 * k + 1], LANDED)

    sp_experts(sp, m, s, d, 1)
    for k in range(4):
        sp.wait_ge(s.out[k], 16 * TILES // 4)


def expert_piece(d, layer, e, b):
    w, c = ((d.moe_w1, DC), (d.moe_w3, DC), (d.moe_w2, FC))[b // 2]
    rows = w[layer][bass.ds(e, 1)].rearrange("o (p c) n -> p (o c n)", c=c)
    return rows[:, (b % 2) * PIECE:(b % 2 + 1) * PIECE]


def sp_experts(sp, m, s, d, layer):
    def load(i, n, e, b):
        sp.wait_ge(s.w.split, i * (2 * BLOCK) + MOE_AT[layer] + n + 1)
        sp.dma_start(m.raw[:, n % RAW, :], expert_piece(d, layer, e, b)).then_inc(s.w.full[n % RAW], LANDED)

    def expert(i, b):
        first = AHEAD + b * BLOCK
        for k in range(2):
            load(i, first + k, i * 2 + b, 2 + k)
        for k in range(2):
            load(i, first + 2 + k, i * 2 + b + 1, k)
        for k in range(2):
            load(i, first + 4 + k, i * 2 + b, 4 + k)

    last = EXPERTS // 2 - 1
    for k in range(AHEAD):
        load(0, k, 0, k)
    with sp.Fori(0, last) as i:
        for b in range(2):
            expert(i, b)
    expert(last, 0)
    for k in range(4):
        load(last, AHEAD + BLOCK + k, EXPERTS - 1, 2 + k)
    ov = s.ov[layer]
    sp.wait_ge(s.routed, layer + 1)
    blocks = sp.value_load(m.ov_tab[0:1, OV:OV + 1], min_val=0, max_val=OV)
    with sp.If(blocks > 0):
        sp.wait_ge(s.w.split, MOE_AT[layer] + EXPERTS * BLOCK + RAW)
        with sp.Fori(0, blocks) as j:
            e = sp.value_load(m.ov_tab[0:1, bass.ds(j, 1)], min_val=0, max_val=EXPERTS - 1)
            for b in range(BLOCK):
                sp.wait_ge(ov.split, j * BLOCK + max(b + 1, RAW))
                sp.dma_start(m.raw[:, b % RAW, :], expert_piece(d, layer, e, b)).then_inc(ov.full[b % RAW], LANDED)
        sp.wait_ge(ov.split, blocks * BLOCK + RAW)
        sp.sem_inc(s.given_back, 1)



def load_gain(pool, m, s, gain):
    pool.dma_start(m.gain[:], gain.partition_broadcast(P)).then_inc(s.gain, 16)


def store_rows(pool, m, s, d, n, stored):
    for t in range(TILES + 1):
        if t < TILES:
            pool.wait_ge(s.h, n * TILES + t + 1)
            pool.dma_start(d.h[t * P:(t + 1) * P, :], m.h[:, t % H_RING, :]).then_inc(s.h_out[t % 2], 16)
        if t >= 1:
            pool.wait_ge(s.h_out[(t - 1) % 2], 16 * (stored * TILES // 2 + (t - 1) // 2 + 1))
            pool.sem_inc(s.h_free, 1)


def tile_std(act, m, s, n, t, junk):
    if t > 0:
        act.wait_ge(s.sq, n * TILES + t)
    act.activation(junk, m.x[:, t, :], ACT.Square, accum_out=m.ss[:, t:t + 1]).then_inc(s.sq, 1)
    act.wait_ge(s.sq, n * TILES + t + 1)
    act.activation(m.std[:, t:t + 1], m.ss[:, t:t + 1], ACT.Sqrt, scale=1.0 / D, bias=m.eps[:, 0:1]).then_inc(s.std, 1)


def tile_hi(act, m, s, n, t):
    act.wait_ge(s.n_tr, n * TILES + t + 3)
    act.activation(m.ht_hi[:, :, t * P:(t + 1) * P],
                   m.tr[t % 2][:].rearrange("p (c n) -> p c n", c=DC), ACT.Copy).then_inc(s.n_hi, 1)


def next_std(act, m, s, n, products, t, junk):
    act.wait_ge(s.y_used, (products - 1) * TILES + t + 1 + 2)
    tile_std(act, m, s, n, t, junk)


def norm_act(act, m, s, n):
    for t in range(TILES):
        tile_hi(act, m, s, n, t)


def tile_scale(dve, m, s, n, t, out, done, step):
    if n in (1, 3):
        if t == 0:
            dve.wait_ge(s.std, (n + 1) * TILES)
            step(dve.reciprocal(m.rstd[:], m.std[:]))
    else:
        dve.wait_ge(s.std, n * TILES + t + 1)
        step(dve.reciprocal(m.rstd[:, t:t + 1], m.std[:, t:t + 1]))
    if t == 0:
        dve.wait_ge(s.gain, 16 * (n + 1))
    dve.scalar_tensor_tensor(out, m.x[:, t, :], m.rstd[:, t:t + 1], m.gain[:], ALU.mult, ALU.mult).then_inc(done, 1)


def norm_dve(dve, m, s, n, step, stored=None, before=None, between=None):
    for t in range(-1, TILES + 2):
        if before is not None and t + 1 < TILES:
            before(t + 1)
        if 0 <= t < TILES:
            if stored is not None:
                dve.wait_ge(s.h_free, stored * TILES + t + 1)
            if t >= H_RING:
                dve.wait_ge(s.n_tr, n * TILES + t - H_RING + 3)
            tile_scale(dve, m, s, n, t, m.h[:, t % H_RING, :], s.h, step)
        if t == TILES and between is not None:
            between()
        if t >= 2:
            u = t - 2
            dve.wait_ge(s.n_hi, n * TILES + u + 1)
            cols = slice(u * P, (u + 1) * P)
            dve.tensor_tensor(m.ht_lo[:, :, cols], m.tr[u % 2][:].rearrange("p (c n) -> p c n", c=DC),
                              m.ht_hi[:, :, cols].bitcast(F32), ALU.subtract).then_inc(s.n_lo, 1)


def norm_pe(pe, m, s, n):
    with pe.Fori(0, TILES // H_RING) as i:
        for b in range(H_RING):
            pe.wait_ge(s.h, i * H_RING + n * TILES + b + 1)
            pe.wait_ge(s.n_lo, i * H_RING + n * TILES + b + 1)
            rows = m.h[:, b, :].rearrange("p (n c) -> p c n", c=DC)
            for c in range(DC):
                last = pe.transpose(m.tr[b % 2][:, c * P:(c + 1) * P], rows[:, c, :], m.ident[:])
            last.then_inc(s.n_tr, 1)


def turned_half(pe, s, n, g):
    pe.wait_ge(s.n_lo, n * TILES + (g + 1) * TILES // 2 + 2)


def project(pe, s, n, out, stationary, moving):
    group_free(pe, s, n)
    for c in range(DC):
        last = three(pe, out, stationary(c, 0), stationary(c, 1), moving(c, 0), moving(c, 1), c == 0, c == DC - 1)
    last.then_inc(s.pj_full, 1)


def out_tile(pe, m, s, n, t, stationary):
    pe.wait_ge(s.y_used, n + 1)
    for half in range(2):
        for c in range(2):
            at = c * D + half * BANK
            last = three(pe, m.tr[t % 2][:, half * BANK:(half + 1) * BANK], stationary(c, 0), stationary(c, 1),
                         m.w_hi[1][:, at:at + BANK], m.w_lo[1][:, at:at + BANK], c == 0, c == 1)
    last.then_inc(s.y_full, 1)


def add_rows(dve, m, s, n, t):
    dve.wait_ge(s.y_full, n + 1)
    dve.tensor_tensor(m.x[:, t, :], m.x[:, t, :], m.tr[t % 2][:], ALU.add).then_inc(s.y_used, 1)



def gates_load(pool, m, s, d):
    pool.dma_start(m.glr_raw[:].rearrange("p (c r) -> p c r", c=DC),
                   d.gla_w_in[0].rearrange("(p c) n -> p c n", c=DC)[:, :, 2 * HK + 2 * HV:]).then_inc(s.gin, 16)
    pool.dma_start(m.bgate[:], d.gla_b_gate[0].partition_broadcast(P)).then_inc(s.gin, 16)
    pool.dma_start(m.gate_up[:], d.gla_w_gate_up[0]).then_inc(s.gup, 16)


def gates_pool(pool, m, s, d):
    for t in range(TILES):
        pool.wait_ge(s.dec_act, t + 1)
        pool.dma_start(d.dec[t * P:(t + 1) * P, :], m.z[:, t, :]).then_inc(s.dec_out, 16)


def gates_pe(pe, m, s):
    pe.wait_ge(s.z_g, 1)
    for g in range(2):
        turned_half(pe, s, 0, g)
        cols = slice(g * BANK, (g + 1) * BANK)
        for c in range(DC):
            r = slice(c * RANK, (c + 1) * RANK)
            last = three(pe, m.pj[g][0:RANK, :], m.glr_hi[:, r], m.glr_lo[:, r],
                         m.ht_hi[:, c, cols], m.ht_lo[:, c, cols], c == 0, c == DC - 1)
        last.then_inc(s.z_mm, 1)
    pe.wait_ge(s.z_act, 2)
    pe.wait_ge(s.gup, 16)
    for t in range(TILES):
        if t >= 2:
            pe.wait_ge(s.z_dve, 2 * t - 3)
        pe.matmul(m.pj[t % 2][:], m.glr_t[:, t * P:(t + 1) * P], m.gate_up[:], start=True, stop=True).then_inc(s.z_mm, 1)
    for t in range(TILES):
        log_hi, log_lo = log_parts(m, t)
        pe.wait_ge(s.g_lo, t + 1)
        if t >= 2:
            pe.wait_ge(s.dec_act, t - 1)
        pe.matmul(m.ps[t % 2][:], m.after[:], log_hi, start=True, stop=False)
        pe.matmul(m.ps[t % 2][:], m.after[:], log_lo, start=False, stop=True)
        chunks = m.halves[:, CHUNKS - 2 - 2 * t:2 * CHUNKS - 2 - 2 * t]
        pe.matmul(m.pj[0][0:CHUNKS, :], chunks, log_hi, start=(t == 0), stop=False)
        pe.matmul(m.pj[0][0:CHUNKS, :], chunks, log_lo, start=False, stop=(t == TILES - 1)).then_inc(s.dec_mm, 1)
    pe.wait_ge(s.dec_act, TILES + 1)
    for h in range(HEADS):
        last = pe.transpose(m.tr[0][:, h * CHUNKS:(h + 1) * CHUNKS], m.total[:, h * DK:(h + 1) * DK],
                            m.ident[0:CHUNKS, 0:CHUNKS])
    last.then_inc(s.dec_mm, 1)


def log_parts(m, t):
    cols = slice(t % 4 * HK, (t % 4 + 1) * HK)
    return m.w_hi[1][:, cols], m.w_lo[1][:, cols]


def gates_act(act, m, s):
    for g in range(2):
        act.wait_ge(s.z_mm, g + 1)
        act.activation(m.glr_t[:, g * BANK:(g + 1) * BANK], m.pj[g][0:RANK, :], ACT.Copy).then_inc(s.z_act, 1)
    for t in range(TILES):
        act.wait_ge(s.z_dve, 2 * t + 2)
        act.activation(m.logsig[:, t, :], m.logsig[:, t, :], ACT.Exp).then_inc(s.z_act, 1)
        if t == TILES // 2 - 1:
            split_hi(act, m, s.w, 0, raw_count(0, 4, 0))
    for t in range(TILES):
        act.wait_ge(s.z_act, t + 3)
        act.activation(m.logsig[:, t, :], m.logsig[:, t, :], ACT.Ln, bias=m.one[:, 0:1]).then_inc(s.z_act, 1)
    for t in range(TILES + 2):
        if t < TILES:
            act.wait_ge(s.z_g, t + 2)
            if t >= 4:
                act.wait_ge(s.dec_mm, t - 3)
            act.activation(log_parts(m, t)[0], m.logsig[:, t, :], ACT.Copy).then_inc(s.g_hi, 1)
        if t >= 2:
            u = t - 2
            act.wait_ge(s.dec_mm, u + 1)
            act.activation(m.z[:, u, :], m.ps[u % 2][:], ACT.Exp, scale=1.0 / TAU).then_inc(s.dec_act, 1)
    act.activation(m.total, m.pj[0][0:CHUNKS, :], ACT.Copy).then_inc(s.dec_act, 1)
    act.wait_ge(s.dec_mm, TILES + 1)
    act.activation(m.e_end[:], m.tr[0][:, 0:HEADS * CHUNKS], ACT.Exp, scale=1.0 / TAU)


def low_rank_split(dve, m, s, step):
    dve.wait_ge(s.gin, 32)
    step(dve.tensor_copy(m.glr_hi[:], m.glr_raw[:]))
    dve.tensor_tensor(m.glr_lo[:], m.glr_raw[:], m.glr_hi[:].bitcast(F32), ALU.subtract).then_inc(s.z_g, 1)


def gates_dve(dve, m, s, step):
    for t in range(TILES):
        dve.wait_ge(s.z_mm, t + 3)
        dve.tensor_tensor(m.z[:, t, :], m.pj[t % 2][:], m.bgate[:], ALU.add).then_inc(s.z_dve, 1)
        dve.wait_ge(s.z_dve, 2 * t + 1)
        dve.scalar_tensor_tensor(m.logsig[:, t, :], m.z[:, t, :], -1.0, m.z[:, t, :], ALU.mult, ALU.min).then_inc(s.z_dve, 1)
    split_lo(dve, m, s.w, 0, 0)
    for t in range(TILES + 1):
        if t < TILES:
            dve.wait_ge(s.z_act, TILES + t + 3)
            dve.scalar_tensor_tensor(m.logsig[:, t, :], m.z[:, t, :], 0.0, m.logsig[:, t, :],
                                     ALU.min, ALU.subtract).then_inc(s.z_g, 1)
        if t >= 1:
            hi, lo = log_parts(m, t - 1)
            dve.wait_ge(s.g_hi, t)
            dve.tensor_tensor(lo, m.logsig[:, t - 1, :], hi.bitcast(F32), ALU.subtract).then_inc(s.g_lo, 1)



def heads_pool(pool, m, s, d):
    def load(h):
        pool.dma_start(m.head_g[:], d.gla_head_g[0][bass.ds(h, 1), :].partition_broadcast(P)
                       .rearrange("q o n -> q (o n)")).then_inc(s.head_in, 16)
        pool.dma_start(m.dec[:], d.dec[:, bass.ds(h * DK, DK)].rearrange("(t p) k -> p t k", p=P)).then_inc(s.head_in, 16)

    pool.wait_ge(s.dec_out, 16 * TILES)
    load(0)
    with pool.Fori(1, HEADS) as h:
        pool.wait_ge(s.og, h * TILES + TILES)
        load(h)


def heads_pe(pe, m, s):
    with pe.Fori(0, HEADS) as h:
        w = [m.w_hi, m.w_lo]
        ht = [m.ht_hi, m.ht_lo]
        first = h * HEAD_GROUPS

        def rows(n, t, slot):
            project(pe, s, first + n, m.pj[t % 2][:, 0:DV],
                    lambda c, part: ht[part][:, c, t * P:(t + 1) * P],
                    lambda c, part: w[part][slot][:, c * SLICE:(c + 1) * SLICE])

        wait_split(pe, s.w, h * 4 + GLA_AT)
        for g in range(4):
            project(pe, s, first + g, m.pj[g % 2][:],
                    lambda c, part: w[part][0][:, c * SLICE + g // 2 * DK:c * SLICE + (g // 2 + 1) * DK],
                    lambda c, part: ht[part][:, c, g % 2 * BANK:(g % 2 + 1) * BANK])
        wait_split(pe, s.w, h * 4 + GLA_AT + 1)
        for t in range(TILES):
            rows(4 + t, t, 1)
            if t == 0:
                pe.wait_ge(s.pj_act, first + 4 + 2)
                pe.wait_ge(s.y_used, h * TILES + 2)
                for k in range(TILES):
                    last = pe.transpose(m.tr[0][:, k * P:(k + 1) * P], m.k_t[:, k * P:(k + 1) * P], m.ident[:])
                last.then_inc(s.k_tr, 1)
        pe.wait_ge(s.kd, h + 1)
        wait_split(pe, s.w, h * 4 + GLA_AT + 2)
        for t in range(TILES):
            pe.wait_ge(s.pj_act, first + 4 + t + 1 + 2)
            for c in range(2 * t, 2 * t + 2):
                part = slice(c % 2 * CHUNK, (c % 2 + 1) * CHUNK)
                pe.wait_ge(s.s_upd, h * CHUNKS + c + 1)
                pe.matmul(m.ps[c % 2][:, 0:DV], m.kd[part, t, :], m.v[part, t, :],
                          start=True, stop=True).then_inc(s.u_full, 1)
            if t < TILES - 1:
                rows(12 + t, t, 0)
            pe.wait_ge(s.o_evac, h * TILES + t + 1)
            for c in range(2 * t, 2 * t + 2):
                pe.wait_ge(s.s_upd, h * CHUNKS + c + 3)
                pe.matmul(m.tr[t % 2][c % 2 * CHUNK:(c % 2 + 1) * CHUNK, 0:DV],
                          m.q_t[:, c * CHUNK:(c + 1) * CHUNK], m.state[:, c % 2, :],
                          start=True, stop=True).then_inc(s.o_mm, 1)

        rows(12 + TILES - 1, TILES - 1, 0)

        def turn(t):
            pe.wait_ge(s.og, h * TILES + t + 1 + TILES)
            pe.wait_ge(s.ot_lo, h * TILES + t + 1)
            o = m.o[:, t, :].rearrange("p (n c) -> p c n", c=2)
            for c in range(2):
                last = pe.transpose(m.ps[t % 2][:, c * P:(c + 1) * P], o[:, c, :], m.ident[:])
            last.then_inc(s.ot_tr, 1)

        wait_split(pe, s.w, h * 4 + GLA_AT + 3)
        ot = [m.ot_hi, m.ot_lo]
        turn(0)
        for t in range(TILES):
            if t + 1 < TILES:
                turn(t + 1)
            pe.wait_ge(s.ot_lo, h * TILES + t + 3)
            out_tile(pe, m, s, h * TILES + t, t, lambda c, part: ot[part][:, t, c * P:(c + 1) * P])


def heads_act(act, m, s):
    def head(h, last):
        first = h * HEAD_GROUPS

        def full(g):
            act.wait_ge(s.pj_full, first + g + 1)

        for g in range(2):
            full(g)
            act.activation(m.q_t[:, g * BANK:(g + 1) * BANK], m.pj[g][:], ACT.Copy, scale=DK ** -0.5).then_inc(s.pj_act, 1)
        for g in range(2):
            full(2 + g)
            act.activation(m.k_t[:, g * BANK:(g + 1) * BANK], m.pj[g][:], ACT.Copy).then_inc(s.pj_act, 1)
        split_hi(act, m, s.w, 2, raw_count(h, 4, 2))
        for t in range(TILES):
            full(4 + t)
            act.activation(m.v[:, t, :], m.pj[t % 2][:, 0:DV], ACT.Copy).then_inc(s.pj_act, 1)
        split_hi(act, m, s.w, 3, raw_count(h, 4, 3))
        def gate(t):
            full(12 + t)
            act.wait_ge(s.og, h * TILES + t + 1)
            act.activation(m.rg[:, t, :], m.pj[t % 2][:, 0:DV], ACT.Silu).then_inc(s.pj_act, 1)

        for t in range(TILES):
            if t < TILES - 1:
                gate(t)
            act.wait_ge(s.o_mm, h * CHUNKS + 2 * t + 4)
            act.activation(m.o[:, t, :], m.tr[t % 2][:, 0:DV], ACT.Copy)
            act.wait_ge(s.o_evac, h * TILES + t + 2)
            act.activation(m.tr[t % 2][:, BANK:BANK + DV], m.tr[t % 2][:, 0:DV], ACT.Square,
                           accum_out=m.oss[:, t:t + 1]).then_inc(s.o_evac, 1)
        act.wait_ge(s.o_evac, h * TILES + TILES + 2)
        act.activation(m.ostd[:], m.oss[:], ACT.Sqrt, scale=1.0 / DV, bias=m.eps[:, 0:1]).then_inc(s.o_std, 1)
        gate(TILES - 1)
        for t in range(TILES):
            act.wait_ge(s.ot_tr, h * TILES + t + 1)
            act.activation(m.ot_hi[:, t, :], m.ps[t % 2][:, 0:DV], ACT.Copy).then_inc(s.ot_hi, 1)
            if t == TILES // 2:
                split_hi(act, m, s.w, 4, raw_count(h, 4, 4))
            if last and t >= 2:
                next_std(act, m, s, 1, HEADS, t - 2, m.dec[:].rearrange("p t k -> p (t k)"))
        if last:
            for t in range(TILES - 2, TILES):
                next_std(act, m, s, 1, HEADS, t, m.dec[:].rearrange("p t k -> p (t k)"))
        else:
            split_hi(act, m, s.w, 5, raw_count(h, 4, 5), (s.y_full, h * TILES + TILES))

    split_hi(act, m, s.w, 1, raw_count(0, 4, 1))
    with act.Fori(0, HEADS - 1) as h:
        head(h, False)
    head(HEADS - 1, True)


def heads_dve(dve, m, s):
    def head(h):
        dve.wait_ge(s.head_in, h * 32 + 32)
        dve.tensor_copy(m.e_now[:], m.e_end[:, bass.ds(h * CHUNKS, CHUNKS)]).then_inc(s.e_now, 1)
        split_lo(dve, m, s.w, 2, h * 4 + GLA_AT + 2)
        dve.wait_ge(s.k_tr, h + 1)
        dve.tensor_tensor(m.kd[:], m.tr[0][:].rearrange("p (t k) -> p t k", t=TILES), m.dec[:], ALU.mult).then_inc(s.kd, 1)
        dve.wait_ge(s.e_now, h + 1)
        def gate_gain(t):
            dve.wait_ge(s.pj_act, h * HEAD_GROUPS + 12 + t + 1 + 2)
            dve.tensor_tensor(m.rg[:, t, :], m.rg[:, t, :], m.head_g[:], ALU.mult).then_inc(s.rgh, 1)

        for c in range(CHUNKS):
            dve.wait_ge(s.u_full, h * CHUNKS + c + 1)
            dve.wait_ge(s.o_mm, h * CHUNKS + c + 1)
            if c == 0:
                dve.tensor_copy(m.state[:, 0, :], m.ps[0][:, 0:DV]).then_inc(s.s_upd, 1)
            else:
                dve.wait_ge(s.s_upd, h * CHUNKS + c + 2)
                dve.scalar_tensor_tensor(m.state[:, c % 2, :], m.state[:, (c - 1) % 2, :], m.e_now[:, c:c + 1],
                                         m.ps[c % 2][:, 0:DV], ALU.mult, ALU.add).then_inc(s.s_upd, 1)
            if c == 1:
                split_lo(dve, m, s.w, 3, h * 4 + GLA_AT + 3)
            if c % 2 == 1 and c < CHUNKS - 1:
                gate_gain(c // 2)
        dve.wait_ge(s.o_std, h + 1)
        dve.reciprocal(m.orstd[:], m.ostd[:]).then_inc(s.e_std, 1)
        dve.wait_ge(s.e_std, h + 1)
        for t in range(TILES + 2):
            if t == 1:
                gate_gain(TILES - 1)
            if t < TILES:
                dve.wait_ge(s.rgh, h * TILES + (TILES - 1 if t < TILES - 1 else TILES))
                dve.scalar_tensor_tensor(m.o[:, t, :], m.o[:, t, :], m.orstd[:, t:t + 1], m.rg[:, t, :],
                                         ALU.mult, ALU.mult).then_inc(s.og, 1)
            if 1 <= t <= TILES:
                dve.wait_ge(s.ot_hi, h * TILES + t)
                dve.tensor_tensor(m.ot_lo[:, t - 1, :], m.ps[(t - 1) % 2][:, 0:DV],
                                  m.ot_hi[:, t - 1, :].bitcast(F32), ALU.subtract).then_inc(s.ot_lo, 1)
            if t == TILES - 1:
                split_lo(dve, m, s.w, 4, h * 4 + GLA_AT + 4)
            if t >= 2:
                add_rows(dve, m, s, h * TILES + t - 2, t - 2)

    split_lo(dve, m, s.w, 1, 1)
    with dve.Fori(0, HEADS - 1) as h:
        head(h)
        split_lo(dve, m, s.w, 5, h * 4 + GLA_AT + 5)
    head(HEADS - 1)



def sgu_pool(pool, m, s, d):
    pool.dma_start(m.ws[:], d.sgu_w_s[0].rearrange("g t q -> t g q")).then_inc(s.ws_in, 16)
    pool.dma_start(m.bs[:], d.sgu_b_s[0].rearrange("g t -> (g t)").partition_broadcast(P)).then_inc(s.ws_in, 16)
    pool.dma_start(m.ln_g[:], d.sgu_ln_g[0][0:SLICE].partition_broadcast(P)).then_inc(s.v_in, 16)
    pool.dma_start(m.ln_b[:], d.sgu_ln_b[0][0:SLICE].partition_broadcast(P)).then_inc(s.v_in, 16)
    with pool.Fori(0, SLICES // RAW) as i:
        for b in range(RAW):
            pool.wait_ge(s.pj_act, i * (RAW * TILES) + GROUPS_AT_V + TILES * (b + 1) + 2)
            pool.dma_start(d.v[:, bass.ds(i * (RAW * SLICE) + b * SLICE, SLICE)].rearrange("(t p) c -> p t c", p=P),
                           m.v_out[:, b % 2, :, :]).then_inc(s.v_st, 16)
            pool.wait_ge(s.v_st, i * (16 * RAW) + 16 * (b + 1))
            pool.sem_inc(s.v_free, 1)
    def load(j, v_only=False):
        cols = bass.ds(j * SLICE, SLICE)
        pool.dma_start(m.v_s[:], d.v[:, cols].rearrange("(t p) c -> p t c", p=P)).then_inc(s.v_in, 16)
        if not v_only:
            pool.dma_start(m.ln_g[:], d.sgu_ln_g[0][cols].partition_broadcast(P)).then_inc(s.v_in, 16)
            pool.dma_start(m.ln_b[:], d.sgu_ln_b[0][cols].partition_broadcast(P)).then_inc(s.v_in, 16)

    def scale(j):
        for half in range(2):
            part = m.v_s[:, half * TILES // 2:(half + 1) * TILES // 2, :]
            gain = m.ln_g[:].unsqueeze(1).to_broadcast([P, TILES // 2, SLICE])
            shift = m.ln_b[:].unsqueeze(1).to_broadcast([P, TILES // 2, SLICE])
            pool.wait_ge(s.ln_hat, j * 2 + half + 2)
            pool.tensor_tensor(part, part, gain, ALU.mult).then_inc(s.vn, 1)
            pool.wait_ge(s.vn, j * 4 + 2 * half + 1)
            pool.tensor_tensor(part, part, shift, ALU.add).then_inc(s.vn, 1)

    load(0, v_only=True)
    scale(0)
    with pool.Fori(1, SLICES) as j:
        pool.wait_ge(s.mix_full, j * 4)
        load(j)
        scale(j)


def sgu_pe(pe, m, s):
    ht = [m.ht_hi, m.ht_lo]
    w = [m.w_hi, m.w_lo]
    with pe.Fori(0, SLICES // RAW) as i:
        for b in range(RAW):
            wait_split(pe, s.w, i * RAW + SGU_V_AT + b)
            for t in range(TILES):
                project(pe, s, i * (RAW * TILES) + GROUPS_AT_V + b * TILES + t, m.pj[t % 2][:, 0:SLICE],
                        lambda c, part: ht[part][:, c, t * P:(t + 1) * P],
                        lambda c, part: w[part][b % 2][:, c * SLICE:(c + 1) * SLICE])
    pe.wait_ge(s.ws_masked, 1)
    for g in range(SG):
        last = pe.transpose(m.ps[0][:, g * P:(g + 1) * P], m.ws[:, g, :], m.ident[:])
    last.then_inc(s.ws_tr, 1)
    gt = [m.gt_hi, m.gt_lo]
    with pe.Fori(0, SLICES // 2) as i:
        for b in range(2):
            wait_split(pe, s.w, i * RAW + SGU_U_AT + 2 * b)
            vt = m.v_s[:].rearrange("p t (n c) -> p t c n", c=2)
            for q in range(5):
                half, c = q // 2, q % 2
                if q < 4:
                    project(pe, s, i * 8 + GROUPS_AT_U + 4 * b + q, m.pj[q % 2][:],
                            lambda k, part: w[part][0][:, k * SLICE:(k + 1) * SLICE].rearrange("p (n c) -> p c n", c=2)[:, c, :],
                            lambda k, part: ht[part][:, k, half * BANK:(half + 1) * BANK])
                if q >= 1:
                    half, c = (q - 1) // 2, (q - 1) % 2
                    if c == 0:
                        pe.wait_ge(s.vn, i * 8 + 4 * b + 2 * half + 2)
                    pe.wait_ge(s.mix_used, i * 8 + 4 * b + q)
                    for k in range(4):
                        last = pe.matmul(m.ps[(q - 1) % 2][:, k * P:(k + 1) * P], vt[:, half * 4 + k, c, :],
                                         m.ws_t[:, bass.ds(i * P, P)], start=True, stop=True)
                    last.then_inc(s.mix_full, 1)
            wait_split(pe, s.w, i * RAW + SGU_U_AT + 2 * b + 1)
            for t in range(TILES):
                if t % 4 == 0:
                    pe.wait_ge(s.gt_lo, i * 8 + 4 * b + t // 4 * 2 + 4)
                out_tile(pe, m, s, i * (2 * TILES) + (HEADS + b) * TILES + t, t,
                         lambda c, part: gt[part][:, c, t * P:(t + 1) * P])


def sgu_act(act, m, s):
    with act.Fori(0, SLICES // RAW) as i:
        for b in range(RAW):
            act.wait_ge(s.v_free, i * RAW + b + 1)
            for t in range(TILES):
                act.wait_ge(s.pj_full, i * (RAW * TILES) + GROUPS_AT_V + TILES * b + t + 1)
                act.wait_ge(s.bn, i * (RAW * 8) + 8 * b + t + 1)
                act.activation(m.v_out[:, b % 2, t, :], m.pj[t % 2][:, 0:SLICE], ACT.Gelu).then_inc(s.pj_act, 1)
            split_hi(act, m, s.w, SGU_V_AT + b + 2, raw_count(i, 4, SGU_V_AT + b + 2))
    act.wait_ge(s.ws_tr, 1)
    act.activation(m.ws_t[:], m.ps[0][:], ACT.Copy)
    act.wait_ge(s.lvar, 1)
    act.activation(m.lstd[:], m.mv[:, :, 1], ACT.Sqrt, bias=m.eps[:, 0:1]).then_inc(s.lvar, 1)
    def slice_(i, b, last):
        for q in range(4):
            half, c = q // 2, q % 2
            act.wait_ge(s.pj_full, i * 8 + GROUPS_AT_U + 4 * b + q + 1)
            act.wait_ge(s.gt_lo, i * 8 + 4 * b + q + 1)
            act.activation(m.ut[:, q % 2, :], m.pj[q % 2][:], ACT.Gelu).then_inc(s.pj_act, 1)
            act.wait_ge(s.gt, i * 8 + 4 * b + q + 1)
            act.activation(m.gt_hi[:, c, half * BANK:(half + 1) * BANK], m.ut[:, q % 2, :], ACT.Copy).then_inc(s.gt_hi, 1)
        split_hi(act, m, s.w, SGU_U_AT + 2 * b + 2, raw_count(i, 4, SGU_U_AT + 2 * b + 2))
        if last:
            for t in range(TILES):
                next_std(act, m, s, 3, HEADS + SLICES, t, m.v_s[:, 0:D // SLICE, :].rearrange("p t n -> p (t n)"))
        else:
            split_hi(act, m, s.w, SGU_U_AT + 2 * b + 3, raw_count(i, 4, SGU_U_AT + 2 * b + 3),
                     (s.y_full, i * (2 * TILES) + (HEADS + b + 1) * TILES))

    with act.Fori(0, SLICES // 2 - 1) as i:
        slice_(i, 0, False)
        slice_(i, 1, False)
    slice_(SLICES // 2 - 1, 0, False)
    slice_(SLICES // 2 - 1, 1, True)


def sgu_dve(dve, m, s, step):
    dve.wait_ge(s.ws_in, 32)
    dve.memset(m.ws[0:CHUNK, :, CHUNK:P], 0.0).then_inc(s.ws_masked, 1)
    with dve.Fori(0, SLICES // RAW) as i:
        for b in range(RAW):
            for t in range(TILES):
                dve.wait_ge(s.pj_act, i * (RAW * TILES) + GROUPS_AT_V + TILES * b + t + 1 + 2)
                dve.bn_stats(m.stats[:, t, bass.ds(i * (RAW * 6) + b * 6, 6)], m.v_out[:, b % 2, t, :]).then_inc(s.bn, 1)
            split_lo(dve, m, s.w, SGU_V_AT + b + 2, i * RAW + SGU_V_AT + b + 2)
    dve.wait_ge(s.bn, SLICES * TILES + 16)
    for t in range(TILES):
        last = dve.bn_aggr(m.mv[:, t, :], m.stats[:, t, :])
    last.then_inc(s.lvar, 1)
    dve.wait_ge(s.lvar, 2)
    step(dve.reciprocal(m.lrstd[:], m.lstd[:]))
    step(dve.scalar_tensor_tensor(m.lshift[:], m.mv[:, :, 0], -1.0, m.lrstd[:], ALU.mult, ALU.mult))
    dve.drain().then_inc(s.ln_hat, 1)

    def normalise(j, tiles):
        for t in tiles:
            if t == 0:
                dve.wait_ge(s.v_in, j * 48 + 48)
            last = dve.tensor_scalar(m.v_s[:, t, :], m.v_s[:, t, :], m.lrstd[:, t:t + 1], m.lshift[:, t:t + 1],
                                     ALU.mult, ALU.add)
            if t % (TILES // 2) == TILES // 2 - 1:
                last.then_inc(s.ln_hat, 1)

    def slice_(i, b, last):
        for q in range(4):
            half, c = q // 2, q % 2
            dve.wait_ge(s.mix_full, i * 8 + 4 * b + q + 1)
            bias = m.bs[:, bass.ds(i * P, P)].unsqueeze(1).to_broadcast([P, 4, P])
            dve.tensor_tensor(m.mix[:].rearrange("p (k t) -> p k t", k=4),
                              m.ps[q % 2][:].rearrange("p (k t) -> p k t", k=4), bias, ALU.add).then_inc(s.mix_used, 1)
            dve.wait_ge(s.mix_used, i * 8 + 4 * b + q + 3)
            dve.wait_ge(s.pj_act, i * 8 + GROUPS_AT_U + 4 * b + q + 1 + 2)
            dve.tensor_tensor(m.ut[:, q % 2, :], m.ut[:, q % 2, :], m.mix[:], ALU.mult).then_inc(s.gt, 1)
            dve.wait_ge(s.gt_hi, i * 8 + 4 * b + q + 1)
            cols = slice(half * BANK, (half + 1) * BANK)
            dve.tensor_tensor(m.gt_lo[:, c, cols], m.ut[:, q % 2, :], m.gt_hi[:, c, cols].bitcast(F32),
                              ALU.subtract).then_inc(s.gt_lo, 1)
        for t in range(TILES):
            add_rows(dve, m, s, i * (2 * TILES) + (HEADS + b) * TILES + t, t)
            if t == 1:
                split_lo(dve, m, s.w, SGU_U_AT + 2 * b + 2, i * RAW + SGU_U_AT + 2 * b + 2)
            if 2 <= t < 6 and not last:
                normalise(i * 2 + b + 1, (2 * t - 4, 2 * t - 3))
        if not last:
            split_lo(dve, m, s.w, SGU_U_AT + 2 * b + 3, i * RAW + SGU_U_AT + 2 * b + 3)

    normalise(0, range(TILES))
    with dve.Fori(0, SLICES // 2 - 1) as i:
        slice_(i, 0, False)
        slice_(i, 1, False)
    slice_(SLICES // 2 - 1, 0, False)
    slice_(SLICES // 2 - 1, 1, True)



def route_load(act, m, s, d, layer):
    act.dma_start(m.r_raw[:, :, 0:NG], d.moe_w_group[layer].rearrange("(p c) g -> p c g", c=DC)).then_inc(s.r_in, 16)
    for g in range(NG):
        at = NG + g * NE
        act.dma_start(m.r_raw[:, :, at:at + NE], d.moe_w_sub[layer][g].rearrange("(p c) e -> p c e", c=DC)).then_inc(s.r_in, 16)
    act.dma_start(m.r_bias[:, 0:NG], d.moe_b_group[layer].partition_broadcast(P)).then_inc(s.r_in, 16)
    act.dma_start(m.r_bias[:, NG:ROUTES], d.moe_b_sub[layer].rearrange("g e -> (g e)").partition_broadcast(P)).then_inc(s.r_in, 16)


ROUTER_LOADS = 16 * (NG + 3)


def route_pe(pe, m, s, layer):
    pe.wait_ge(s.r_lo, layer + 1)
    for g in range(2):
        turned_half(pe, s, 1 + 2 * layer, g)
        cols = slice(g * BANK, (g + 1) * BANK)
        for c in range(DC):
            last = three(pe, m.pj[g][0:ROUTES, :], m.r_hi[:, c, :], m.r_lo[:, c, :],
                         m.ht_hi[:, c, cols], m.ht_lo[:, c, cols], c == 0, c == DC - 1)
        last.then_inc(s.r_tr, 1)
    for g in range(2):
        pe.wait_ge(s.r_copied, layer * 2 + g + 1)
        for t in range(g * TILES // 2, (g + 1) * TILES // 2):
            last = pe.transpose(m.ps[0][:, t * ROUTES:(t + 1) * ROUTES], m.logit_t[:, t * P:(t + 1) * P],
                                m.ident[0:ROUTES, 0:ROUTES])
    last.then_inc(s.r_mm, 1)
    pe.wait_ge(s.masked, layer * 2 + 1)
    flat = m.emask[:].rearrange("p t e -> p (t e)")
    pe.matmul(m.ps[1][:, 0:TILES * EXPERTS], m.before[:], flat, start=True, stop=True)
    pe.matmul(m.ps[0][:, 0:TILES * EXPERTS], m.ones[:], flat, start=True, stop=True).then_inc(s.r_mm, 1)
    pe.wait_ge(s.masked, layer * 2 + 2)
    for a in range(TOP * TILES):
        last = pe.matmul(m.ps[1][:, 0:2 * COLS], m.rowoh[:, a, :], m.colval[:, a, :, :].rearrange("p v c -> p (v c)"),
                         start=(a == 0), stop=(a == TOP * TILES - 1))
    last.then_inc(s.r_mm, 1)


def route_act(act, m, s, layer):
    split_hi(act, m, s.w, 1, raw_count(0, 4, MOE_AT[layer] + 1))
    for g in range(2):
        act.wait_ge(s.r_tr, layer * 2 + g + 1)
        act.activation(m.logit_t[:, g * BANK:(g + 1) * BANK], m.pj[g][0:ROUTES, :], ACT.Copy).then_inc(s.r_copied, 1)
    act.wait_ge(s.r_act, layer * 4 + 1)
    act.activation(m.gexp[:], m.gexp[:], ACT.Exp).then_inc(s.r_act, 1)
    act.wait_ge(s.r_act, layer * 4 + 3)
    act.activation(m.e2[:], m.e2[:], ACT.Exp).then_inc(s.r_act, 1)


def router_split(dve, m, s, layer, step):
    dve.wait_ge(s.r_in, (layer + 1) * ROUTER_LOADS)
    step(dve.tensor_copy(m.r_hi[:], m.r_raw[:]))
    dve.tensor_tensor(m.r_lo[:], m.r_raw[:], m.r_hi[:].bitcast(F32), ALU.subtract).then_inc(s.r_lo, 1)


def route_dve(dve, m, s, layer, step):
    def tiles(ap, *shape):
        return ap.to_broadcast([P, *shape])

    step(dve.memset(m.glog[:], -3.0e38))
    split_lo(dve, m, s.w, 1, MOE_AT[layer] + 1)
    dve.wait_ge(s.r_mm, layer * 3 + 1)
    step(dve.tensor_tensor(m.logit[:], m.ps[0][:, 0:TILES * ROUTES].rearrange("p (t r) -> p t r", t=TILES),
                           tiles(m.r_bias[:].unsqueeze(1), TILES, ROUTES), ALU.add))
    step(dve.tensor_copy(m.glog[:, :, 0:NG], m.logit[:, :, 0:NG]))
    for t in range(TILES):
        last = dve.max(m.gmax[:, t, :], m.glog[:, t, :])
    step(last)
    for t in range(TILES):
        last = dve.max_index(m.gidx[:, t, :], m.gmax[:, t, :], m.glog[:, t, :])
    step(last)
    dve.tensor_tensor(m.gexp[:], m.glog[:, :, 0:NG], tiles(m.gmax[:, :, 0:1], TILES, NG), ALU.subtract).then_inc(s.r_act, 1)
    step(dve.tensor_copy(m.gsel[:], m.gidx[:, :, 0]))
    step(dve.tensor_tensor(m.goh[:], tiles(m.count[:, 0:NG].unsqueeze(1), TILES, NG),
                           tiles(m.gsel[:].unsqueeze(2), TILES, NG), ALU.is_equal))
    for g in range(NG):
        at = NG + g * NE
        last = dve.tensor_tensor(m.sel[:, :, g, :], m.logit[:, :, at:at + NE],
                                 tiles(m.goh[:, :, g:g + 1], TILES, NE), ALU.mult)
    step(last)
    step(dve.tensor_reduce(m.chosen[:], m.sel[:].rearrange("p t g e -> p t e g"), AX_X, ALU.add))
    for t in range(TILES):
        last = dve.max(m.cmax[:, t, :], m.chosen[:, t, :])
    step(last)
    for t in range(TILES):
        last = dve.max_index(m.cidx[:, t, :], m.cmax[:, t, :], m.chosen[:, t, :])
    step(last)
    dve.wait_ge(s.r_act, layer * 4 + 2)
    dve.tensor_tensor(m.e2[:], m.cmax[:, :, 1], m.cmax[:, :, 0], ALU.subtract).then_inc(s.r_act, 1)
    step(dve.tensor_reduce(m.gw[:], m.gexp[:], AX_X, ALU.add))
    step(dve.reciprocal(m.gw[:], m.gw[:]))
    step(dve.tensor_copy(m.csel[:], m.cidx[:, :, 0:TOP]))
    for k in range(TOP):
        last = dve.scalar_tensor_tensor(m.eid[:, k, :], m.gsel[:], float(NE), m.csel[:, :, k], ALU.mult, ALU.add)
    step(last)
    eid = m.eid[:].rearrange("p k t -> p (k t)")
    n = TOP * TILES
    step(dve.tensor_tensor(m.eoh[:], tiles(m.count[:, 0:EXPERTS].unsqueeze(1), n, EXPERTS),
                           tiles(eid.unsqueeze(2), n, EXPERTS), ALU.is_equal))
    dve.tensor_tensor(m.emask[:], m.eoh[:, 0:TILES, :], m.eoh[:, TILES:, :], ALU.add).then_inc(s.masked, 1)
    dve.wait_ge(s.r_act, layer * 4 + 4)
    step(dve.tensor_scalar(m.gate[:, 0, :], m.e2[:], 1.0, None, ALU.add))
    step(dve.reciprocal(m.gate[:, 0, :], m.gate[:, 0, :]))
    step(dve.tensor_tensor(m.gate[:, 0, :], m.gate[:, 0, :], m.gw[:], ALU.mult))
    step(dve.tensor_tensor(m.gate[:, 1, :], m.gate[:, 0, :], m.e2[:], ALU.mult))
    step(dve.memset(m.pre[:, 0, :], 0.0))
    dve.wait_ge(s.r_mm, layer * 3 + 2)
    for t in range(TILES):
        step(dve.tensor_tensor(m.pre[:, t + 1, :], m.pre[:, t, :], m.ps[0][:, t * EXPERTS:(t + 1) * EXPERTS], ALU.add))
    step(dve.tensor_tensor(m.rank[:], m.ps[1][:, 0:TILES * EXPERTS].rearrange("p (t e) -> p t e", t=TILES),
                           m.pre[:, 0:TILES, :], ALU.add))
    for k in range(TOP):
        last = dve.tensor_tensor(m.pick[:, k * TILES:(k + 1) * TILES, :], m.eoh[:, k * TILES:(k + 1) * TILES, :],
                                 m.rank[:], ALU.mult)
    step(last)
    step(dve.tensor_reduce(m.rk[:], m.pick[:], AX_X, ALU.add))
    count = m.pre[:, TILES, :]
    step(dve.tensor_scalar(m.nov[:], count, float(P), None, ALU.is_gt))
    for k in range(2, SEQ // P):
        step(dve.scalar_tensor_tensor(m.nov[:], count, float(k * P), m.nov[:], ALU.is_gt, ALU.add))
    step(dve.tensor_copy(m.inc[:, 0, :], m.nov[:]))
    k, now = 1, 0
    while k < EXPERTS:
        dve.tensor_copy(m.inc[:, 1 - now, 0:k], m.inc[:, now, 0:k])
        step(dve.tensor_tensor(m.inc[:, 1 - now, k:], m.inc[:, now, k:], m.inc[:, now, 0:EXPERTS - k], ALU.add))
        k, now = 2 * k, 1 - now
    inc = m.inc[:, now, :]
    step(dve.tensor_tensor(m.ovb[:], inc, m.nov[:], ALU.subtract))
    step(dve.tensor_scalar(m.q[:], m.rk[:], float(P), None, ALU.is_ge))
    for k in range(2, SEQ // P):
        step(dve.scalar_tensor_tensor(m.q[:], m.rk[:], float(k * P), m.q[:], ALU.is_ge, ALU.add))
    step(dve.scalar_tensor_tensor(m.rk[:], m.q[:], -float(P), m.rk[:], ALU.mult, ALU.add))
    step(dve.tensor_tensor(m.pick[:], m.eoh[:], tiles(m.ovb[:].unsqueeze(1), n, EXPERTS), ALU.mult))
    step(dve.tensor_reduce(m.ovk[:], m.pick[:], AX_X, ALU.add))
    step(dve.scalar_tensor_tensor(m.ovk[:], m.ovk[:], float(EXPERTS - 1), m.q[:], ALU.add, ALU.add))
    step(dve.tensor_tensor(m.ovk[:], m.ovk[:], eid, ALU.subtract))
    step(dve.tensor_scalar(m.t1[:], m.q[:], 0.0, None, ALU.is_gt))
    step(dve.tensor_tensor(m.ovk[:], m.ovk[:], m.t1[:], ALU.mult))
    step(dve.tensor_tensor(m.ovk[:], m.ovk[:], eid, ALU.add))
    dve.wait_ge(s.h_free, (layer + 1) * TILES + H_RING)
    dve.tensor_tensor(m.rowoh[:], tiles(m.count[:].unsqueeze(1), n, P), tiles(m.rk[:].unsqueeze(2), n, P), ALU.is_equal)
    step(dve.tensor_tensor(m.coloh[:], tiles(m.count[:, 0:COLS].unsqueeze(1), n, COLS),
                           tiles(m.ovk[:].unsqueeze(2), n, COLS), ALU.is_equal))
    step(dve.tensor_tensor(m.colval[:, :, 0, :], m.coloh[:], tiles(m.block[:].unsqueeze(2), n, COLS), ALU.mult))
    dve.tensor_scalar(m.colval[:, :, 1, :], m.coloh[:], m.row[:, 0:1], None, ALU.mult).then_inc(s.masked, 1)
    step(dve.tensor_tensor(m.ovx[:], tiles(inc.unsqueeze(1), OV, EXPERTS),
                           tiles(m.count[:, 0:OV].unsqueeze(2), OV, EXPERTS), ALU.is_le))
    dve.tensor_copy(m.ovf[:, OV:OV + 1], inc[:, EXPERTS - 1:EXPERTS])
    step(dve.tensor_reduce(m.ovf[:, 0:OV], m.ovx[:], AX_X, ALU.add))
    step(dve.tensor_scalar(m.ovf[:, 0:OV], m.ovf[:, 0:OV], float(EXPERTS - 1), None, ALU.min))
    step(dve.tensor_copy(m.ov_tab[:], m.ovf[:]))
    dve.wait_ge(s.r_mm, layer * 3 + 3)
    empty, dst, tok = m.tab[:, 0, :], m.tab[:, 1, :], m.tab[:, 2, :]
    dve.tensor_scalar(empty, m.ps[1][:, 0:COLS], 0.0, float(NOWHERE), ALU.is_equal, ALU.mult)
    step(dve.tensor_scalar(dst, m.ps[1][:, 0:COLS], float(P), -float(P), ALU.mult, ALU.add))
    step(dve.tensor_tensor(dst, dst, m.ps[1][:, COLS:2 * COLS], ALU.add))
    step(dve.tensor_tensor(dst, dst, empty, ALU.add))
    step(dve.tensor_scalar(tok, dst, float(SEQ), -float(SEQ), ALU.is_ge, ALU.mult))
    step(dve.tensor_tensor(tok, tok, dst, ALU.add))
    step(dve.tensor_copy(m.tok_idx[:], tok))
    step(dve.tensor_copy(m.dst_idx[:], dst))
    dve.drain().then_inc(s.routed, 1)



def gather(pool, m, q, d, i, a, b, col):
    slot = b % q.ring
    pool.wait_ge(q.xt_tr, i * a + b + 1)
    pool.tensor_copy(m.tok_col[:, slot, 0:1], m.tok_idx[:, bass.ds(col, 1)]).then_inc(q.tok_col, 1)
    pool.wait_ge(q.tok_col, i * a + b + 1)
    pool.sem_inc(q.go, 1)
    pool.indirect_dma_start(out=m.xg[:, slot, :], out_offset=None, in_=d.h[:, :],
                            in_offset=bass.IndirectOffsetOnAxis(ap=m.tok_col[:, slot, 0:1], axis=0),
                            bounds_check=SEQ - 1, oob_is_err=False).then_inc(q.xg_full[slot], 16)


def uses(i, a, b, ring):
    return i * (a // ring) + (b // ring + 1)


def scatter(pool, m, q, d, i, a, b, col):
    slot = b % q.ring
    pool.tensor_copy(m.dst_col[:, slot, 0:1], m.dst_idx[:, bass.ds(col, 1)]).then_inc(q.dst_col, 1)
    pool.wait_ge(q.dst_col, i * a + b + 1)
    pool.wait_ge(q.y_act, i * a + b + 2)
    pool.sem_inc(q.go, 1)
    pool.indirect_dma_start(out=d.y[:, :], out_offset=bass.IndirectOffsetOnAxis(ap=m.dst_col[:, slot, 0:1], axis=0),
                            in_=m.y[:, slot, :], in_offset=None,
                            bounds_check=ASSIGN - 1, oob_is_err=False).then_inc(q.y_out, 16)
    pool.wait_ge(q.y_out, i * (16 * a) + 16 * (b + 1))
    pool.sem_inc(q.y_free, 1)


def turn_rows(pe, m, q, i, a, b):
    slot = b % q.ring
    pe.wait_ge(q.xg_full[slot], uses(i, a, b, q.ring) * 16)
    pe.wait_ge(q.xt_lo, i * a + b + 1)
    rows = m.xg[:, slot, :].rearrange("p (n c) -> p c n", c=DC)
    for c in range(DC):
        last = pe.transpose(m.tr[0][:, c * P:(c + 1) * P], rows[:, c, :], m.ident[:])
    last.then_inc(q.xt_tr, 1)


def wide(pe, m, q, w_slots, st, n, k, slot, bank, used):
    wait_split(pe, st, n)
    for c in range(4):
        row = k * 4 + c
        cols = slice(c * FF, (c + 1) * FF)
        last = three(pe, m.pj[bank][:], m.xt_hi[:, slot, row, :], m.xt_lo[:, slot, row, :],
                     m.w_hi[w_slots][:, cols], m.w_lo[w_slots][:, cols], row == 0, row == DC - 1)
    last.then_inc(used, 1)


def turn_hid(pe, m, q, i, a, b):
    pe.wait_ge(q.hid, i * a + b + 2)
    pe.wait_ge(q.ht_lo, i * a + b + 1)
    hid = m.hid[:].rearrange("p (n c) -> p c n", c=FC)
    for c in range(FC):
        last = pe.transpose(m.ps[0][:, c * P:(c + 1) * P], hid[:, c, :], m.ident[:])
    last.then_inc(q.ht_tr, 1)


def narrow(pe, m, q, w_slot, st, n, k, used):
    wait_split(pe, st, n)
    for half in range(2):
        for c in range(2):
            row = 2 * k + c
            at = c * D + half * BANK
            rows = slice(row * P, (row + 1) * P)
            last = three(pe, m.tr[1][:, half * BANK:(half + 1) * BANK], m.hidt_hi[:, rows], m.hidt_lo[:, rows],
                         m.w_hi[w_slot][:, at:at + BANK], m.w_lo[w_slot][:, at:at + BANK], row == 0, row == FC - 1)
    last.then_inc(used, 1)


def rows_hi(act, m, q, i, a, b):
    slot = b % q.ring
    act.wait_ge(q.xt_tr, i * a + b + 1 + q.ring)
    act.activation(m.xt_hi[:, slot], m.tr[0][:].rearrange("p (c n) -> p c n", c=DC), ACT.Copy).then_inc(q.xt_hi, 1)


def rows_lo(dve, m, q, i, a, b):
    slot = b % q.ring
    dve.wait_ge(q.xt_hi, i * a + b + 1)
    dve.tensor_tensor(m.xt_lo[:, slot], m.tr[0][:].rearrange("p (c n) -> p c n", c=DC),
                      m.xt_hi[:, slot].bitcast(F32), ALU.subtract).then_inc(q.xt_lo, 1)


def silu(act, m, q, count):
    act.wait_ge(q.used, count)
    act.activation(m.sil[:], m.pj[0][:], ACT.Silu).then_inc(q.sil, 1)


def hid_hi(act, m, q, i, a, b):
    act.wait_ge(q.ht_tr, i * a + b + 1)
    act.activation(m.hidt_hi[:], m.ps[0][:], ACT.Copy).then_inc(q.ht_hi, 1)


def rows_out(act, m, q, i, a, b, count):
    slot = b % q.ring
    act.wait_ge(q.used, count)
    act.wait_ge(q.y_free, i * a + b + 1)
    act.activation(m.y[:, slot, :], m.tr[1][:], ACT.Copy).then_inc(q.y_act, 1)


def gate_hid(dve, m, q, i, a, b, count):
    dve.wait_ge(q.sil, i * a + b + 2)
    dve.wait_ge(q.used, count)
    dve.tensor_tensor(m.hid[:], m.sil[:], m.pj[1][:], ALU.mult).then_inc(q.hid, 1)


def hid_lo(dve, m, q, i, a, b):
    dve.wait_ge(q.ht_hi, i * a + b + 1)
    dve.tensor_tensor(m.hidt_lo[:], m.ps[0][:], m.hidt_hi[:].bitcast(F32), ALU.subtract).then_inc(q.ht_lo, 1)


def overflow(engine, m, body):
    blocks = engine.value_load(m.ov_tab[0:1, OV:OV + 1], min_val=0, max_val=OV)
    with engine.If(blocks > 0):
        with engine.Fori(0, blocks) as j:
            body(j)


def experts_pool(pool, m, s, d, layer, next_gain):
    q, at = s.e, layer * EXPERTS
    for b in range(3):
        gather(pool, m, q, d, 0, 2, at + b, b)
    load_gain(pool, m, s, next_gain)
    loops = (EXPERTS - 3) // 2
    with pool.Fori(0, loops) as i:
        for b in range(2):
            gather(pool, m, q, d, i, 2, at + b + 3, i * 2 + b + 3)
            scatter(pool, m, q, d, i, 2, at + b, i * 2 + b)
    for b in range(EXPERTS - 2 * loops):
        if 2 * loops + b + 3 < EXPERTS:
            gather(pool, m, q, d, loops, 2, at + b + 3, 2 * loops + b + 3)
        scatter(pool, m, q, d, loops, 2, at + b, 2 * loops + b)
    oq = s.oe[layer]

    def body(j):
        gather(pool, m, oq, d, j, 1, 0, j + EXPERTS)
        scatter(pool, m, oq, d, j, 1, 0, j + EXPERTS)

    overflow(pool, m, body)


def experts_pe(pe, m, s, layer):
    q, at = s.e, layer * EXPERTS

    def w_piece(i, n):
        return i * (2 * BLOCK) + MOE_AT[layer] + n, n % MOE_SPLIT

    def x_w1(i, b, k):
        if k == 0:
            pe.wait_ge(q.xt_lo, i * 2 + at + b + 2)
            pe.wait_ge(q.sil, i * 2 + at + b + 1)
        n, slot = w_piece(i, (b - 1) * BLOCK + AHEAD + 2 + k if b > 0 else k)
        wide(pe, m, q, slot, s.w, n, k, b % 2, 0, q.used)

    def expert(i, b, w1=True, turn=True):
        first = AHEAD + b * BLOCK
        pe.wait_ge(q.hid, i * 2 + at + b + 1)
        for k in range(2):
            n, slot = w_piece(i, first + k)
            wide(pe, m, q, slot, s.w, n, k, b % 2, 1, q.used)
        if w1:
            x_w1(i, b + 1, 0)
        turn_hid(pe, m, q, i, 2, at + b)
        if w1:
            x_w1(i, b + 1, 1)
        pe.wait_ge(q.ht_lo, i * 2 + at + b + 2)
        pe.wait_ge(q.y_act, i * 2 + at + b + 1)
        for k in range(2):
            n, slot = w_piece(i, first + (4 if w1 else 2) + k)
            narrow(pe, m, q, slot, s.w, n, k, q.used)
            if turn and k == 0:
                turn_rows(pe, m, q, i, 2, at + b + 2)

    turn_rows(pe, m, q, 0, 2, at)
    x_w1(0, 0, 0)
    x_w1(0, 0, 1)
    turn_rows(pe, m, q, 0, 2, at + 1)
    last = EXPERTS // 2 - 1
    with pe.Fori(0, last) as i:
        for b in range(2):
            expert(i, b)
    expert(last, 0, turn=False)
    expert(last, 1, w1=False, turn=False)

    def body(j):
        oq, st = s.oe[layer], s.ov[layer]
        pe.wait_ge(q.y_act, (layer + 1) * EXPERTS + 1)
        pe.wait_ge(oq.y_act, j + 1)
        turn_rows(pe, m, oq, j, 1, 0)
        pe.wait_ge(oq.xt_lo, j + 2)
        for k in range(4):
            wide(pe, m, oq, k % MOE_SPLIT, st, j * BLOCK + k, k % 2, 0, k // 2, oq.used)
        turn_hid(pe, m, oq, j, 1, 0)
        pe.wait_ge(oq.ht_lo, j + 2)
        for k in range(2):
            narrow(pe, m, oq, k % MOE_SPLIT, st, j * BLOCK + 4 + k, k, oq.used)

    overflow(pe, m, body)


def experts_act(act, m, s, layer):
    q, at = s.e, layer * EXPERTS
    base = layer * EXPERTS * BLOCK

    def used(i, n):
        return i * (2 * BLOCK) + base + n + 1

    def hi(i, n):
        last_use = (q.used, used(i, n - MOE_SPLIT)) if n >= MOE_SPLIT else None
        split_hi(act, m, s.w, n, raw_count(i, 2 * BLOCK, MOE_AT[layer] + n), last_use, MOE_SPLIT)

    def expert(i, b, w1=True, turn=True):
        first = AHEAD + b * BLOCK
        if w1:
            hi(i, first + 4)
            hi(i, first + 5)
        hid_hi(act, m, q, i, 2, at + b)
        if w1:
            hi(i, first + 6)
            hi(i, first + 7)
            silu(act, m, q, used(i, first + 3))
            hi(i, first + 8)
        if turn:
            rows_hi(act, m, q, i, 2, at + b + 2)
        if w1:
            hi(i, first + 9)
        rows_out(act, m, q, i, 2, at + b, used(i, first + (5 if w1 else 3)))

    hi(0, 2)
    rows_hi(act, m, q, 0, 2, at)
    hi(0, 3)
    hi(0, 4)
    silu(act, m, q, used(0, 1))
    hi(0, 5)
    rows_hi(act, m, q, 0, 2, at + 1)
    last = EXPERTS // 2 - 1
    with act.Fori(0, last) as i:
        for b in range(2):
            expert(i, b)
    expert(last, 0, turn=False)
    expert(last, 1, w1=False, turn=False)

    def body(j):
        act.wait_ge(q.used, (layer + 1) * EXPERTS * BLOCK)
        act.wait_ge(q.y_free, (layer + 1) * EXPERTS + 2)
        oq, st = s.oe[layer], s.ov[layer]
        for k in range(MOE_SPLIT):
            split_hi(act, m, st, k, ov_count(j, k), (oq.y_act, j + 1), MOE_SPLIT)
        rows_hi(act, m, oq, j, 1, 0)
        for k in range(MOE_SPLIT, BLOCK):
            split_hi(act, m, st, k, ov_count(j, k), (oq.used, j * BLOCK + k - MOE_SPLIT + 1), MOE_SPLIT)
        silu(act, m, oq, j * BLOCK + 2)
        hid_hi(act, m, oq, j, 1, 0)
        rows_out(act, m, oq, j, 1, 0, (j + 1) * BLOCK)

    overflow(act, m, body)


def experts_dve(dve, m, s, layer):
    q, at = s.e, layer * EXPERTS
    base = layer * EXPERTS * BLOCK

    def lo(i, n):
        split_lo(dve, m, s.w, n, i * (2 * BLOCK) + MOE_AT[layer] + n, MOE_SPLIT)

    def expert(i, b, w1=True, turn=True):
        first = AHEAD + b * BLOCK
        if w1:
            lo(i, first + 4)
        gate_hid(dve, m, q, i, 2, at + b, i * (2 * BLOCK) + base + first + 2)
        if w1:
            lo(i, first + 5)
        hid_lo(dve, m, q, i, 2, at + b)
        if w1:
            lo(i, first + 6)
            lo(i, first + 7)
            lo(i, first + 8)
        if turn:
            rows_lo(dve, m, q, i, 2, at + b + 2)
        if w1:
            lo(i, first + 9)

    lo(0, 2)
    rows_lo(dve, m, q, 0, 2, at)
    lo(0, 3)
    lo(0, 4)
    lo(0, 5)
    rows_lo(dve, m, q, 0, 2, at + 1)
    last = EXPERTS // 2 - 1
    with dve.Fori(0, last) as i:
        for b in range(2):
            expert(i, b)
    expert(last, 0, turn=False)
    expert(last, 1, w1=False, turn=False)

    def body(j):
        oq, st = s.oe[layer], s.ov[layer]
        for k in range(MOE_SPLIT):
            split_lo(dve, m, st, k, j * BLOCK + k, MOE_SPLIT)
        rows_lo(dve, m, oq, j, 1, 0)
        for k in range(MOE_SPLIT, BLOCK):
            split_lo(dve, m, st, k, j * BLOCK + k, MOE_SPLIT)
        gate_hid(dve, m, oq, j, 1, 0, j * BLOCK + 4)
        hid_lo(dve, m, oq, j, 1, 0)

    overflow(dve, m, body)




def sum_load(pool, m, s, d, layer, t):
    ring = PAIRS[layer]
    if t >= ring:
        pool.wait_ge(s.sum, (layer * TILES + t - ring + 1) * TOP)
    pool.dma_start(m.pair[layer][:, t % ring, :, :], d.y.rearrange("(k t p) n -> t p k n", k=TOP, p=P)[t]) \
        .then_inc(s.pair_in[t % ring], 16)


def sum_tile(dve, m, s, layer, t):
    slot = t % PAIRS[layer]
    before = TILES // PAIRS[0] if layer == 1 and slot < PAIRS[0] else 0
    dve.wait_ge(s.pair_in[slot], 16 * (before + t // PAIRS[layer] + 1))
    for k in range(TOP):
        dve.scalar_tensor_tensor(m.x[:, t, :], m.pair[layer][:, slot, k, :], m.gate[:, k, t:t + 1], m.x[:, t, :],
                                 ALU.mult, ALU.add).then_inc(s.sum, 1)
        dve.wait_ge(s.sum, (layer * TILES + t) * TOP + k + 1)



def pool_program(pool, m, s, d):
    pool.sem_inc(s.h_free, H_RING)
    pool.sem_inc(s.v_free, 2)
    for q in (s.e, *s.oe):
        pool.sem_inc(q.y_free, q.ring)
    load_gain(pool, m, s, d.gla_norm[0])
    pool.memset(m.eps[:], EPS).then_inc(s.const, 1)
    step = Chain(pool, s.const_step)
    for t in (m.ident, m.halves_f):
        step(pool.memset(t[:], 0.0))
    step(pool.affine_select(out=m.ident[:], in_=m.ident[:], compare_op=ALU.not_equal, fill=1.0, base=0,
                            pattern=[[-1, P]], channel_multiplier=1))
    for t in (m.after_f, m.one, m.count):
        step(pool.memset(t[:], 1.0))
    step(pool.tensor_copy(m.ones[:], m.count[:]))
    step(pool.memset(m.halves_f[0:CHUNK, CHUNKS - 2:CHUNKS - 1], 1.0))
    step(pool.memset(m.halves_f[CHUNK:P, CHUNKS - 1:CHUNKS], 1.0))
    step(pool.tensor_copy(m.halves[:], m.halves_f[:]))
    step(pool.affine_select(out=m.count[:], in_=m.count[:], compare_op=ALU.is_ge, fill=0.0, base=-1,
                            pattern=[[1, P]], channel_multiplier=-1))
    step(pool.tensor_copy(m.before[:], m.count[:]))
    step(pool.affine_select(out=m.after_f[:], in_=m.after_f[:], compare_op=ALU.is_ge, fill=0.0, base=-1,
                            pattern=[[-1, P]], channel_multiplier=1))
    step(pool.memset(m.after_f[CHUNK:P, 0:CHUNK], 0.0))
    step(pool.tensor_copy(m.after[:], m.after_f[:]))
    step(pool.iota(m.count_i[:], pattern=[[1, P]], base=0, channel_multiplier=0))
    step(pool.iota(m.block_i[:], pattern=[[TILES, TOP], [1, TILES]], base=1, channel_multiplier=0))
    step(pool.iota(m.row_i[:], pattern=[[1, 1]], base=0, channel_multiplier=1))
    step(pool.tensor_copy(m.count[:], m.count_i[:]))
    step(pool.tensor_copy(m.block[:], m.block_i[:]))
    pool.tensor_copy(m.row[:], m.row_i[:]).then_inc(s.const, 1)
    gates_load(pool, m, s, d)

    gates_pool(pool, m, s, d)
    meet(s, pool, 0, 1)
    load_gain(pool, m, s, d.moe_norm[0])
    heads_pool(pool, m, s, d)
    meet(s, pool, 0, 2)
    moe_pool(pool, m, s, d, 0, 1, 2, d.sgu_norm[0])
    for t in range(TILES):
        sum_load(pool, m, s, d, 0, t)
    meet(s, pool, 0, 5)
    load_gain(pool, m, s, d.moe_norm[1])
    sgu_pool(pool, m, s, d)
    meet(s, pool, 0, 6)
    moe_pool(pool, m, s, d, 1, 3, 6, d.final_norm)
    for t in range(PAIRS[1]):
        sum_load(pool, m, s, d, 1, t)
    for t in range(TILES):
        if t + PAIRS[1] < TILES:
            sum_load(pool, m, s, d, 1, t + PAIRS[1])
        pool.wait_ge(s.fin, t + 1)
        pool.dma_start(d.out[0, t * P:(t + 1) * P, :], m.o_out[:, t % 4, :]).then_inc(s.out[t % 4], 16)
    for k in range(4):
        pool.wait_ge(s.out[k], 16 * TILES // 4)


def moe_pool(pool, m, s, d, layer, n, met, next_gain):
    store_rows(pool, m, s, d, n, layer)
    meet(s, pool, 0, met + 1)
    experts_pool(pool, m, s, d, layer, next_gain)
    meet(s, pool, 0, met + 2)


def pe_program(pe, m, s, d):
    pe.sem_inc(s.n_tr, 2)
    pe.sem_inc(s.o_mm, 2)
    pe.sem_inc(s.e.xt_tr, 2)
    for k in range(2):
        pe.sem_inc(s.oe[k].xt_tr, 1)
    pe.wait_ge(s.const, 2)
    norm_pe(pe, m, s, 0)
    gates_pe(pe, m, s)
    meet(s, pe, 3, 1)
    heads_pe(pe, m, s)
    meet(s, pe, 3, 2)
    moe_pe(pe, m, s, 0, 1, 2)
    norm_pe(pe, m, s, 2)
    turned_half(pe, s, 2, 1)
    meet(s, pe, 3, 5)
    sgu_pe(pe, m, s)
    meet(s, pe, 3, 6)
    moe_pe(pe, m, s, 1, 3, 6)


def moe_pe(pe, m, s, layer, n, met):
    norm_pe(pe, m, s, n)
    route_pe(pe, m, s, layer)
    meet(s, pe, 3, met + 1)
    experts_pe(pe, m, s, layer)
    meet(s, pe, 3, met + 2)


def act_program(act, m, s, d):
    act.sem_inc(s.pj_act, 2)
    act.sem_inc(s.o_evac, 2)
    act.sem_inc(s.e.sil, 1)
    act.sem_inc(s.e.y_act, 1)
    for k in range(2):
        act.sem_inc(s.oe[k].sil, 1)
        act.sem_inc(s.oe[k].y_act, 1)
    act.wait_ge(s.const, 1)

    def came(t):
        if t % (TILES // X_LOADS) == 0:
            act.wait_ge(s.x_in[t * X_LOADS // TILES], 16)

    for t in range(TILES):
        came(t)
        tile_std(act, m, s, 0, t, m.logsig[:, TILES - 2:, :].rearrange("p t n -> p (t n)"))
    norm_act(act, m, s, 0)
    gates_act(act, m, s)
    meet(s, act, 1, 1)
    heads_act(act, m, s)
    meet(s, act, 1, 2)
    moe_act(act, m, s, d, 0, 1, 2)
    meet(s, act, 1, 5)
    sgu_act(act, m, s)
    meet(s, act, 1, 6)
    moe_act(act, m, s, d, 1, 3, 6)


def moe_act(act, m, s, d, layer, n, met):
    route_load(act, m, s, d, layer)
    norm_act(act, m, s, n)
    route_act(act, m, s, layer)
    meet(s, act, 1, met + 1)
    experts_act(act, m, s, layer)
    meet(s, act, 1, met + 2)
    if layer == 0:
        for k in range(2):
            split_hi(act, m, s.w, SGU_V_AT + k, raw_count(0, 4, SGU_V_AT + k))
    for t in range(TILES + 2):
        if t < TILES:
            act.wait_ge(s.sum, (layer * TILES + t + 1) * TOP)
            tile_std(act, m, s, n + 1, t, m.squares[:])
        if layer == 0 and t >= 2:
            tile_hi(act, m, s, n + 1, t - 2)


def dve_program(dve, m, s, d):
    step = Chain(dve, s.step)
    dve.sem_inc(s.w.split, RAW)
    dve.sem_inc(s.og, TILES)
    for sem in (s.n_lo, s.s_upd, s.y_used, s.ot_lo, s.mix_used, s.gt_lo):
        dve.sem_inc(sem, 2)
    dve.sem_inc(s.bn, 16)
    for q in (s.e, *s.oe):
        for sem in (q.xt_lo, q.hid, q.ht_lo):
            dve.sem_inc(sem, 1)
    for k in range(2):
        dve.sem_inc(s.ov[k].split, RAW)
    norm_dve(dve, m, s, 0, step, between=lambda: low_rank_split(dve, m, s, step))
    gates_dve(dve, m, s, step)
    meet(s, dve, 2, 1)
    heads_dve(dve, m, s)
    meet(s, dve, 2, 2)
    moe_dve(dve, m, s, step, 0, 1, 2)
    for k in range(2):
        split_lo(dve, m, s.w, SGU_V_AT + k, SGU_V_AT + k)
    norm_dve(dve, m, s, 2, step, before=lambda t: sum_tile(dve, m, s, 0, t))
    meet(s, dve, 2, 5)
    sgu_dve(dve, m, s, step)
    meet(s, dve, 2, 6)
    moe_dve(dve, m, s, step, 1, 3, 6)
    for t in range(TILES + 1):
        if t < TILES:
            sum_tile(dve, m, s, 1, t)
        if t >= 1:
            u = t - 1
            if u >= 4:
                dve.wait_ge(s.out[u % 4], 16 * (u // 4))
            tile_scale(dve, m, s, 4, u, m.o_out[:, u % 4, :], s.fin, step)


def moe_dve(dve, m, s, step, layer, n, met):
    norm_dve(dve, m, s, n, step, layer, between=lambda: router_split(dve, m, s, layer, step))
    route_dve(dve, m, s, layer, step)
    meet(s, dve, 2, met + 1)
    experts_dve(dve, m, s, layer)
    meet(s, dve, 2, met + 2)


_INS = ["x", "gla_norm", "gla_w_in", "gla_w_gate_up", "gla_b_gate", "gla_head_g", "gla_w_out", "sgu_norm",
        "sgu_w_in", "sgu_ln_g", "sgu_ln_b", "sgu_w_s", "sgu_b_s", "sgu_w_out", "moe_norm", "moe_w_group",
        "moe_b_group", "moe_w_sub", "moe_b_sub", "moe_w1", "moe_w3", "moe_w2", "final_norm"]


def kernel(**inputs):
    import numpy as np
    import concourse.bacc as bacc
    from concourse.bass_utils import run_bass_kernel_spmd

    nc = bacc.Bacc("TRN2", target_bir_lowering=False, num_devices=1)
    arrays, args = {}, []
    for name in _INS:
        a = np.ascontiguousarray(inputs[name])
        arrays[f"in_{name}_dram"] = a
        args.append(nc.dram_tensor(f"in_{name}_dram", a.shape, mybir.dt.from_np(a.dtype), kind="ExternalInput").ap())
    args.append(nc.dram_tensor("out_dram", (1, SEQ, D), F32, kind="ExternalOutput").ap())
    build(nc, *args)
    r = run_bass_kernel_spmd(nc, [arrays], core_ids=[0])
    return r.results[0]["out_dram"]
```
